# Optimizing a Trainium2 kernel written in Bass

```python
import jax, jax.numpy as jnp
from jax import lax
import numpy as np

D_MODEL = 1024
BATCH = 1
SEQ = 512
DEPTH = 2
DEC_BATCH = 8
DEC_SEQ = 4
PAST_LEN = 512
PAGE_SIZE = 128

N_A_LAYERS = DEPTH // 2
N_B_LAYERS = DEPTH - N_A_LAYERS
CHUNK = 128
E_A = 2 * D_MODEL
N_GROUPS_A = 8
GROUP_A = E_A // N_GROUPS_A
N_HEADS = 16
HEAD_DIM = 64
E_B = N_HEADS * HEAD_DIM
Q_BLOCK = 128
PLE_DIM = 256
SB_BIAS_INIT = -7.0
EPS = 1e-6

kernel_name = "yoco_gmlp_stickbreaking_step"

def rms_norm(x, g):
    x32 = x.astype(jnp.float32)
    y = x32 * lax.rsqrt(jnp.mean(x32 * x32, axis=-1, keepdims=True) + EPS)
    return (y * g.astype(jnp.float32)).astype(x.dtype)

def layer_norm(x, g, b):
    x32 = x.astype(jnp.float32)
    mu = jnp.mean(x32, axis=-1, keepdims=True)
    xc = x32 - mu
    y = xc * lax.rsqrt(jnp.mean(xc * xc, axis=-1, keepdims=True) + EPS)
    return (y * g.astype(jnp.float32) + b.astype(jnp.float32)).astype(x.dtype)

def chunk_gmlp(xn, w_in, ln_g, ln_b, w_s, b_s, w_out):
    b_, t, _ = xn.shape
    u, v, gate = jnp.split(xn @ w_in, 3, axis=-1)
    v = layer_norm(v, ln_g, ln_b)
    c = min(CHUNK, t)
    causal = jnp.tril(jnp.ones((c, c), dtype=bool))
    ws = jnp.where(causal[None], w_s[:, :c, :c], 0.0)
    vc = v.reshape(b_, t // c, c, N_GROUPS_A, GROUP_A)
    s = jnp.einsum('gts,bnsgc->bntgc', ws, vc) + b_s[:, :c].T[None, None, :, :, None]
    s = s.reshape(b_, t, E_A)
    y = (u * s * jax.nn.silu(gate)) @ w_out
    return y, v

def stick_breaking(q, k, v, bias, q_pos, k_pos):
    b_, t, h, dh = q.shape
    blk = min(Q_BLOCK, t)
    nb = t // blk
    scale = dh ** -0.5
    k32 = k.astype(jnp.float32)
    v32 = v.astype(jnp.float32)
    bias32 = bias.astype(jnp.float32)[None, :, None, None]
    qb = q.reshape(b_, nb, blk, h, dh).transpose(1, 0, 2, 3, 4)
    pb = q_pos.reshape(nb, blk)

    def block(args):
        qi, pi = args
        z = jnp.einsum('bqhd,bkhd->bhqk', qi.astype(jnp.float32), k32) * scale + bias32
        mask = (k_pos[None, :] < pi[:, None])[None, None]
        log_1mb = jnp.where(mask, jax.nn.log_sigmoid(-z), 0.0)
        after = lax.cumsum(log_1mb, axis=3, reverse=True) - log_1mb
        w = jnp.where(mask, jnp.exp(jax.nn.log_sigmoid(z) + after), 0.0)
        return jnp.einsum('bhqk,bkhd->bqhd', w, v32)

    o = lax.map(block, (qb, pb))
    return o.transpose(1, 0, 2, 3, 4).reshape(b_, t, h, dh).astype(q.dtype)

def stick_branch(xn, w_in, w_out, bias, k_all, v_all, q_pos, k_pos):
    b_, t, _ = xn.shape
    q, gate = jnp.split(xn @ w_in, 2, axis=-1)
    o = stick_breaking(q.reshape(b_, t, N_HEADS, HEAD_DIM), k_all, v_all, bias, q_pos, k_pos)
    return (o.reshape(b_, t, E_B) * jax.nn.silu(gate)) @ w_out

def per_layer_embed(h, p_i, w_ple_i, g_ple_i, w_gate_i):
    gate = jax.nn.sigmoid(rms_norm(h, g_ple_i) @ w_gate_i)
    return h + (p_i @ w_ple_i) * gate

def trunk(x, p, past_k, past_v, keep_chunk_state, g_norm, w_in_a, ln_v_g, ln_v_b, w_spatial, b_spatial,
          w_out_a, g_kv, w_kv, w_in_b, w_out_b, b_sb, w_ple, g_ple, w_ple_gate, g_final):
    b_, t, _ = x.shape
    start = 0 if past_k is None else past_k.shape[1]
    h = x
    chunk_rows = []
    k_new = v_new = k_all = v_all = None
    q_pos = start + jnp.arange(t)
    k_pos = None
    for i in range(DEPTH):
        xn = rms_norm(h, g_norm[i])
        if i < N_A_LAYERS:
            y, v_rows = chunk_gmlp(xn, w_in_a[i], ln_v_g[i], ln_v_b[i], w_spatial[i], b_spatial[i], w_out_a[i])
            if keep_chunk_state:
                chunk_rows.append(v_rows)
        else:
            j = i - N_A_LAYERS
            y = stick_branch(xn, w_in_b[j], w_out_b[j], b_sb[j], k_all, v_all, q_pos, k_pos)
        h = h + y
        h = per_layer_embed(h, p[i], w_ple[i], g_ple[i], w_ple_gate[i])
        if i == N_A_LAYERS - 1:
            k_flat, v_flat = jnp.split(rms_norm(h, g_kv) @ w_kv, 2, axis=-1)
            k_new = k_flat.reshape(b_, t, N_HEADS, HEAD_DIM)
            v_new = v_flat.reshape(b_, t, N_HEADS, HEAD_DIM)
            if past_k is None:
                k_all, v_all = k_new, v_new
            else:
                k_all = jnp.concatenate([past_k, k_new], axis=1)
                v_all = jnp.concatenate([past_v, v_new], axis=1)
            k_pos = jnp.arange(k_all.shape[1])
    y_out = rms_norm(h, g_final)
    chunk_state = jnp.stack(chunk_rows) if keep_chunk_state else None
    return y_out, k_new, v_new, chunk_state

def setup_inputs(seed: int = 0) -> dict:
    key = jax.random.key(seed)
    ks = jax.random.split(key, 24)
    f32 = jnp.float32
    n_pages = PAST_LEN // PAGE_SIZE
    n_used = DEC_BATCH * n_pages
    n_pool = n_used + n_used // 4
    nrm = lambda k, shape, s: (jax.random.normal(k, shape, f32) * s).astype(f32)
    page_table = jax.random.permutation(ks[4], n_pool)[:n_used].reshape(DEC_BATCH, n_pages).astype(jnp.int32)
    return {
        "x_prompt": nrm(ks[0], (BATCH, SEQ, D_MODEL), 1.0),
        "x_sample": nrm(ks[1], (DEC_BATCH, DEC_SEQ, D_MODEL), 1.0),
        "cache_k": nrm(ks[2], (n_pool, PAGE_SIZE, N_HEADS, HEAD_DIM), 1.0),
        "cache_v": nrm(ks[3], (n_pool, PAGE_SIZE, N_HEADS, HEAD_DIM), 1.0),
        "page_table": page_table,
        "p_prompt": nrm(ks[5], (DEPTH, BATCH, SEQ, PLE_DIM), 1.0),
        "p_sample": nrm(ks[6], (DEPTH, DEC_BATCH, DEC_SEQ, PLE_DIM), 1.0),
        "g_norm": 1.0 + nrm(ks[7], (DEPTH, D_MODEL), 0.02),
        "w_in_a": nrm(ks[8], (N_A_LAYERS, D_MODEL, 3 * E_A), D_MODEL ** -0.5),
        "ln_v_g": 1.0 + nrm(ks[9], (N_A_LAYERS, E_A), 0.02),
        "ln_v_b": nrm(ks[10], (N_A_LAYERS, E_A), 0.02),
        "w_spatial": nrm(ks[11], (N_A_LAYERS, N_GROUPS_A, CHUNK, CHUNK), CHUNK ** -0.5),
        "b_spatial": nrm(ks[12], (N_A_LAYERS, N_GROUPS_A, CHUNK), 0.02),
        "w_out_a": nrm(ks[13], (N_A_LAYERS, E_A, D_MODEL), 0.5 * E_A ** -0.5),
        "g_kv": 1.0 + nrm(ks[14], (D_MODEL,), 0.02),
        "w_kv": nrm(ks[15], (D_MODEL, 2 * E_B), D_MODEL ** -0.5),
        "w_in_b": nrm(ks[16], (N_B_LAYERS, D_MODEL, 2 * E_B), D_MODEL ** -0.5),
        "w_out_b": nrm(ks[17], (N_B_LAYERS, E_B, D_MODEL), E_B ** -0.5),
        "b_sb": SB_BIAS_INIT + nrm(ks[22], (N_B_LAYERS, N_HEADS), 0.1),
        "w_ple": nrm(ks[18], (DEPTH, PLE_DIM, D_MODEL), 0.5 * PLE_DIM ** -0.5),
        "g_ple": 1.0 + nrm(ks[19], (DEPTH, D_MODEL), 0.02),
        "w_ple_gate": nrm(ks[20], (DEPTH, D_MODEL, D_MODEL), D_MODEL ** -0.5),
        "g_final": 1.0 + nrm(ks[21], (D_MODEL,), 0.02),
    }

def reference(x_prompt, x_sample, cache_k, cache_v, page_table, p_prompt, p_sample, g_norm, w_in_a, ln_v_g,
              ln_v_b, w_spatial, b_spatial, w_out_a, g_kv, w_kv, w_in_b, w_out_b, b_sb, w_ple, g_ple, w_ple_gate,
              g_final):
    weights = (g_norm, w_in_a, ln_v_g, ln_v_b, w_spatial, b_spatial, w_out_a, g_kv, w_kv, w_in_b, w_out_b,
               b_sb, w_ple, g_ple, w_ple_gate, g_final)
    y_prompt, k_prompt, v_prompt, _ = trunk(x_prompt, p_prompt, None, None, False, *weights)
    n_seq, n_pages = page_table.shape
    past_k = cache_k[page_table].reshape(n_seq, n_pages * PAGE_SIZE, N_HEADS, HEAD_DIM)
    past_v = cache_v[page_table].reshape(n_seq, n_pages * PAGE_SIZE, N_HEADS, HEAD_DIM)
    y_sample, k_sample, v_sample, chunk_v_sample = trunk(x_sample, p_sample, past_k, past_v, True, *weights)
    return (y_prompt, y_sample, k_prompt, v_prompt, k_sample, v_sample, chunk_v_sample)


_drawn_inputs = setup_inputs


def setup_inputs(seed=0):
    import zlib

    import numpy as np

    out = dict(_drawn_inputs(seed))
    spreads = {}
    factors = {'cache_k': 24.12,
     'g_norm': 2.781,
     'ln_v_g': 7.79,
     'ln_v_b': 7.985,
     'b_spatial': 8.0,
     'g_kv': 8.229,
     'b_sb': 64.0,
     'g_ple': 64.0,
     'g_final': 7.525,
     'cache_v': 8.0,
     'w_in_b': 8.0,
     'w_out_b': 8.0}
    for name, (base, spread) in spreads.items():
        noise = np.random.default_rng([zlib.crc32(name.encode()), seed]).standard_normal(out[name].shape)
        drawn = base * np.exp(spread * noise) if base else spread * noise
        out[name] = __import__('jax').numpy.asarray(drawn.astype(out[name].dtype))
    for name, factor in factors.items():
        out[name] = (out[name] * factor).astype(out[name].dtype)
    return out
```

```python
from contextlib import ExitStack, contextmanager

import concourse.bass as bass
from concourse import mybir

F32 = mybir.dt.float32
F32R = mybir.dt.float32r
BF16 = mybir.dt.bfloat16
I32 = mybir.dt.int32
ACT = mybir.ActivationFunctionType
ALU = mybir.AluOpType

P = 128
SLOTS = 4
AHEAD = 3
EPS = 1e-6
FAR = -1e30


class Count:

    def __init__(self, start=0):
        self.before, self.here, self.reg, self.per = start, 0, None, 0

    def now(self, ahead=0):
        n = self.before + self.here + ahead
        return n if self.reg is None else self.reg * self.per + n

    def step(self, n=1):
        self.here += n

    def slot(self, ring, ahead=0):
        assert self.per % ring == 0
        return (self.before + self.here + ahead) % ring

    def lap(self, ring, ahead=0):
        assert self.per % ring == 0
        n = (self.before + self.here + ahead) // ring
        return n if self.reg is None else self.reg * (self.per // ring) + n


@contextmanager
def repeat(eng, turns, *counts):
    with eng.Fori(0, turns) as i:
        for c, per in counts:
            c.before, c.here, c.reg, c.per = c.before + c.here, 0, i, per
        yield i
        for c, per in counts:
            assert c.here == per, (c.here, per)
    for c, per in counts:
        c.before, c.here, c.reg, c.per = c.before + per * turns, 0, None, 0


def build(nc, x_prompt, x_sample, cache_k, cache_v, page_table, p_prompt, p_sample, g_norm, w_in_a, ln_v_g,
          ln_v_b, w_spatial, b_spatial, w_out_a, g_kv, w_kv, w_in_b, w_out_b, b_sb, w_ple, g_ple, w_ple_gate,
          g_final, y_prompt, y_sample, k_prompt, v_prompt, k_sample, v_sample, chunk_v_sample):
    D = g_kv.shape[0]
    TP = x_prompt.shape[1]
    NB, NQ = x_sample.shape[0], x_sample.shape[1]
    NS = NB * NQ
    T = TP + NS
    TH = T // 2
    KT = D // P
    E_A = ln_v_g.shape[1]
    NG = w_spatial.shape[1]
    NH = b_sb.shape[1]
    DH = D // NH
    NP = NH // 2
    QB = TP // P
    TT = QB + 1
    PLE = p_prompt.shape[3]
    PKT = PLE // P
    NPOOL = cache_k.shape[0]
    PAGES = page_table.shape[1]
    HALF = E_A // D
    SCALE = float(DH) ** -0.5
    assert TH * 2 == T and TP == QB * P and D == KT * P and E_A == HALF * D and NP == KT
    assert g_norm.shape[0] == 2 and PAGES == QB and SCALE == 0.125 and NG == HALF * 4

    w_in_a_v = w_in_a[0].rearrange("(kt p) n -> p kt n", p=P)
    w_out_a_v = w_out_a[0].rearrange("(hf kt p) n -> hf p kt n", p=P, hf=HALF)
    w_kv_v = w_kv.rearrange("(kt p) n -> p kt n", p=P)
    w_in_b_v = w_in_b[0].rearrange("(kt p) n -> p kt n", p=P)
    w_out_b_v = w_out_b[0].rearrange("(kt p) n -> p kt n", p=P)
    w_gate_v = w_ple_gate.rearrange("l (kt p) n -> l p kt n", p=P)
    w_ple_v = w_ple.rearrange("l (kt p) n -> l p kt n", p=P)
    xp_v = x_prompt[0].rearrange("(t p) d -> p t d", p=P)
    xs_v = x_sample.rearrange("b q d -> (b q) d")
    kp_v = k_prompt[0].rearrange("(t p) h d -> p t (h d)", p=P)
    vp_v = v_prompt[0].rearrange("(t p) h d -> p t (h d)", p=P)
    yp_v = y_prompt[0].rearrange("(t p) d -> p t d", p=P)
    ck_v = cache_k.rearrange("g t h d -> g t (h d)")
    cv_v = cache_v.rearrange("g t h d -> g t (h d)")

    N_AV = E_A // P
    N_UG = 2 * KT
    N_PL = KT + 2
    END_AV = N_AV
    END_A = N_AV + HALF * (N_UG + KT)
    END_PL0 = END_A + N_PL
    END_B = END_PL0 + 4 * NP
    END_BO = END_B + KT
    END = END_BO + N_PL

    with ExitStack() as ctx:
        def sem(name):
            return ctx.enter_context(nc.semaphore(name))

        top = [nc.sbuf_base + (-nc.sbuf_base) % 32]

        def size(shape):
            n = 4
            for s in shape[1:]:
                n *= s
            return n + (-n) % 32

        def place(name, shape, dt=F32, at=None):
            where = top[0] if at is None else at[0]
            t = nc.alloc_sbuf_tensor_at(name, shape, dt, offset=where)
            if at is None:
                top[0] += size(shape)
            else:
                at[0] += size(shape)
            return t

        ident = place("ident", [P, P])
        ones = place("ones", [P, P])
        negtri = place("negtri", [P, P])
        negones = place("negones", [P, P])
        rep = place("rep", [P, NB, NQ])
        blockdiag = place("blockdiag", [NS, NB, NQ])
        ident_b = place("ident_b", [P, P], BF16)
        unseen = place("unseen", [P, P], BF16)
        unseen_n = place("unseen_n", [NS, NH, NB, NQ], BF16)
        N_COL = 2 * KT + KT + 2 * KT + KT + 2 * (E_A // P)
        cols = place("cols", [P, N_COL])
        bias = place("bias", [P, NH])
        pages = place("pages", [1, NB * PAGES], I32)
        bst = place("bst", [P, TT, N_AV // 4, 6])
        mv = place("mv", [P, TT, 2])
        ln_s = place("ln_s", [P, 4, TT])
        c0 = [0]

        def col(n):
            a = c0[0]
            c0[0] += n
            return cols[:, a:a + n]

        g_norm_c = [col(KT), col(KT)]
        g_kv_c = col(KT)
        g_ple_c = [col(KT), col(KT)]
        g_final_c = col(KT)
        ln_g_c = col(E_A // P)
        ln_b_c = col(E_A // P)

        h = place("h", [P, KT, T])
        ms = place("ms", [P, T])
        rinv = place("rinv", [P, T])
        sumsq = place("sumsq", [P, T])
        raw = place("raw", [P, SLOTS, KT, P])
        w_hi = place("w_hi", [P, SLOTS, KT, P], F32R)
        w_lo = place("w_lo", [P, SLOTS, KT, P], F32R)
        at_x0, at_x1 = [top[0]], [top[0] + 2 * size([P, KT, T])]
        top[0] += 4 * size([P, KT, T])
        x1_base = at_x1[0]
        x0_base = at_x0[0]
        act_hi = [place("act_hi0", [P, KT, T], F32R, at_x0), None]
        act_lo = [place("act_lo0", [P, KT, T], F32R, at_x0), None]
        act_hi[1] = place("act_hi1", [P, KT, T], F32R, at_x1)
        act_lo[1] = place("act_lo1", [P, KT, T], F32R, at_x1)
        at = [x1_base]
        vt = place("vt", [P, 2, T], F32, at)
        ws_nat = place("ws_nat", [P, NG, P], F32, at)
        params = place("params", [N_COL, P], F32, at)
        lng_bc = place("lng_bc", [NS, E_A], F32, at)
        lnb_bc = place("lnb_bc", [NS, E_A], F32, at)
        assert at[0] <= at_x1[0]

        area = top[0]
        at = [area]
        v_nat = place("v_nat", [P, TT, E_A], F32, at)
        vhat = place("vhat", [P, TT, P], F32, at)
        ws_t = place("ws_t", [P, NG, P], F32, at)
        ws_ts = place("ws_ts", [NS, NG, NB, NQ], F32, at)
        row_sum = place("row_sum", [P, NG, P + NS], F32, at)
        bs_bc = place("bs_bc", [P, NG, P + NS], F32, at)
        bs_ln = place("bs_ln", [P, P + NS], F32, at)
        u_r = place("u_r", [P, T], F32, at)
        g_r = place("g_r", [P, T], F32, at)
        s_t = place("s_t", [P, T], F32, at)
        v_out = place("v_out", [NS, E_A], F32, at)
        ends = [at[0]]
        at = [area]
        x_nat = place("x_nat", [P, TT, D], F32, at)
        at = [area]
        p_nat = place("p_nat", [P, TT, PLE], F32, at)
        p_hi = place("p_hi", [P, PKT, T], F32R, at)
        p_lo = place("p_lo", [P, PKT, T], F32R, at)
        p_t = place("p_t", [P, PKT, T], F32, at)
        ple = place("ple", [P, KT // 2, T], F32, at)
        gate = place("gate", [P, 2, T], F32, at)
        sq_a = place("sq_a", [P, T], F32, at)
        ends.append(at[0])
        at = [area]
        kt_t = place("kt_t", [P, 2, T], F32, at)
        qt_t = place("qt_t", [P, 2, T], F32, at)
        vt_t = place("vt_t", [P, T], F32, at)
        k_nat = place("k_nat", [P, 2, QB, P], F32, at)
        vb_nat = place("vb_nat", [P, 2, QB, P], F32, at)
        gb_r = place("gb_r", [P, T], F32, at)
        silu_g = place("silu_g", [P, 2, TP], F32, at)
        soft = place("soft", [P, 2, QB * (QB + 1) // 2 * P], F32, at)
        absz = place("absz", [P, 2, TP], F32, at)
        relz = place("relz", [P, 2, TP], F32, at)
        wts = place("wts", [P, 2, TP], F32, at)
        o_s = place("o_s", [P, TP], F32, at)
        ats = [area]
        ktb = place("ktb", [P, KT, PAGES * P], F32, ats)
        vpage1 = place("vpage1", [P, PAGES, D], F32, ats)
        xs_b = place("xs_b", [P, PAGES, NH, NQ], F32, ats)
        as_b = place("as_b", [P, PAGES, NH, NQ], F32, ats)
        sp_b = place("sp_b", [P, PAGES, NH, NQ], F32, ats)
        d_b = place("d_b", [P, PAGES, NH, NQ], F32, ats)
        ws_b = place("ws_b", [P, PAGES, NH, NQ], F32, ats)
        kpage1 = place("kpage1", [P, PAGES, D], F32, ats)
        at_s = [max(at[0], ats[0])]
        kts = place("kts", [P, NP, NS], F32, at_s)
        qts = place("qts", [P, NP, NS], F32, at_s)
        silu_s = place("silu_s", [P, NP, NS], F32, at_s)
        ks_nat = place("ks_nat", [NS, D], F32, at_s)
        vs_nat = place("vs_nat", [NS, D], F32, at_s)
        ends.append(at_s[0])
        ats = [at_s[0]]
        qbd = place("qbd", [P, NP, 2, NS], F32, ats)
        xs_n = place("xs_n", [NS, NH, NS], F32, ats)
        as_n = place("as_n", [NS, NH, NS], F32, ats)
        sp_n = place("sp_n", [NS, NH, NS], F32, ats)
        ws_n = place("ws_n", [NS, NH, NS], F32, ats)
        os_s = place("os_s", [P, NP, NS], F32, ats)
        bias_q = place("bias_q", [P, NH, NQ], F32, ats)
        ends.append(ats[0])
        at = [x1_base]
        kpage0 = place("kpage0", [P, PAGES, D], F32, at)
        vpage0 = place("vpage0", [P, PAGES, D], F32, at)
        assert at[0] <= at_x1[0]
        kpage, vpage = [kpage0, kpage1], [vpage0, vpage1]
        at = [x0_base]
        y_t = place("y_t", [P, KT, T], F32, at)
        at = [max(ends[1], area)]
        y_nat = place("y_nat", [P, TT, D], F32, at)
        ends.append(at[0])
        assert max(ends) <= nc.sbuf_usable_end, (max(ends), nc.sbuf_usable_end)
        sq_b = sq_a

        acc = [ctx.enter_context(nc.psum_tensor(f"acc{n}", [P, 2, 512], F32)) for n in range(2)]
        zb = [ctx.enter_context(nc.psum_tensor(f"zb{n}", [P, 512], F32)) for n in range(2)]
        ob = [ctx.enter_context(nc.psum_tensor(f"ob{n}", [P, 512], F32)) for n in range(2)]

        def wait_apart(eng, semaphore, value):
            if isinstance(value, int):
                eng.wait_ge(semaphore, value)
                return
            value = eng.to_reg(value)
            eng.wait_ge(const_set, N_CONST)
            eng.wait_ge(semaphore, value)

        def rows(ap, n):
            return ap.partition_broadcast(n)

        def both(t):
            return t[:, :, 0:TH]

        def halves(ap):
            return ap.rearrange("p (c t) -> p c t", c=2)

        const_set = sem("const_set")
        x_in = sem("x_in")
        params_in = sem("params_in")
        small_in = sem("small_in")
        p_in = sem("p_in")
        raw_in = [sem(f"raw_in{s}") for s in range(SLOTS)]
        raw_scaled = sem("raw_scaled")
        hi_made = sem("hi_made")
        lo_made = sem("lo_made")
        panel_done = sem("panel_done")
        turned = sem("turned")
        acc_read = sem("acc_read")
        h_new = sem("h_new")
        x_hi = sem("x_hi")
        x_lo = sem("x_lo")
        squared = sem("squared")
        sq_step = sem("sq_step")
        ssq_out = sem("ssq_out")
        vec = sem("vec")
        mean_sq = sem("mean_sq")
        rooted = sem("rooted")
        normed = sem("normed")
        ws_masked = sem("ws_masked")
        bs_ready = sem("bs_ready")
        vh_made = sem("vh_made")
        mixed = sem("mixed")
        silu_done = sem("silu_done")
        s_ready = sem("s_ready")
        us_done = sem("us_done")
        y_made = sem("y_made")
        vout_step = sem("vout_step")
        vout_done = sem("vout_done")
        out_done = sem("out_done")
        kv_out = [sem(f"kv_out{b}") for b in range(2)]
        p_hi_made = sem("p_hi_made")
        p_lo_made = sem("p_lo_made")
        stats_done = sem("stats_done")
        gate_sig = sem("gate_sig")
        gate_used = sem("gate_used")
        z_full = sem("z_full")
        rel_done = sem("rel_done")
        act_step = sem("act_step")
        log_done = sem("log_done")
        soft_done = sem("soft_done")
        after_done = sem("after_done")
        exp_done = sem("exp_done")
        o_full = sem("o_full")
        o_read = sem("o_read")
        sg_ready = sem("sg_ready")
        o_hi = sem("o_hi")
        o_lo = sem("o_lo")
        page_in = [sem(f"page_in{n}") for n in range(2)]
        pages_in = sem("pages_in")
        qbd_set = sem("qbd_set")
        zs_full = sem("zs_full")
        xs_done = sem("xs_done")
        logs_done = sem("logs_done")
        softs_done = sem("softs_done")
        afters_done = sem("afters_done")
        ds_done = sem("ds_done")
        exps_done = sem("exps_done")
        os_full = sem("os_full")
        os_read = sem("os_read")
        y_scaled = sem("y_scaled")

        N_CONST = 18

        N_START = 1 + KT + 2
        ACC_UG = N_START + 2 * N_AV + 4
        ACC_PL0 = ACC_UG + HALF * (N_UG + KT)
        ACC_B = ACC_PL0 + PKT + 2 * KT
        ACC_S = ACC_B + 6 * NP
        ACC_BO = ACC_S + NB * (KT // 2)
        ACC_Y = ACC_BO + KT + PKT + 2 * KT
        ACC_END = ACC_Y + TT

        def sl(n):
            return slice(n, n + 1) if isinstance(n, int) else bass.ds(n, 1)

        def soft_at(kb):
            m = QB - 1 - kb
            return m * (m + 1) // 2 * P

        def bias_of(a, e):
            return bias[:, sl(a * 2 + e)]

        block = ctx.enter_context(nc.Block())

        @block.sync
        def _(sp):
            panel = Count()

            def load(src, view=None):
                if panel.reg is None and panel.now() < SLOTS:
                    pass
                else:
                    sp.wait_ge(lo_made, panel.now(1 - SLOTS))
                s = panel.slot(SLOTS)
                dst = raw[:, s, :, :]
                if view is not None:
                    dst = dst.rearrange("p (kt a) n -> p kt (a n)", kt=PKT)
                sp.dma_start(dst, src).then_inc(raw_in[s], 16)
                panel.step()

            for t in range(QB):
                sp.dma_start(x_nat[:, t, :], xp_v[:, t, :]).then_inc(x_in, 16)
            sp.dma_start(x_nat[0:NS, QB, :], xs_v).then_inc(x_in, 16)
            r = 0
            for src, n in ((g_norm[0], KT), (g_norm[1], KT), (g_kv, KT), (g_ple[0], KT), (g_ple[1], KT),
                           (g_final, KT), (ln_v_g[0], E_A // P), (ln_v_b[0], E_A // P)):
                sp.dma_start(params[r:r + n, :], src.rearrange("(r c) -> r c", c=P)).then_inc(params_in, 16)
                r += n
            for k in range(SLOTS):
                load(w_in_a_v[:, :, E_A + k * P:E_A + (k + 1) * P])
            sp.dma_start(ws_nat[:, :, :], w_spatial[0].rearrange("g t s -> t g s")).then_inc(small_in, 16)
            sp.dma_start(bs_bc[:, :, 0:P], rows(b_spatial[0], P)).then_inc(small_in, 16)
            sp.dma_start(bias[:, :], rows(b_sb[0], P)).then_inc(small_in, 16)
            sp.dma_start(lng_bc[:, :], rows(ln_v_g[0], NS)).then_inc(small_in, 16)
            sp.dma_start(lnb_bc[:, :], rows(ln_v_b[0], NS)).then_inc(small_in, 16)
            sp.dma_start(pages[:, :], page_table.rearrange("(a b) g -> a (b g)", a=1)).then_inc(pages_in, 16)
            with repeat(sp, N_AV // SLOTS - 1, (panel, SLOTS)) as i:
                for k in range(SLOTS):
                    load(w_in_a_v[:, :, bass.ds(i * (SLOTS * P) + (E_A + (SLOTS + k) * P), P)])
            for hf in range(HALF):
                with repeat(sp, N_UG // SLOTS, (panel, SLOTS)) as i:
                    for k in range(SLOTS):
                        at0 = hf * D + (k // 2) * P + (k % 2) * 2 * E_A
                        load(w_in_a_v[:, :, bass.ds(i * (2 * P) + at0, P)])
                with repeat(sp, KT // SLOTS, (panel, SLOTS)) as i:
                    for k in range(SLOTS):
                        load(w_out_a_v[hf][:, :, bass.ds(i * (SLOTS * P) + k * P, P)])
                if hf == 0:
                    sp.wait_ge(vout_done, 1)
                    sp.dma_start(chunk_v_sample[0].rearrange("b q e -> (b q) e"), v_out[:, :]).then_inc(out_done, 16)

            def embed_panels(layer):
                for n in range(KT):
                    if n % 4 == 0:
                        load(w_ple_v[layer][:, :, n * P:(n + 4) * P], view="ple")
                    load(w_gate_v[layer][:, :, n * P:(n + 1) * P])

            def embed_inputs(layer):
                for t in range(QB):
                    sp.dma_start(p_nat[:, t, :], p_prompt[layer, 0, t * P:(t + 1) * P, :]).then_inc(p_in, 16)
                sp.dma_start(p_nat[0:NS, QB, :], p_sample[layer].rearrange("b q e -> (b q) e")).then_inc(p_in, 16)

            sp.wait_ge(vh_made, N_AV)
            embed_inputs(0)
            embed_panels(0)

            def load_pair(i):
                for k in range(2):
                    load(w_kv_v[:, :, bass.ds(i * P + k * D, P)] if not isinstance(i, int) else
                         w_kv_v[:, :, i * P + k * D:i * P + k * D + P])
                for k in range(2):
                    load(w_in_b_v[:, :, bass.ds(i * P + k * D, P)] if not isinstance(i, int) else
                         w_in_b_v[:, :, i * P + k * D:i * P + k * D + P])

            def store_pair(i, b):
                sp.wait_ge(acc_read, i * 6 + (ACC_B + 5 + 2))
                cs = bass.ds(i * P, P) if not isinstance(i, int) else slice(i * P, (i + 1) * P)
                sp.dma_start(kp_v[:, :, cs], k_nat[:, b, :, :]).then_inc(kv_out[b], 16)
                sp.dma_start(vp_v[:, :, cs], vb_nat[:, b, :, :]).then_inc(kv_out[b], 16)

            load_pair(0)
            load_pair(1)
            with repeat(sp, NP // 2 - 1, (panel, 8)) as m:
                for b in range(2):
                    load_pair(m * 2 + (2 + b))
                    store_pair(m * 2 + b, b)
            for n in range(AHEAD):
                load(w_out_b_v[:, :, n * P:(n + 1) * P])
            store_pair(NP - 2, 0)
            store_pair(NP - 1, 1)
            sp.dma_start(k_sample.rearrange("b q h d -> (b q) (h d)"), ks_nat[:, :]).then_inc(out_done, 16)
            sp.dma_start(v_sample.rearrange("b q h d -> (b q) (h d)"), vs_nat[:, :]).then_inc(out_done, 16)
            sp.wait_ge(pages_in, 16)
            sp.wait_ge(o_lo, NP)
            sp.wait_ge(kv_out[0], 16 * NP)
            sp.wait_ge(kv_out[1], 16 * NP)

            def load_pages(b, slot):
                for g in range(PAGES):
                    one = pages[0:1, bass.ds(b * PAGES + g, 1)] if not isinstance(b, int) else \
                        pages[0:1, b * PAGES + g:b * PAGES + g + 1]
                    page = sp.value_load(one, min_val=0, max_val=NPOOL - 1)
                    sp.dma_start(kpage[slot][:, g, :], ck_v[bass.ds(page, 1), :, :].rearrange("a t d -> t (a d)"))\
                        .then_inc(page_in[slot], 16)
                    sp.dma_start(vpage[slot][:, g, :], cv_v[bass.ds(page, 1), :, :].rearrange("a t d -> t (a d)"))\
                        .then_inc(page_in[slot], 16)

            load_pages(0, 0)
            load_pages(1, 1)
            with sp.Fori(0, NB // 2 - 1) as m:
                for b in range(2):
                    sp.wait_ge(os_full, m * 2 + (b + 1))
                    load_pages(m * 2 + (2 + b), b)
            for n in range(AHEAD, KT):
                load(w_out_b_v[:, :, n * P:(n + 1) * P])
            sp.wait_ge(os_read, NB)
            embed_inputs(1)
            embed_panels(1)
            for t in range(TT):
                sp.wait_ge(acc_read, ACC_Y + t + 1 + 2)
                if t < QB:
                    sp.dma_start(yp_v[:, t, :], y_nat[:, t, :]).then_inc(out_done, 16)
                else:
                    sp.dma_start(y_sample.rearrange("b q d -> (b q) d"), y_nat[0:NS, t, :]).then_inc(out_done, 16)
            sp.wait_ge(out_done, 16 * (3 + TT))
            assert panel.now() == END

        @block.gpsimd
        def _(pool):
            panel, accs, sq_n, news, blk = Count(), Count(), Count(), Count(), Count()

            pool.memset(ident[:, :], 0.0).then_inc(const_set, 1)
            pool.memset(ones[:, :], 1.0).then_inc(const_set, 1)
            pool.memset(negones[:, :], -1.0).then_inc(const_set, 1)
            pool.memset(negtri[:, :], -1.0).then_inc(const_set, 1)
            pool.memset(rep[:, :, :], 0.0).then_inc(const_set, 1)
            pool.memset(blockdiag[:, :, :], 1.0).then_inc(const_set, 1)
            pool.memset(mv[:, :, :], 1.0).then_inc(const_set, 1)
            pool.memset(ws_ts[:, 0, 0, :], 0.0).then_inc(panel_done, SLOTS)
            pool.memset(ws_ts[:, 0, 1, :], 0.0).then_inc(acc_read, 2)
            pool.memset(ws_ts[:, 0, 2, :], 0.0).then_inc(o_read, 2)
            pool.memset(unseen[:, :], FAR).then_inc(const_set, 1)
            pool.memset(unseen_n[:, :, :, :], 0.0).then_inc(const_set, 1)
            pool.wait_ge(const_set, 9)
            pool.affine_select(out=ident[:, :], in_=ident[:, :], compare_op=ALU.not_equal, fill=1.0, base=0,
                               pattern=[[-1, P]], channel_multiplier=1).then_inc(const_set, 1)
            pool.affine_select(out=negtri[:, :], in_=negtri[:, :], compare_op=ALU.is_ge, fill=0.0, base=0,
                               pattern=[[-1, P]], channel_multiplier=1).then_inc(const_set, 1)
            pool.affine_select(out=rep[:, :, :], in_=rep[:, :, :], compare_op=ALU.not_equal, fill=1.0, base=0,
                               pattern=[[0, NB], [-1, NQ]], channel_multiplier=1).then_inc(const_set, 1)
            pool.affine_select(out=blockdiag[:, :, :], in_=blockdiag[:, :, :], compare_op=ALU.is_ge, fill=0.0,
                               base=0, pattern=[[-NQ, NB], [0, NQ]], channel_multiplier=1).then_inc(const_set, 1)
            pool.affine_select(out=unseen[:, :], in_=unseen[:, :], compare_op=ALU.is_ge, fill=0.0, base=0,
                               pattern=[[-1, P]], channel_multiplier=1).then_inc(const_set, 1)
            pool.affine_select(out=unseen_n[:, :, :, :], in_=unseen_n[:, :, :, :], compare_op=ALU.is_ge, fill=FAR,
                               base=0, pattern=[[0, NH], [-NQ, NB], [0, NQ]], channel_multiplier=1)\
                .then_inc(const_set, 1)
            pool.wait_ge(const_set, 15)
            pool.tensor_copy(ident_b[:, :], ident[:, :]).then_inc(const_set, 1)
            pool.affine_select(out=unseen_n[:, :, :, :], in_=unseen_n[:, :, :, :], compare_op=ALU.is_gt, fill=FAR,
                               base=0, pattern=[[0, NH], [NQ, NB], [1, NQ]], channel_multiplier=-1)\
                .then_inc(const_set, 1)
            pool.affine_select(out=blockdiag[:, :, :], in_=blockdiag[:, :, :], compare_op=ALU.is_ge, fill=0.0,
                               base=NQ - 1, pattern=[[NQ, NB], [0, NQ]], channel_multiplier=-1)\
                .then_inc(const_set, 1)

            def gain_of(p):
                if p < END_AV:
                    return g_norm_c[0]
                if p < END_A:
                    return g_norm_c[0] if (p - END_AV) % (N_UG + KT) < N_UG else None
                if p < END_PL0:
                    return g_ple_c[0] if (p - END_A) % 5 else None
                if p < END_B:
                    return g_kv_c if (p - END_PL0) % 4 < 2 else g_norm_c[1]
                if p < END_BO:
                    return None
                return g_ple_c[1] if (p - END_BO) % 5 else None

            def scale(gain):
                s = panel.slot(SLOTS)
                pool.wait_ge(raw_in[s], panel.lap(SLOTS) * 16 + 16)
                if gain is None:
                    pool.engine_nop().then_inc(raw_scaled, 1)
                else:
                    pool.tensor_tensor(raw[:, s, :, :], raw[:, s, :, :], gain[:, :, None].to_broadcast([P, KT, P]),
                                       ALU.mult).then_inc(raw_scaled, 1)
                panel.step()

            def scale_next():
                if panel.reg is None and panel.now() >= END:
                    return
                p = panel.before + panel.here
                if panel.reg is not None:
                    for t in range(turns[0]):
                        assert gain_of(p + t * panel.per) is gain_of(p)
                scale(gain_of(p))

            turns = [0]

            sq_scratch = [g_r]

            def squares(n, embedded=False):
                if embedded:
                    news.step()
                    pool.wait_ge(h_new, news.now())
                else:
                    accs.step()
                    pool.wait_ge(acc_read, accs.now(2))
                sq_n.step()
                hn = h[:, n, :]
                if n == 0:
                    pool.tensor_tensor(sumsq[:, :], hn, hn, ALU.mult).then_inc(squared, 1)
                    return
                pool.wait_ge(squared, sq_n.now(-1))
                pool.tensor_tensor(sq_scratch[0][:, :], hn, hn, ALU.mult).then_inc(sq_step, 1)
                sq_steps.step()
                pool.wait_ge(sq_step, sq_steps.now())
                pool.tensor_tensor(sumsq[:, :], sumsq[:, :], sq_scratch[0][:, :], ALU.add).then_inc(squared, 1)

            sq_steps = Count()

            pool.wait_ge(acc_read, 2 + 1)
            for _ in range(AHEAD):
                scale_next()
            accs.step()
            for n in range(KT):
                squares(n)
            accs.step(2)
            pool.wait_ge(acc_read, accs.now(2))
            pool.affine_select(out=ws_t[:, :, :], in_=ws_t[:, :, :], compare_op=ALU.is_ge, fill=0.0, base=0,
                               pattern=[[0, NG], [1, P]], channel_multiplier=-1).then_inc(ws_masked, 1)
            pool.wait_ge(small_in, 80)
            pool.tensor_copy(bs_bc[:, :, P:P + NS].rearrange("p g (b q) -> p g b q", q=NQ),
                             bs_bc[:, :, 0:NQ][:, :, None, :].to_broadcast([P, NG, NB, NQ]))\
                .then_inc(bs_ready, 1)

            turns[0] = N_AV // SLOTS - 1
            with repeat(pool, turns[0], (panel, SLOTS)):
                for k in range(SLOTS):
                    scale_next()
            for k in range(SLOTS):
                scale_next()
            pool.wait_ge(vout_step, 1)
            pool.tensor_tensor(v_out[:, :], v_out[:, :], lng_bc[:, :], ALU.mult).then_inc(vout_step, 1)
            pool.wait_ge(vout_step, 2)
            pool.tensor_tensor(v_out[:, :], v_out[:, :], lnb_bc[:, :], ALU.add).then_inc(vout_done, 1)
            ytile = Count()

            def mix(hf):
                def turn():
                    for k in range(2):
                        scale_next()
                        scale_next()
                        ytile.step()
                        pool.wait_ge(s_ready, ytile.now())
                        pool.tensor_tensor(u_r[:, :], u_r[:, :], s_t[:, :], ALU.mult).then_inc(us_done, 1)
                        pool.wait_ge(us_done, ytile.now())
                        pool.wait_ge(silu_done, ytile.now())
                        pool.tensor_tensor(s_t[:, :], u_r[:, :], g_r[:, :], ALU.mult).then_inc(y_made, 1)

                turns[0] = N_UG // SLOTS - 1
                with repeat(pool, turns[0], (panel, SLOTS), (ytile, 2)):
                    turn()
                turn()

            mix(0)
            for n in range(KT):
                scale_next()
            mix(1)
            accs.step(ACC_PL0 - KT - N_START)
            for n in range(KT):
                scale_next()
                squares(n)
            sq_scratch[0] = sq_a

            def embed():
                gt = embed_n
                for n in range(KT):
                    if n % 4 == 0:
                        scale_next()
                    scale_next()
                    gt.step()
                    pool.wait_ge(gate_sig, gt.now())
                    pool.tensor_tensor(gate[:, n % 2, :], gate[:, n % 2, :], ple[:, n % 4, :], ALU.mult)\
                        .then_inc(gate_used, 1)
                    if n > 0:
                        squares(n - 1, True)
                squares(KT - 1, True)

            embed_n = Count()
            embed()

            turns[0] = NP - 1
            with repeat(pool, turns[0], (panel, 4)):
                for k in range(4):
                    scale_next()
            for k in range(4):
                scale_next()

            pool.wait_ge(acc_read, ACC_S - 2 + 2)
            pool.memset(qbd[:, :, :, :], 0.0).then_inc(qbd_set, 1)
            pool.wait_ge(qbd_set, 1)
            for e in range(2):
                r = slice(e * DH, (e + 1) * DH)
                pool.tensor_copy(qbd[r, :, e, :], qts[r, :, :]).then_inc(qbd_set, 1)

            accs.step(ACC_BO - ACC_PL0)
            for n in range(KT):
                scale_next()
                squares(n)
            embed()

        @block.scalar
        def _(act):
            panel, accs, news, roots = Count(), Count(), Count(), Count()

            def split_next():
                if panel.reg is None and panel.now() >= END:
                    return
                s = panel.slot(SLOTS)
                act.wait_ge(raw_scaled, panel.now(1))
                act.wait_ge(panel_done, panel.now(1))
                nc.scalar.activation(w_hi[:, s, :, :], raw[:, s, :, :], ACT.Copy).then_inc(hi_made, 1)
                panel.step()

            def split_x(n, into, embedded=False):
                if embedded:
                    news.step()
                    act.wait_ge(h_new, news.now())
                else:
                    accs.step()
                    wait_apart(act, acc_read, accs.now(2))
                nc.scalar.activation(act_hi[into][:, sl(n), :], h[:, sl(n), :], ACT.Copy).then_inc(x_hi, 1)

            def root():
                roots.step()
                act.wait_ge(mean_sq, roots.now())
                nc.scalar.activation(rinv[:, :], ms[:, :], ACT.Sqrt).then_inc(rooted, 1)

            for _ in range(AHEAD):
                split_next()
            accs.step()
            for n in range(KT):
                split_x(n, 0)
            root()
            with repeat(act, N_AV // SLOTS, (panel, SLOTS)):
                for k in range(SLOTS):
                    split_next()
            act.wait_ge(normed, 1)
            nc.scalar.activation(ln_s[:, 1, :], ln_s[:, 0, :], ACT.Sqrt).then_inc(rooted, 1)
            act.wait_ge(normed, 2)
            nc.scalar.activation(v_out[:, :], v_nat[0:NS, QB, :], ACT.Identity, bias=ln_s[0:NS, 3, QB:QB + 1],
                                 scale=ln_s[0:NS, 2, QB:QB + 1]).then_inc(vout_step, 1)
            ytile = Count()

            def mix_tile(j, jy):
                ytile.step()
                split_next()
                for t in range(TT):
                    n = P if t < QB else NS
                    ins = nc.scalar.activation(vhat[0:n, t, :], v_nat[0:n, t, bass.ds(j * P, P)], ACT.Identity,
                                               bias=ln_s[0:n, 3, t:t + 1], scale=ln_s[0:n, 2, t:t + 1])
                ins.then_inc(vh_made, 1)
                split_next()
                accs.step(2)
                act.wait_ge(acc_read, accs.now(2))
                nc.scalar.activation(g_r[:, :], g_r[:, :], ACT.Silu).then_inc(silu_done, 1)
                wait_apart(act, y_made, ytile.now())
                nc.scalar.activation(act_hi[1][:, bass.ds(jy, 1), :].rearrange("p a t -> p (a t)"), s_t[:, :],
                                     ACT.Copy).then_inc(x_hi, 1)

            accs.step(ACC_UG - 1 - KT)
            for hf in range(HALF):
                with repeat(act, N_UG // SLOTS, (panel, SLOTS), (ytile, 2), (accs, 4)) as i:
                    for k in range(2):
                        mix_tile(i * 2 + (hf * KT + k), i * 2 + k)
                if hf == 0:
                    with repeat(act, KT // SLOTS, (panel, SLOTS), (accs, SLOTS)):
                        for k in range(SLOTS):
                            split_next()
                            accs.step()
                else:
                    with repeat(act, KT // SLOTS, (panel, SLOTS), (accs, SLOTS)) as i:
                        for k in range(SLOTS):
                            split_next()
                            split_x(i * SLOTS + k, 0)

            def embed(layer):
                for kt in range(PKT):
                    accs.step()
                    act.wait_ge(acc_read, accs.now(2))
                    nc.scalar.activation(p_hi[:, kt, :], p_t[:, kt, :], ACT.Copy).then_inc(p_hi_made, 1)
                for n in range(KT):
                    if n % 4 == 0:
                        split_next()
                        accs.step(4)
                    split_next()
                    if n == 0:
                        root()
                    accs.step()
                    act.wait_ge(acc_read, accs.now(2))
                    nc.scalar.activation(gate[:, n % 2, :], gate[:, n % 2, :], ACT.Sigmoid).then_inc(gate_sig, 1)
                    if layer == 0 and n > 0:
                        split_x(n - 1, 1, True)
                if layer == 0:
                    split_x(KT - 1, 1, True)

            embed(0)
            root()

            blk, wblk, opair, ah = Count(), Count(), Count(), Count()

            def exp_and_log():
                nc.scalar.preload_act_table_set("natural_log_exp_and_others")

            def logs(n, a):
                e, kb = n // QB, QB - 1 - n % QB
                w = (QB - kb) * P
                blk.step()
                z = absz[:, n % 2, 0:w]
                wait_apart(act, rel_done, blk.now())
                nc.scalar.activation(z, zb[n % 2][:, 0:w], ACT.Abs, bias=bias_of(a, e)).then_inc(act_step, 1)
                ah.step()
                act.wait_ge(act_step, ah.now())
                nc.scalar.activation(z, z, ACT.Exp, scale=-1.0).then_inc(act_step, 1)
                ah.step()
                act.wait_ge(act_step, ah.now())
                nc.scalar.activation(z, z, ACT.Ln, bias=1.0).then_inc(log_done, 1)

            def weights(n, a):
                e, kb = n // QB, QB - 1 - n % QB
                w = (QB - kb) * P
                wblk.step()
                wait_apart(act, after_done, wblk.now())
                nc.scalar.activation(wts[:, n % 2, 0:w], zb[n % 2][:, 0:w], ACT.Exp, bias=bias_of(a, e))\
                    .then_inc(exp_done, 1)

            def pair_step(i, par, dense, att, prev):
                for n in range(2 * QB):
                    if att and (n > 0 or prev):
                        weights((n - 1) % (2 * QB), i - 1 if n > 0 else i - 2)
                    if dense and n % 2 == 0:
                        split_next()
                    if att:
                        logs(n, i - 1)
                    if n == 2 and prev:
                        opair.step()
                        out_hi(i - 2)
                if att and not dense:
                    weights(2 * QB - 1, i - 1)
                    opair.step()
                    out_hi(i - 1)
                if dense:
                    accs.step(6)
                    act.wait_ge(acc_read, accs.now(2))
                    nc.scalar.activation(silu_g[:, par, :], gb_r[:, 0:TP], ACT.Silu)
                    nc.scalar.activation(silu_s[:, sl(i), :].rearrange("p a t -> p (a t)"), gb_r[:, TP:T], ACT.Silu)\
                        .then_inc(sg_ready, 1)
                    exp_and_log()

            def out_hi(a):
                wait_apart(act, o_read, opair.now(2))
                nc.scalar.activation(act_hi[0][:, sl(a), 0:TP].rearrange("p a t -> p (a t)"), o_s[:, :], ACT.Copy)\
                    .then_inc(o_hi, 1)

            pair_step(0, 0, True, False, False)
            pair_step(1, 1, True, True, False)
            with repeat(act, NP // 2 - 1, (panel, 8), (blk, 4 * QB), (wblk, 4 * QB), (ah, 8 * QB), (accs, 12),
                        (opair, 2)) as m:
                pair_step(m * 2 + 2, 0, True, True, True)
                pair_step(m * 2 + 3, 1, True, True, True)
            pair_step(NP, 0, False, True, True)

            samp = Count()

            def logs_s(src, dst):
                samp.step()
                act.wait_ge(xs_done, samp.now())
                nc.scalar.activation(dst, src, ACT.Abs).then_inc(act_step, 1)
                ah.step()
                act.wait_ge(act_step, ah.now())
                nc.scalar.activation(dst, dst, ACT.Exp, scale=-1.0).then_inc(act_step, 1)
                ah.step()
                act.wait_ge(act_step, ah.now())
                nc.scalar.activation(dst, dst, ACT.Ln, bias=1.0).then_inc(logs_done, 1)

            logs_s(xs_n[:, :, :], as_n[:, :, :])
            act.wait_ge(ds_done, 1)
            nc.scalar.activation(ws_n[:, :, :], xs_n[:, :, :], ACT.Exp).then_inc(exps_done, 1)
            with repeat(act, NB, (samp, 1), (ah, 2)):
                logs_s(xs_b[:, :, :, :], as_b[:, :, :, :])
                act.wait_ge(ds_done, samp.now())
                nc.scalar.activation(ws_b[:, :, :, :], d_b[:, :, :, :], ACT.Exp).then_inc(exps_done, 1)
            act.wait_ge(os_read, NB)
            nc.scalar.activation(act_hi[0][:, :, TP:T], os_s[:, :, :], ACT.Copy).then_inc(o_hi, 1)

            accs.step(ACC_BO - ACC_S)
            with repeat(act, KT // SLOTS, (panel, SLOTS), (accs, SLOTS)) as i:
                for k in range(SLOTS):
                    split_next()
                    split_x(i * SLOTS + k, 1)
            embed(1)
            root()

        @block.tensor
        def _(pe):
            panel, accs, blk = Count(), Count(), Count()

            def take_acc():
                pe.wait_ge(acc_read, accs.now(1))
                t = acc[accs.slot(2)]
                accs.step()
                return t

            def products(t, s, xh, xl, kts, start, stop):
                for kt in kts:
                    for wt, xt in ((w_hi, xh), (w_hi, xl), (w_lo, xh)):
                        for c in range(2):
                            mm = pe.matmul(t[:, c, 0:TH], wt[:, s, kt, :], xt[:, kt, c * TH:(c + 1) * TH],
                                           start=start and kt == kts[0] and wt is w_hi and xt is xh,
                                           stop=stop and kt == kts[-1] and wt is w_lo)
                return mm

            def gemm(a):
                pe.wait_ge(lo_made, panel.now(1))
                t = take_acc()
                s = panel.slot(SLOTS)
                products(t, s, act_hi[a], act_lo[a], range(KT), True, True).then_inc(panel_done, 1)
                panel.step()

            def turn_tokens(src):
                t = take_acc()
                for c in range(QB):
                    pe.transpose(t[:, 0, c * P:(c + 1) * P], src[:, c * P:(c + 1) * P], ident[:, :])
                pe.transpose(t[0:NS, 1, 0:P], src[:, TP:T], ident[:, :]).then_inc(turned, 1)

            def sum_squares():
                sums.step()
                pe.wait_ge(squared, sums.now() * KT)
                for c in range(2):
                    mm = pe.matmul(zb[c][:, 0:TH], ones[:, :], sumsq[:, c * TH:(c + 1) * TH], start=True, stop=True)
                mm.then_inc(ssq_out, 1)

            sums = Count()

            pe.wait_ge(const_set, N_CONST)
            pe.wait_ge(params_in, 16 * 8)
            t = take_acc()
            pe.transpose(t[:, 0, 0:N_COL], params[:, :], ident[0:N_COL, 0:N_COL]).then_inc(turned, 1)
            pe.wait_ge(x_in, 16 * TT)
            for n in range(KT):
                t = take_acc()
                for c in range(QB):
                    pe.transpose(t[:, 0, c * P:(c + 1) * P], x_nat[:, c, n * P:(n + 1) * P], ident[:, :])
                pe.transpose(t[:, 1, 0:NS], x_nat[0:NS, QB, n * P:(n + 1) * P], ident[0:NS, 0:NS])\
                    .then_inc(turned, 1)
            pe.wait_ge(small_in, 80)
            for half in range(2):
                t = take_acc()
                for g in range(NG // 2):
                    mm = pe.transpose(t[:, 0, g * P:(g + 1) * P], ws_nat[:, half * (NG // 2) + g, :], ident[:, :])
                mm.then_inc(turned, 1)
            sum_squares()
            pe.wait_ge(x_lo, KT)
            assert accs.now() == N_START

            with repeat(pe, N_AV // SLOTS, (panel, SLOTS), (accs, 2 * SLOTS)):
                for k in range(SLOTS + 1):
                    if k < SLOTS:
                        gemm(0)
                    if k > 0:
                        turn_tokens(vt[:, (k - 1) % 2, :])

            pe.wait_ge(ws_masked, 1)
            t = take_acc()
            pe.matmul(t[0:NS, 0, 0:NG * NQ], rep[:, :, :], ws_t[:, :, 0:NQ], start=True, stop=True)\
                .then_inc(turned, 1)
            for half in range(2):
                t = take_acc()
                pe.matmul(t[:, 0, :], ones[:, :], ws_t[:, half * 4:half * 4 + 4, :], start=True, stop=True)\
                    .then_inc(turned, 1)
            pe.wait_ge(acc_read, accs.now())
            t = take_acc()
            pe.matmul(t[:, 0, 0:NG * NS], ones[0:NS, :], ws_ts[:, :, :, :], start=True, stop=True)\
                .then_inc(turned, 1)

            ytile = Count()

            def spatial(k, g):
                ytile.step()
                pe.wait_ge(vh_made, ytile.now())
                gs = bass.ds(g, 1)
                for c in range(QB):
                    pe.matmul(zb[k][:, c * P:(c + 1) * P], vhat[:, c, :], ws_t[:, gs, :].rearrange("p a t -> p (a t)"),
                              start=True, stop=True)
                pe.matmul(ob[k][:, 0:NS], vhat[0:NS, QB, :],
                          ws_ts[:, gs, :, :].rearrange("p a b q -> p (a b q)"), start=True, stop=True)\
                    .then_inc(mixed, 1)

            for hf in range(HALF):
                with repeat(pe, N_UG // SLOTS, (panel, SLOTS), (accs, 4), (ytile, 2)) as i:
                    for k in range(2):
                        gemm(0)
                        spatial(k, i + hf * (NG // 2))
                        gemm(0)
                pe.wait_ge(x_lo, KT * (2 + hf))
                with repeat(pe, KT // SLOTS, (panel, SLOTS), (accs, SLOTS)):
                    for k in range(SLOTS):
                        gemm(1)

            def embed(layer, a):
                pe.wait_ge(p_in, 16 * TT * (layer + 1))
                for kt in range(PKT):
                    t = take_acc()
                    for c in range(QB):
                        pe.transpose(t[:, 0, c * P:(c + 1) * P], p_nat[:, c, kt * P:(kt + 1) * P], ident[:, :])
                    pe.transpose(t[:, 1, 0:NS], p_nat[0:NS, QB, kt * P:(kt + 1) * P], ident[0:NS, 0:NS])\
                        .then_inc(turned, 1)
                pe.wait_ge(p_lo_made, PKT * (layer + 1))
                for n in range(KT):
                    if n % 4 == 0:
                        pe.wait_ge(lo_made, panel.now(1))
                        s = panel.slot(SLOTS)
                        hi = w_hi[:, s, :, :].rearrange("p (kt a) n -> p kt (a n)", kt=PKT)
                        lo = w_lo[:, s, :, :].rearrange("p (kt a) n -> p kt (a n)", kt=PKT)
                        for m in range(4):
                            t = take_acc()
                            for kt in range(PKT):
                                for wt, xt in ((hi, p_hi), (hi, p_lo), (lo, p_hi)):
                                    for c in range(2):
                                        mm = pe.matmul(t[:, c, 0:TH], wt[:, kt, m * P:(m + 1) * P],
                                                       xt[:, kt, c * TH:(c + 1) * TH],
                                                       start=kt == 0 and wt is hi and xt is p_hi,
                                                       stop=kt == PKT - 1 and wt is lo)
                            mm.then_inc(panel_done if m == 3 else turned, 1)
                        panel.step()
                    if n == 0:
                        sum_squares()
                        pe.wait_ge(x_lo, KT * (4 + layer * 2))
                    gemm(a)

            embed(0, 0)
            sum_squares()
            pe.wait_ge(x_lo, KT * 5)

            wblk, opair = Count(), Count()

            def logits(n, par):
                e, kb = n // QB, QB - 1 - n % QB
                w = (QB - kb) * P
                if not (blk.reg is None and blk.now() < 2):
                    pe.wait_ge(exp_done, blk.now(-1))
                r = slice(e * DH, (e + 1) * DH)
                pe.matmul(zb[n % 2][:, 0:w], kt_t[r, par, kb * P:(kb + 1) * P], qt_t[r, par, kb * P:TP],
                          start=True, stop=False, skip_group_check=True)
                pe.matmul(zb[n % 2][:, 0:P], ident_b[:, :], unseen[:, :], start=False, stop=False,
                          skip_group_check=True).then_inc(z_full, 1)
                blk.step()

            def after(n):
                e, kb = n // QB, QB - 1 - n % QB
                w = (QB - kb) * P
                wblk.step()
                pe.wait_ge(soft_done, wblk.now())
                for later in range(QB - 1, kb, -1):
                    lw = (QB - later) * P
                    pe.matmul(zb[n % 2][:, w - lw:w], negones[:, :], soft[:, e, soft_at(later):soft_at(later) + lw],
                              start=False, stop=False, skip_group_check=True)
                pe.matmul(zb[n % 2][:, 0:w], negtri[:, :], soft[:, e, soft_at(kb):soft_at(kb) + w],
                          start=False, stop=True, skip_group_check=True).then_inc(after_done, 1)

            def values(n, par):
                e, kb = n // QB, QB - 1 - n % QB
                w = (QB - kb) * P
                pe.wait_ge(exp_done, wblk.now())
                if n == 0:
                    opair.step()
                    pe.wait_ge(o_read, opair.now())
                r = slice(e * DH, (e + 1) * DH)
                mm = pe.matmul(ob[par][r, kb * P:TP], vb_nat[:, par, kb, r], wts[:, n % 2, 0:w],
                               start=kb == QB - 1, stop=kb == 0, skip_group_check=True)
                if n == 2 * QB - 1:
                    mm.then_inc(o_full, 1)

            def pair_step(par, dense, att, prev):
                for n in range(2 * QB):
                    if att:
                        logits(n, 1 - par)
                    if att and (n > 0 or prev):
                        after((n - 1) % (2 * QB))
                    if dense:
                        s = panel.slot(SLOTS)
                        if n % 2 == 0:
                            pe.wait_ge(lo_made, panel.now(1))
                            t = take_acc()
                        half = range(KT // 2) if n % 2 == 0 else range(KT // 2, KT)
                        mm = products(t, s, act_hi[1], act_lo[1], half, n % 2 == 0, n % 2 == 1)
                        if n % 2 == 1:
                            mm.then_inc(panel_done, 1)
                            panel.step()
                    if att and (n > 0 or prev):
                        values((n - 1) % (2 * QB), 1 - par if n > 0 else par)
                    if dense and n == 3:
                        turn_tokens(kt_t[:, par, :])
                    if dense and n == 5:
                        turn_tokens(vt_t[:, :])
                if att and not dense:
                    after(2 * QB - 1)
                    values(2 * QB - 1, 1 - par)

            pair_step(0, True, False, False)
            pair_step(1, True, True, False)
            with repeat(pe, NP // 2 - 1, (panel, 8), (accs, 12), (blk, 4 * QB), (wblk, 4 * QB), (opair, 2)):
                pair_step(0, True, True, True)
                pair_step(1, True, True, True)
            pe.wait_ge(acc_read, accs.now(2 - 1))
            pair_step(0, False, True, True)

            pe.wait_ge(qbd_set, 3)
            for hp in range(NP):
                mm = pe.matmul(zb[0][0:NS, hp * 2 * NS:(hp + 1) * 2 * NS], kts[:, hp, :],
                               qbd[:, hp, :, :], start=hp == 0, stop=False, skip_group_check=True)
            pe.matmul(zb[0][0:NS, :], ident_b[0:NS, 0:NS], unseen_n[:, :, :, :], start=False, stop=False,
                      skip_group_check=True).then_inc(zs_full, 1)
            pe.wait_ge(softs_done, 1)
            pe.matmul(zb[0][0:NS, :], negtri[0:NS, 0:NS], sp_n[:, :, :], start=False, stop=True,
                      skip_group_check=True).then_inc(afters_done, 1)
            pe.wait_ge(exps_done, 1)

            seq = Count()

            def sequence(b, par, lap):
                pe.wait_ge(page_in[par], lap * (32 * PAGES) + 32 * PAGES)
                for two in range(KT // 2):
                    t = take_acc()
                    for m in range(2):
                        for g in range(PAGES):
                            mm = pe.transpose(t[:, m, g * P:(g + 1) * P],
                                              kpage[par][:, g, (2 * two + m) * P:(2 * two + m + 1) * P], ident[:, :])
                    mm.then_inc(turned, 1)
                pe.wait_ge(acc_read, accs.now(2))
                q = qbd[:, :, :, :].rearrange("p a e (b q) -> p a e b q", q=NQ)
                sn = sp_n[:, :, :].rearrange("p h (b q) -> p h b q", q=NQ)
                wn = ws_n[:, :, :].rearrange("p h (b q) -> p h b q", q=NQ)
                zv = zb[par][:, 0:PAGES * NH * NQ].rearrange("p (g h q) -> p g h q", g=PAGES, q=NQ)
                bs = bass.ds(b, 1)
                seq.step()
                for g in range(PAGES):
                    for hp in range(NP):
                        mm = pe.matmul(zv[:, g, 2 * hp:2 * hp + 2, :], ktb[:, hp, g * P:(g + 1) * P],
                                       q[:, hp, :, bs, :].rearrange("p e b q -> p e (b q)"),
                                       start=g == 0 and hp == 0, stop=False, skip_group_check=True)
                mm.then_inc(zs_full, 1)
                pe.wait_ge(softs_done, seq.now(1))
                for g in range(PAGES):
                    pe.matmul(zv[:, g, :, :], negones[0:NS, :], sn[:, :, bs, :].rearrange("p h b q -> p h (b q)"),
                              start=False, stop=False, skip_group_check=True)
                    for later in range(g + 1, PAGES):
                        pe.matmul(zv[:, g, :, :], negones[:, :], sp_b[:, later, :, :], start=False, stop=False,
                                  skip_group_check=True)
                    mm = pe.matmul(zv[:, g, :, :], negtri[:, :], sp_b[:, g, :, :], start=False,
                                   stop=g == PAGES - 1, skip_group_check=True)
                mm.then_inc(afters_done, 1)
                pe.wait_ge(exps_done, seq.now(1))
                ov = ob[par][:, 0:NH * NQ].rearrange("p (h q) -> p h q", q=NQ)
                for hp in range(NP):
                    hs = slice(2 * hp, 2 * hp + 2)
                    pe.matmul(ov[:, hs, :], vs_nat[:, hp * P:(hp + 1) * P],
                              wn[:, hs, bs, :].rearrange("p h b q -> p h (b q)"), start=hp == 0, stop=False,
                              skip_group_check=True)
                    for g in range(PAGES):
                        mm = pe.matmul(ov[:, hs, :], vpage[par][:, g, hp * P:(hp + 1) * P], ws_b[:, g, hs, :],
                                       start=False, stop=hp == NP - 1 and g == PAGES - 1, skip_group_check=True)
                mm.then_inc(os_full, 1)

            with repeat(pe, NB // 2, (accs, KT), (seq, 2)) as m:
                for par in range(2):
                    sequence(m * 2 + par, par, m)

            pe.wait_ge(o_lo, NP + 1)
            with repeat(pe, KT // SLOTS, (panel, SLOTS), (accs, SLOTS)):
                for k in range(SLOTS):
                    gemm(0)
            embed(1, 1)
            sum_squares()
            pe.wait_ge(y_scaled, KT)
            for tt in range(TT):
                n = P if tt < QB else NS
                t = take_acc()
                for kt in range(KT):
                    mm = pe.transpose(t[0:n, kt // 4, (kt % 4) * P:(kt % 4 + 1) * P],
                                      y_t[:, kt, tt * P:tt * P + n], ident[:, :])
                mm.then_inc(turned, 1)
            assert panel.now() == END

        @block.vector
        def _(dve):
            panel, done, accs, turns, own, xt = Count(), Count(), Count(), Count(), Count(), Count()

            def split_next():
                if panel.reg is None and panel.now() >= END:
                    return
                s = panel.slot(SLOTS)
                dve.wait_ge(hi_made, panel.now(1))
                dve.tensor_tensor(w_lo[:, s, :, :], raw[:, s, :, :], w_hi[:, s, :, :].bitcast(F32), ALU.subtract)\
                    .then_inc(lo_made, 1)
                panel.step()

            def product():
                done.step()
                dve.wait_ge(panel_done, done.now(SLOTS))
                t = acc[accs.slot(2)]
                accs.step()
                return t

            def turn():
                turns.step()
                dve.wait_ge(turned, turns.now())
                t = acc[accs.slot(2)]
                accs.step()
                return t

            def lo_x(n, into, src=None):
                xt.step()
                dve.wait_ge(x_hi, xt.now())
                one = lambda x: x[:, sl(n), :].rearrange("p a t -> p (a t)")
                dve.tensor_tensor(one(act_lo[into]), one(h) if src is None else src[:, :],
                                  one(act_hi[into]).bitcast(F32), ALU.subtract).then_inc(x_lo, 1)

            def add_product(n):
                t = product()
                hn = halves(h[:, sl(n), :].rearrange("p a t -> p (a t)"))
                dve.tensor_tensor(hn, both(t), hn, ALU.add).then_inc(acc_read, 1)

            def self_wait(ins):
                ins.then_inc(vec, 1)
                own.step()
                dve.wait_ge(vec, own.now())

            norms = Count()

            def inverse_root(r, m, scratch):
                self_wait(dve.reciprocal(r, r))
                self_wait(dve.tensor_tensor(scratch, r, r, ALU.mult))
                self_wait(dve.scalar_tensor_tensor(scratch, scratch, -0.5, m, ALU.mult, ALU.mult))
                self_wait(dve.scalar_tensor_tensor(r, scratch, 1.5, r, ALU.add, ALU.mult))

            def rms():
                norms.step()
                dve.wait_ge(ssq_out, norms.now())
                for c in range(2):
                    ins = dve.tensor_scalar(ms[:, c * TH:(c + 1) * TH], zb[c][:, 0:TH], 1.0 / D, EPS, ALU.mult,
                                            ALU.add)
                ins.then_inc(mean_sq, 1)
                roots.step()
                dve.wait_ge(rooted, roots.now())
                inverse_root(rinv[:, :], ms[:, :], sumsq[:, :])

            roots = Count()

            t = turn()
            dve.tensor_copy(cols[:, :], t[:, 0, 0:N_COL]).then_inc(acc_read, 1)
            for n in range(KT):
                t = turn()
                dve.tensor_copy(h[:, n, TP:T], t[:, 1, 0:NS])
                dve.tensor_copy(h[:, n, 0:TP], t[:, 0, 0:TP]).then_inc(acc_read, 1)
                if n > 0:
                    lo_x(n - 1, 0)
                if n < AHEAD:
                    split_next()
            lo_x(KT - 1, 0)
            for half in range(2):
                t = turn()
                dve.tensor_copy(ws_t[:, half * (NG // 2):(half + 1) * (NG // 2), :], t[:, 0, :]).then_inc(acc_read, 1)
            rms()

            with repeat(dve, N_AV // SLOTS, (panel, SLOTS), (done, SLOTS), (accs, 2 * SLOTS), (turns, SLOTS)) as i:
                for k in range(SLOTS + 1):
                    if k < SLOTS:
                        split_next()
                        t = product()
                        dve.tensor_tensor(halves(vt[:, k % 2, :]), both(t), halves(rinv[:, :]), ALU.mult)\
                            .then_inc(acc_read, 1)
                    if k > 0:
                        t = turn()
                        cs = bass.ds(i * (SLOTS * P) + (k - 1) * P, P)
                        dve.tensor_copy(v_nat[0:NS, QB, cs], t[0:NS, 1, 0:P])
                        dve.tensor_copy(v_nat[:, 0:QB, cs], t[:, 0, :].rearrange("p (c n) -> p c n", n=P))\
                            .then_inc(acc_read, 1)
                dve.wait_ge(acc_read, accs.now(2))
                for tt in range(TT):
                    n = P if tt < QB else NS
                    ins = dve.bn_stats(bst[0:n, tt, bass.ds(i, 1), :].rearrange("p a s -> p (a s)"),
                                       v_nat[0:n, tt, bass.ds(i * (SLOTS * P), SLOTS * P)])
                ins.then_inc(stats_done, 1)
            dve.wait_ge(stats_done, N_AV // SLOTS)
            for tt in range(TT):
                n = P if tt < QB else NS
                ins = dve.bn_aggr(mv[0:n, tt, :], bst[0:n, tt, :, :].rearrange("p a s -> p (a s)"))
            self_wait(ins)
            dve.tensor_scalar(ln_s[:, 0, :], mv[:, :, 1], EPS, None, ALU.add).then_inc(normed, 1)
            roots.step()
            dve.wait_ge(rooted, roots.now())
            inverse_root(ln_s[:, 1, :], ln_s[:, 0, :], ln_s[:, 2, :])
            dve.tensor_copy(ln_s[:, 2, :], ln_s[:, 1, :])
            dve.scalar_tensor_tensor(ln_s[:, 3, :], mv[:, :, 0], -1.0, ln_s[:, 1, :], ALU.mult, ALU.mult)\
                .then_inc(normed, 1)
            t = turn()
            dve.tensor_tensor(ws_ts[:, :, :, :],
                              t[0:NS, 0, 0:NG * NQ].rearrange("p (g q) -> p g q", q=NQ)[:, :, None, :]
                              .to_broadcast([NS, NG, NB, NQ]),
                              blockdiag[:, None, :, :].to_broadcast([NS, NG, NB, NQ]), ALU.mult)\
                .then_inc(acc_read, 1)
            for half in range(2):
                t = turn()
                dve.tensor_copy(row_sum[:, half * 4:half * 4 + 4, 0:P], t[:, 0, :].rearrange("p (g t) -> p g t", t=P))\
                    .then_inc(acc_read, 1)
            t = turn()
            dve.tensor_copy(row_sum[:, :, P:P + NS], t[:, 0, 0:NG * NS].rearrange("p (g t) -> p g t", t=NS))\
                .then_inc(acc_read, 1)
            dve.wait_ge(acc_read, accs.now(2))
            dve.wait_ge(bs_ready, 1)

            ytile = Count()
            for hf in range(HALF):
                with repeat(dve, N_UG // SLOTS, (panel, SLOTS), (done, SLOTS), (accs, SLOTS), (ytile, 2), (xt, 2),
                            (own, 2)) as i:
                    for k in range(2):
                        j = i * 2 + (hf * KT + k)
                        split_next()
                        t = product()
                        dve.tensor_tensor(halves(u_r[:, :]), both(t), halves(rinv[:, :]), ALU.mult)\
                            .then_inc(acc_read, 1)
                        gs = bass.ds(i + hf * (NG // 2), 1)
                        self_wait(dve.scalar_tensor_tensor(
                            bs_ln[:, :], row_sum[:, gs, :].rearrange("p a t -> p (a t)"), ln_b_c[:, bass.ds(j, 1)],
                            bs_bc[:, gs, :].rearrange("p a t -> p (a t)"), ALU.mult, ALU.add))
                        ytile.step()
                        dve.wait_ge(mixed, ytile.now())
                        dve.scalar_tensor_tensor(s_t[:, TP:T], ob[k][:, 0:NS], ln_g_c[:, bass.ds(j, 1)],
                                                 bs_ln[:, P:P + NS], ALU.mult, ALU.add)
                        dve.scalar_tensor_tensor(
                            s_t[:, 0:TP].rearrange("p (c t) -> p c t", t=P),
                            zb[k][:, :].rearrange("p (c t) -> p c t", t=P), ln_g_c[:, bass.ds(j, 1)],
                            bs_ln[:, None, 0:P].to_broadcast([P, QB, P]), ALU.mult, ALU.add).then_inc(s_ready, 1)
                        split_next()
                        t = product()
                        dve.tensor_tensor(halves(g_r[:, :]), both(t), halves(rinv[:, :]), ALU.mult)\
                            .then_inc(acc_read, 1)
                        lo_x(i * 2 + k, 1, s_t)
                if hf < HALF - 1:
                    with repeat(dve, KT // SLOTS, (panel, SLOTS), (done, SLOTS), (accs, SLOTS)) as i:
                        for k in range(SLOTS):
                            split_next()
                            add_product(i * SLOTS + k)
                else:
                    with repeat(dve, KT // SLOTS, (panel, SLOTS), (done, SLOTS), (accs, SLOTS), (xt, SLOTS)) as i:
                        for k in range(SLOTS):
                            split_next()
                            add_product(i * SLOTS + k)
                            lo_x(i * SLOTS + k, 0)

            gates = Count()

            def embed(layer):
                for kt in range(PKT):
                    t = turn()
                    dve.tensor_copy(p_t[:, kt, TP:T], t[:, 1, 0:NS])
                    dve.tensor_copy(p_t[:, kt, 0:TP], t[:, 0, 0:TP]).then_inc(acc_read, 1)
                dve.wait_ge(acc_read, accs.now(2))
                for kt in range(PKT):
                    dve.wait_ge(p_hi_made, layer * PKT + kt + 1)
                    dve.tensor_tensor(p_lo[:, kt, :], p_t[:, kt, :], p_hi[:, kt, :].bitcast(F32), ALU.subtract)\
                        .then_inc(p_lo_made, 1)

                def finish(n):
                    dve.wait_ge(gate_used, layer * KT + n + 1)
                    dve.tensor_tensor(h[:, n, :], h[:, n, :], gate[:, n % 2, :], ALU.add).then_inc(h_new, 1)

                for n in range(KT):
                    if n % 4 == 0:
                        if n > 0:
                            finish(n - 1)
                        split_next()
                        for m in range(4):
                            t = turn() if m < 3 else product()
                            dve.tensor_copy(halves(ple[:, m, :]), both(t)).then_inc(acc_read, 1)
                    if n == 0:
                        rms()
                    split_next()
                    t = product()
                    if n > 1:
                        dve.wait_ge(h_new, layer * KT + n - 1)
                    dve.tensor_tensor(halves(gate[:, n % 2, :]), both(t), halves(rinv[:, :]), ALU.mult)\
                        .then_inc(acc_read, 1)
                    if n > 0 and n % 4 != 0:
                        finish(n - 1)
                    if n > 1 and layer == 0:
                        lo_x(n - 2, 1)
                finish(KT - 1)
                if layer == 0:
                    lo_x(KT - 2, 1)
                    lo_x(KT - 1, 1)

            embed(0)
            rms()

            blk, opair, pair = Count(), Count(), Count()

            def relu_z(n, a):
                e, kb = n // QB, QB - 1 - n % QB
                w = (QB - kb) * P
                dve.wait_ge(z_full, blk.now(1))
                dve.tensor_scalar(relz[:, n % 2, 0:w], zb[n % 2][:, 0:w], bias_of(a, e), 0.0, ALU.add, ALU.max)\
                    .then_inc(rel_done, 1)

            def softplus(n):
                e, kb = n // QB, QB - 1 - n % QB
                w = (QB - kb) * P
                blk.step()
                dve.wait_ge(rel_done, blk.now())
                dve.wait_ge(log_done, blk.now())
                a = soft_at(kb)
                dve.tensor_tensor(soft[:, e, a:a + w], relz[:, n % 2, 0:w], absz[:, n % 2, 0:w], ALU.add)\
                    .then_inc(soft_done, 1)

            def out_pair(a, par):
                opair.step()
                dve.wait_ge(o_full, opair.now())
                dve.wait_ge(sg_ready, opair.now())
                dve.tensor_tensor(o_s[:, :], ob[par][:, :], silu_g[:, par, :], ALU.mult).then_inc(o_read, 1)
                dve.wait_ge(o_read, opair.now(2))
                dve.wait_ge(o_hi, opair.now())
                one = lambda x: x[:, sl(a), 0:TP].rearrange("p a t -> p (a t)")
                dve.tensor_tensor(one(act_lo[0]), o_s[:, :], one(act_hi[0]).bitcast(F32), ALU.subtract)\
                    .then_inc(o_lo, 1)

            def turned_pair(dst, dst_s, i, par):
                t = turn()
                cs = slice(i * P, (i + 1) * P) if isinstance(i, int) else bass.ds(i * P, P)
                dve.tensor_copy(dst_s[:, cs], t[0:NS, 1, 0:P])
                dve.tensor_copy(dst[:, par, :, :], t[:, 0, :].rearrange("p (c n) -> p c n", n=P))\
                    .then_inc(acc_read, 1)

            def pair_step(i, par, dense, att, prev, stored):
                for n in range(2 * QB):
                    if att:
                        relu_z(n, i - 1)
                    if dense and n % 2 == 1:
                        split_next()
                    if dense and n == 4:
                        if stored is not None:
                            dve.wait_ge(kv_out[par], stored)
                        turned_pair(k_nat, ks_nat, i, par)
                    if dense and n == 6:
                        turned_pair(vb_nat, vs_nat, i, par)
                    if att:
                        softplus(n)
                    if n == 2 and prev:
                        out_pair(i - 2, par)
                    if dense and n == 1:
                        t = product()
                        dve.tensor_tensor(kts[:, sl(i), :].rearrange("p a t -> p (a t)"), t[:, 1, TH - NS:TH],
                                          rinv[:, TP:T], ALU.mult)
                        dve.tensor_tensor(halves(kt_t[:, par, :]), both(t), halves(rinv[:, :]), ALU.mult)\
                            .then_inc(acc_read, 1)
                    if dense and n == 3:
                        t = product()
                        dve.tensor_tensor(halves(vt_t[:, :]), both(t), halves(rinv[:, :]), ALU.mult)\
                            .then_inc(acc_read, 1)
                    if dense and n == 5:
                        t = product()
                        dve.scalar_tensor_tensor(qts[:, sl(i), :].rearrange("p a t -> p (a t)"), t[:, 1, TH - NS:TH],
                                                 SCALE, rinv[:, TP:T], ALU.mult, ALU.mult)
                        dve.scalar_tensor_tensor(halves(qt_t[:, par, :]), both(t), SCALE, halves(rinv[:, :]),
                                                 ALU.mult, ALU.mult).then_inc(acc_read, 1)
                    if dense and n == 7:
                        t = product()
                        if att:
                            dve.wait_ge(sg_ready, i if isinstance(i, int) else i)
                        dve.tensor_tensor(halves(gb_r[:, :]), both(t), halves(rinv[:, :]), ALU.mult)\
                            .then_inc(acc_read, 1)
                if att and not dense:
                    out_pair(i - 1, 1 - par)

            pair_step(0, 0, True, False, False, None)
            pair_step(1, 1, True, True, False, None)
            with repeat(dve, NP // 2 - 1, (panel, 8), (done, 8), (accs, 12), (turns, 4), (blk, 4 * QB),
                        (opair, 2)) as m:
                pair_step(m * 2 + 2, 0, True, True, True, m * 32 + 32)
                pair_step(m * 2 + 3, 1, True, True, True, m * 32 + 32)
            pair_step(NP, 0, False, True, True, None)

            def soft_s(n, z, x, lg, sp, bc):
                dve.wait_ge(zs_full, n)
                dve.tensor_tensor(x, z, bc, ALU.add).then_inc(xs_done, 1)
                dve.wait_ge(xs_done, n)
                dve.wait_ge(logs_done, n)
                dve.scalar_tensor_tensor(sp, x, 0.0, lg, ALU.max, ALU.add).then_inc(softs_done, 1)

            z = zb[0][0:NS, :].rearrange("p (h t) -> p h t", t=NS)
            bc = bias[0:NS, :][:, :, None].to_broadcast([NS, NH, NS])
            soft_s(1, z, xs_n[:, :, :], as_n[:, :, :], sp_n[:, :, :], bc)
            dve.wait_ge(afters_done, 1)
            dve.tensor_tensor(xs_n[:, :, :], z, bc, ALU.add).then_inc(ds_done, 1)

            samp = Count(1)
            self_wait(dve.tensor_copy(bias_q[:, :, :], bias[:, :][:, :, None].to_broadcast([P, NH, NQ])))
            with repeat(dve, NB // 2, (turns, KT), (accs, KT), (samp, 2)) as m:
                for par in range(2):
                    samp.step()
                    for two in range(KT // 2):
                        t = turn()
                        dve.tensor_copy(ktb[:, 2 * two:2 * two + 2, :], t[:, :, :]).then_inc(acc_read, 1)
                    z = zb[par][:, 0:PAGES * NH * NQ].rearrange("p (g n) -> p g n", g=PAGES)
                    flat = lambda x: x[:, :, :, :].rearrange("p g h q -> p g (h q)")
                    bc = bias_q[:, :, :].rearrange("p h q -> p (h q)")[:, None, :].to_broadcast([P, PAGES, NH * NQ])
                    dve.wait_ge(zs_full, samp.now())
                    dve.tensor_tensor(flat(xs_b), z, bc, ALU.add).then_inc(xs_done, 1)
                    dve.wait_ge(xs_done, samp.now())
                    dve.wait_ge(logs_done, samp.now())
                    dve.scalar_tensor_tensor(sp_b[:, :, :, :].rearrange("p g h q -> p (g h q)"),
                                             xs_b[:, :, :, :].rearrange("p g h q -> p (g h q)"), 0.0,
                                             as_b[:, :, :, :].rearrange("p g h q -> p (g h q)"), ALU.max, ALU.add)\
                        .then_inc(softs_done, 1)
                    dve.wait_ge(afters_done, samp.now())
                    dve.tensor_tensor(flat(d_b), z, bc, ALU.add).then_inc(ds_done, 1)
                    dve.wait_ge(os_full, samp.now(-1))
                    bq = bass.ds(m * (2 * NQ) + par * NQ, NQ)
                    for e in range(2):
                        r = slice(e * DH, (e + 1) * DH)
                        ov = ob[par][r, 0:NH * NQ].rearrange("p (a e q) -> p a e q", e=2, q=NQ)[:, :, e, :]
                        ins = dve.tensor_tensor(os_s[r, :, bq], ov, silu_s[r, :, bq], ALU.mult)
                    ins.then_inc(os_read, 1)
            dve.wait_ge(os_read, NB)
            dve.wait_ge(o_hi, NP + 1)
            dve.tensor_tensor(act_lo[0][:, :, TP:T], os_s[:, :, :], act_hi[0][:, :, TP:T].bitcast(F32),
                              ALU.subtract).then_inc(o_lo, 1)

            with repeat(dve, KT // SLOTS, (panel, SLOTS), (done, SLOTS), (accs, SLOTS), (xt, SLOTS)) as i:
                for k in range(SLOTS):
                    split_next()
                    add_product(i * SLOTS + k)
                    lo_x(i * SLOTS + k, 1)
            embed(1)
            rms()
            for n in range(KT):
                dve.scalar_tensor_tensor(y_t[:, n, :], h[:, n, :], g_final_c[:, n:n + 1], rinv[:, :], ALU.mult,
                                         ALU.mult).then_inc(y_scaled, 1)
            for tt in range(TT):
                n = P if tt < QB else NS
                t = turn()
                dve.tensor_copy(y_nat[0:n, tt, :].rearrange("p (c n) -> p c n", c=2), t[0:n, :, :])\
                    .then_inc(acc_read, 1)
            assert panel.now() == END and accs.now() == ACC_END


_INS = ['x_prompt', 'x_sample', 'cache_k', 'cache_v', 'page_table', 'p_prompt', 'p_sample', 'g_norm', 'w_in_a',
        'ln_v_g', 'ln_v_b', 'w_spatial', 'b_spatial', 'w_out_a', 'g_kv', 'w_kv', 'w_in_b', 'w_out_b', 'b_sb',
        'w_ple', 'g_ple', 'w_ple_gate', 'g_final']


def kernel(**inputs):
    import numpy as _np
    import concourse.bacc as _bacc
    from concourse import mybir as _mybir
    from concourse.bass_utils import run_bass_kernel_spmd as _run

    nc = _bacc.Bacc("TRN2", target_bir_lowering=False, num_devices=1, dynamic_dma_scratch_size=1024)
    arrays, args = {}, []
    for name in _INS:
        a = _np.ascontiguousarray(inputs[name])
        arrays[f"in_{name}_dram"] = a
        args.append(nc.dram_tensor(f"in_{name}_dram", a.shape, _mybir.dt.from_np(a.dtype), kind="ExternalInput").ap())
    xp, xs = inputs['x_prompt'].shape, inputs['x_sample'].shape
    heads = tuple(inputs['cache_k'].shape[2:])
    e_a = inputs['ln_v_g'].shape[1]
    outs = [xp, xs, tuple(xp[:2]) + heads, tuple(xp[:2]) + heads, tuple(xs[:2]) + heads, tuple(xs[:2]) + heads,
            (1,) + tuple(xs[:2]) + (e_a,)]
    for i, shape in enumerate(outs):
        args.append(nc.dram_tensor(f"out_{i}_dram", tuple(shape), _mybir.dt.float32, kind="ExternalOutput").ap())
    build(nc, *args)
    r = _run(nc, [arrays], core_ids=[0])
    return tuple(r.results[0][f"out_{i}_dram"] for i in range(len(outs)))
```

```python
from contextlib import ExitStack, contextmanager

import concourse.bass as bass
from concourse import mybir

F32 = mybir.dt.float32
F32R = mybir.dt.float32r
BF16 = mybir.dt.bfloat16
I32 = mybir.dt.int32
ACT = mybir.ActivationFunctionType
ALU = mybir.AluOpType

P = 128
SLOTS = 4
AHEAD = 3
EPS = 1e-6
FAR = -1e30


class Count:

    def __init__(self, start=0):
        self.before, self.here, self.reg, self.per = start, 0, None, 0

    def now(self, ahead=0):
        n = self.before + self.here + ahead
        return n if self.reg is None else self.reg * self.per + n

    def step(self, n=1):
        self.here += n

    def slot(self, ring, ahead=0):
        assert self.per % ring == 0
        return (self.before + self.here + ahead) % ring

    def lap(self, ring, ahead=0):
        assert self.per % ring == 0
        n = (self.before + self.here + ahead) // ring
        return n if self.reg is None else self.reg * (self.per // ring) + n


@contextmanager
def repeat(eng, turns, *counts):
    with eng.Fori(0, turns) as i:
        for c, per in counts:
            c.before, c.here, c.reg, c.per = c.before + c.here, 0, i, per
        yield i
        for c, per in counts:
            assert c.here == per, (c.here, per)
    for c, per in counts:
        c.before, c.here, c.reg, c.per = c.before + per * turns, 0, None, 0


def build(nc, x_prompt, x_sample, cache_k, cache_v, page_table, p_prompt, p_sample, g_norm, w_in_a, ln_v_g,
          ln_v_b, w_spatial, b_spatial, w_out_a, g_kv, w_kv, w_in_b, w_out_b, b_sb, w_ple, g_ple, w_ple_gate,
          g_final, y_prompt, y_sample, k_prompt, v_prompt, k_sample, v_sample, chunk_v_sample):
    D = g_kv.shape[0]
    TP = x_prompt.shape[1]
    NB, NQ = x_sample.shape[0], x_sample.shape[1]
    NS = NB * NQ
    T = TP + NS
    TH = T // 2
    KT = D // P
    E_A = ln_v_g.shape[1]
    NG = w_spatial.shape[1]
    NH = b_sb.shape[1]
    DH = D // NH
    NP = NH // 2
    QB = TP // P
    TT = QB + 1
    PLE = p_prompt.shape[3]
    PKT = PLE // P
    NPOOL = cache_k.shape[0]
    PAGES = page_table.shape[1]
    HALF = E_A // D
    SCALE = float(DH) ** -0.5
    HQ = NH * NQ
    QZ = HQ + 2 * NQ
    assert TH * 2 == T and TP == QB * P and D == KT * P and E_A == HALF * D and NP == KT
    assert g_norm.shape[0] == 2 and PAGES == QB and SCALE == 0.125 and NG == HALF * 4

    w_in_a_v = w_in_a[0].rearrange("(kt p) n -> p kt n", p=P)
    w_out_a_v = w_out_a[0].rearrange("(hf kt p) n -> hf p kt n", p=P, hf=HALF)
    w_kv_v = w_kv.rearrange("(kt p) n -> p kt n", p=P)
    w_in_b_v = w_in_b[0].rearrange("(kt p) n -> p kt n", p=P)
    w_out_b_v = w_out_b[0].rearrange("(kt p) n -> p kt n", p=P)
    w_gate_v = w_ple_gate.rearrange("l (kt p) n -> l p kt n", p=P)
    w_ple_v = w_ple.rearrange("l (kt p) n -> l p kt n", p=P)
    xp_v = x_prompt[0].rearrange("(t p) d -> p t d", p=P)
    xs_v = x_sample.rearrange("b q d -> (b q) d")
    kp_v = k_prompt[0].rearrange("(t p) h d -> p t (h d)", p=P)
    vp_v = v_prompt[0].rearrange("(t p) h d -> p t (h d)", p=P)
    yp_v = y_prompt[0].rearrange("(t p) d -> p t d", p=P)
    ck_v = cache_k.rearrange("g t h d -> g t (h d)")
    cv_v = cache_v.rearrange("g t h d -> g t (h d)")

    N_AV = E_A // P
    N_UG = 2 * KT
    N_PL = KT
    END_AV = N_AV
    END_A = N_AV + HALF * (N_UG + KT)
    END_PL0 = END_A + N_PL
    END_B = END_PL0 + 4 * NP
    END_BO = END_B + KT
    END = END_BO + N_PL

    with ExitStack() as ctx:
        def sem(name):
            return ctx.enter_context(nc.semaphore(name))

        top = [nc.sbuf_base + (-nc.sbuf_base) % 32]

        def size(shape):
            n = 4
            for s in shape[1:]:
                n *= s
            return n + (-n) % 32

        def place(name, shape, dt=F32, at=None):
            where = top[0] if at is None else at[0]
            t = nc.alloc_sbuf_tensor_at(name, shape, dt, offset=where)
            if at is None:
                top[0] += size(shape)
            else:
                at[0] += size(shape)
            return t

        ident = place("ident", [P, P])
        ones = place("ones", [P, P])
        negtri = place("negtri", [P, P])
        negones = place("negones", [P, P])
        negtri_r = place("negtri_r", [P, P], F32R)
        negones_r = place("negones_r", [P, P], F32R)
        rep = place("rep", [P, NB, NQ])
        blockdiag = place("blockdiag", [NS, NB, NQ])
        ident_b = place("ident_b", [P, P], BF16)
        unseen = place("unseen", [P, P], BF16)
        unseen_n = place("unseen_n", [NS, NH, NB, NQ], BF16)
        N_COL = 2 * KT + KT + 2 * KT + KT + 2 * (E_A // P)
        cols = place("cols", [P, N_COL])
        bias = place("bias", [P, NH])
        eps = place("eps", [P, 1])
        bias_row = place("bias_row", [HQ, 1])
        pages = place("pages", [1, NB * PAGES], I32)
        bst = place("bst", [P, TT, N_AV // 4, 6])
        mv = place("mv", [P, TT, 2])
        ln_s = place("ln_s", [P, 4, TT])
        c0 = [0]

        def col(n):
            a = c0[0]
            c0[0] += n
            return cols[:, a:a + n]

        g_norm_c = [col(KT), col(KT)]
        g_kv_c = col(KT)
        g_ple_c = [col(KT), col(KT)]
        g_final_c = col(KT)
        ln_g_c = col(E_A // P)
        ln_b_c = col(E_A // P)

        h = place("h", [P, KT, T])
        ms = place("ms", [P, T])
        rinv = place("rinv", [P, T])
        sumsq = place("sumsq", [P, T])
        raw = place("raw", [P, SLOTS, KT, P])
        w_hi = place("w_hi", [P, SLOTS, KT, P], F32R)
        w_lo = place("w_lo", [P, SLOTS, KT, P], F32R)
        at_x0, at_x1 = [top[0]], [top[0] + 2 * size([P, KT, T])]
        top[0] += 4 * size([P, KT, T])
        x1_base = at_x1[0]
        x0_base = at_x0[0]
        act_hi = [place("act_hi0", [P, KT, T], F32R, at_x0), None]
        act_lo = [place("act_lo0", [P, KT, T], F32R, at_x0), None]
        act_hi[1] = place("act_hi1", [P, KT, T], F32R, at_x1)
        act_lo[1] = place("act_lo1", [P, KT, T], F32R, at_x1)
        at = [x1_base]
        vt = place("vt", [P, 2, T], F32, at)
        ws_nat = place("ws_nat", [P, NG, P], F32, at)
        params = place("params", [N_COL, P], F32, at)
        lng_bc = place("lng_bc", [NS, E_A], F32, at)
        lnb_bc = place("lnb_bc", [NS, E_A], F32, at)
        assert at[0] <= at_x1[0]

        area = top[0]
        at = [area]
        v_nat = place("v_nat", [P, TT, E_A], F32, at)
        vhat = place("vhat", [P, 2, TT, P], F32, at)
        ws_t = place("ws_t", [P, NG, P], F32, at)
        ws_ts = place("ws_ts", [NS, NG, NB, NQ], F32, at)
        row_sum = place("row_sum", [P, NG, P + NS], F32, at)
        bs_bc = place("bs_bc", [P, NG, P + NS], F32, at)
        bs_ln = place("bs_ln", [P, P + NS], F32, at)
        u_r = place("u_r", [P, T], F32, at)
        g_r = place("g_r", [P, T], F32, at)
        assert at[0] - size([P, T]) > area + size([P, TT, E_A])
        s_t = place("s_t", [P, T], F32, at)
        v_out = place("v_out", [NS, E_A], F32, at)
        ends = [at[0]]
        at = [area]
        x_nat = place("x_nat", [P, TT, D], F32, at)
        sq_x = place("sq_x", [P, KT, T], F32, at)
        assert at[0] <= area + size([P, TT, E_A])
        at = [area]
        p_nat = place("p_nat", [P, TT, PLE], F32, at)
        wp_raw = place("wp_raw", [P, PKT, D], F32, at)
        p_t = place("p_t", [P, PKT, T], F32, at)
        p_hi = place("p_hi", [P, PKT, T], F32R, at)
        p_lo = place("p_lo", [P, PKT, T], F32R, at)
        wp_hi = place("wp_hi", [P, PKT, D], F32R, at)
        wp_lo = place("wp_lo", [P, PKT, D], F32R, at)
        gate = place("gate", [P, 2, T], F32, at)
        sq_a = place("sq_a", [P, T], F32, at)
        ends.append(at[0])
        at = [area]
        kt_t = place("kt_t", [P, 2, T], F32, at)
        qt_t = place("qt_t", [P, 2, T], F32, at)
        vt_t = place("vt_t", [P, T], F32, at)
        k_nat = place("k_nat", [P, 2, QB, P], F32, at)
        vb_nat = place("vb_nat", [P, 2, QB, P], F32, at)
        gb_r = place("gb_r", [P, T], F32, at)
        silu_g = place("silu_g", [P, 2, TP], F32, at)
        soft_hi = place("soft_hi", [P, 2, QB * (QB + 1) // 2 * P], F32R, at)
        soft_lo = place("soft_lo", [P, 2, QB * (QB + 1) // 2 * P], F32R, at)
        absz = place("absz", [P, 2, TP], F32, at)
        relz = place("relz", [P, 2, TP], F32, at)
        wts = place("wts", [P, 2, TP], F32, at)
        o_s = place("o_s", [P, TP], F32, at)
        ats = [area]
        kp_hi = place("kp_hi", [P, KT, PAGES * P], F32R, ats)
        kp_lo = place("kp_lo", [P, KT, PAGES * P], F32R, ats)
        vpage1 = place("vpage1", [P, PAGES, D], F32, ats)
        at_s = [max(at[0], ats[0] + size([NS, NH, NS]) + 2 * size([P, NP * QZ]) + size([P, NP, 2, NS]) +
                    3 * size([NS, NH, NS]))]
        at_s0 = at_s[0]
        kts = place("kts", [P, NP, NS], F32, at_s)
        qts = place("qts", [P, NP, NS], F32, at_s)
        qts_hi = place("qts_hi", [P, NP, NS], F32R, at_s)
        qts_lo = place("qts_lo", [P, NP, NS], F32R, at_s)
        silu_s = place("silu_s", [P, NP, NS], F32, at_s)
        ks_nat = place("ks_nat", [NS, D], F32, at_s)
        vs_nat = place("vs_nat", [NS, D], F32, at_s)
        ends.append(at_s[0])
        sp_n = place("sp_n", [NS, NH, NS], F32, ats)
        qz_hi = place("qz_hi", [P, NP * QZ], F32R, ats)
        qz_lo = place("qz_lo", [P, NP * QZ], F32R, ats)
        new = [ats[0]]
        qbd = place("qbd", [P, NP, 2, NS], F32, ats)
        xs_n = place("xs_n", [NS, NH, NS], F32, ats)
        as_n = place("as_n", [NS, NH, NS], F32, ats)
        ws_n = place("ws_n", [NS, NH, NS], F32, ats)
        z_row = place("z_row", [HQ, PAGES * P], F32, new)
        sp_b = place("sp_b", [P, PAGES, HQ], F32, new)
        ws_b = place("ws_b", [P, PAGES, HQ], F32, new)
        o_row = place("o_row", [HQ, D], F32, new)
        assert new[0] <= ats[0] and PAGES * P == NH * NS
        assert ats[0] <= at_s0
        at = [x1_base]
        kpage = place("kpage", [P, PAGES, D], F32, at)
        vpage0 = place("vpage0", [P, PAGES, D], F32, at)
        os_s = place("os_s", [P, NP, NS], F32, at)
        on_s = place("on_s", [P, NP, NS], F32, at)
        assert at[0] <= at_x1[0]
        vpage = [vpage0, vpage1]
        at = [x0_base]
        y_t = place("y_t", [P, KT, T], F32, at)
        at = [max(ends[1], area)]
        y_nat = place("y_nat", [P, TT, D], F32, at)
        ends.append(at[0])
        assert max(ends) <= nc.sbuf_usable_end, (max(ends), nc.sbuf_usable_end)
        sq_b = sq_a

        acc = [ctx.enter_context(nc.psum_tensor(f"acc{n}", [P, 2, 512], F32)) for n in range(2)]
        zb = [ctx.enter_context(nc.psum_tensor(f"zb{n}", [P, 512], F32)) for n in range(2)]
        ob = [ctx.enter_context(nc.psum_tensor(f"ob{n}", [P, 512], F32)) for n in range(2)]

        def wait_apart(eng, semaphore, value):
            if isinstance(value, int):
                if value > 0:
                    eng.wait_ge(semaphore, value)
                return
            value = eng.to_reg(value)
            eng.wait_ge(const_set, N_CONST)
            eng.wait_ge(semaphore, value)

        def rows(ap, n):
            return ap.partition_broadcast(n)

        def both(t):
            return t[:, :, 0:TH]

        def halves(ap):
            return ap.rearrange("p (c t) -> p c t", c=2)

        const_set = sem("const_set")
        x_in = sem("x_in")
        params_in = sem("params_in")
        small_in = sem("small_in")
        p_in = sem("p_in")
        raw_in = [sem(f"raw_in{s}") for s in range(SLOTS)]
        raw_scaled = sem("raw_scaled")
        hi_made = sem("hi_made")
        lo_made = sem("lo_made")
        panel_done = sem("panel_done")
        turned = sem("turned")
        acc_read = sem("acc_read")
        x_squared = sem("x_squared")
        h_new = sem("h_new")
        x_hi = sem("x_hi")
        x_lo = sem("x_lo")
        squared = sem("squared")
        sq_step = sem("sq_step")
        ssq_out = sem("ssq_out")
        vec = sem("vec")
        mean_sq = sem("mean_sq")
        logged = sem("logged")
        rooted = sem("rooted")
        normed = sem("normed")
        ws_masked = sem("ws_masked")
        bs_ready = sem("bs_ready")
        vh_made = sem("vh_made")
        mixed = sem("mixed")
        silu_done = sem("silu_done")
        s_ready = sem("s_ready")
        us_done = sem("us_done")
        y_made = sem("y_made")
        vout_step = sem("vout_step")
        vout_done = sem("vout_done")
        out_done = sem("out_done")
        kv_out = [sem(f"kv_out{b}") for b in range(2)]
        p_hi_made = sem("p_hi_made")
        p_lo_made = sem("p_lo_made")
        stats_done = sem("stats_done")
        gate_sig = sem("gate_sig")
        wp_in = sem("wp_in")
        wp_hi_made = sem("wp_hi_made")
        wp_lo_made = sem("wp_lo_made")
        z_full = sem("z_full")
        rel_done = sem("rel_done")
        act_step = sem("act_step")
        log_done = sem("log_done")
        soft_done = sem("soft_done")
        soft_split = sem("soft_split")
        after_done = sem("after_done")
        exp_done = sem("exp_done")
        o_full = sem("o_full")
        o_read = sem("o_read")
        sg_ready = sem("sg_ready")
        o_hi = sem("o_hi")
        o_lo = sem("o_lo")
        k_in = sem("k_in")
        v_in = [sem(f"v_in{n}") for n in range(2)]
        bias_in = sem("bias_in")
        q_split = sem("q_split")
        qz_set = sem("qz_set")
        kp_hi_made = sem("kp_hi_made")
        zrow_full = sem("zrow_full")
        zrow_read = sem("zrow_read")
        os_sum = sem("os_sum")
        pages_in = sem("pages_in")
        qbd_set = sem("qbd_set")
        qz_zeroed = sem("qz_zeroed")
        zs_full = sem("zs_full")
        xs_done = sem("xs_done")
        logs_done = sem("logs_done")
        softs_done = sem("softs_done")
        afters_done = sem("afters_done")
        ds_done = sem("ds_done")
        exps_done = sem("exps_done")
        os_full = sem("os_full")
        os_read = sem("os_read")
        y_scaled = sem("y_scaled")

        N_CONST = 21

        N_START = 1 + KT + 2
        ACC_UG = N_START + 2 * N_AV + 4
        ACC_PL0 = ACC_UG + HALF * (N_UG + KT) + PKT
        ACC_B = ACC_PL0 + 2 * KT
        ACC_S = ACC_B + 6 * NP
        ACC_BO = ACC_S + NB * (KT // 2 + 1) + PKT
        TURN_S = N_START + N_AV + 4 + PKT + KT + 2 * NP
        TURNS_B = KT // 2 + 1
        ACC_Y = ACC_BO + 3 * KT
        ACC_END = ACC_Y + TT

        def sl(n):
            return slice(n, n + 1) if isinstance(n, int) else bass.ds(n, 1)

        def soft_at(kb):
            m = QB - 1 - kb
            return m * (m + 1) // 2 * P

        def bias_of(a, e):
            return bias[:, sl(a * 2 + e)]

        block = ctx.enter_context(nc.Block())

        @block.sync
        def _(sp):
            panel = Count()

            def load(src):
                if panel.reg is None and panel.now() < SLOTS:
                    pass
                else:
                    sp.wait_ge(lo_made, panel.now(1 - SLOTS))
                s = panel.slot(SLOTS)
                sp.dma_start(raw[:, s, :, :], src).then_inc(raw_in[s], 16)
                panel.step()

            for t in range(QB):
                sp.dma_start(x_nat[:, t, :], xp_v[:, t, :]).then_inc(x_in, 16)
            sp.dma_start(x_nat[0:NS, QB, :], xs_v).then_inc(x_in, 16)
            r = 0
            for src, n in ((g_norm[0], KT), (g_norm[1], KT), (g_kv, KT), (g_ple[0], KT), (g_ple[1], KT),
                           (g_final, KT), (ln_v_g[0], E_A // P), (ln_v_b[0], E_A // P)):
                sp.dma_start(params[r:r + n, :], src.rearrange("(r c) -> r c", c=P)).then_inc(params_in, 16)
                r += n
            for k in range(SLOTS):
                load(w_in_a_v[:, :, E_A + k * P:E_A + (k + 1) * P])
            sp.dma_start(ws_nat[:, :, :], w_spatial[0].rearrange("g t s -> t g s")).then_inc(small_in, 16)
            sp.dma_start(bs_bc[:, :, 0:P], rows(b_spatial[0], P)).then_inc(small_in, 16)
            sp.dma_start(bias[:, :], rows(b_sb[0], P)).then_inc(small_in, 16)
            sp.dma_start(lng_bc[:, :], rows(ln_v_g[0], NS)).then_inc(small_in, 16)
            sp.dma_start(lnb_bc[:, :], rows(ln_v_b[0], NS)).then_inc(small_in, 16)
            sp.dma_start(bias_row[:, :], b_sb[0].rearrange("(h a b) -> h a b", a=1, b=1).to_broadcast([NH, NQ, 1]))\
                .then_inc(bias_in, 16)
            sp.dma_start(pages[:, :], page_table.rearrange("(a b) g -> a (b g)", a=1)).then_inc(pages_in, 16)
            with repeat(sp, N_AV // SLOTS - 1, (panel, SLOTS)) as i:
                for k in range(SLOTS):
                    load(w_in_a_v[:, :, bass.ds(i * (SLOTS * P) + (E_A + (SLOTS + k) * P), P)])
            def embed_inputs(layer):
                for t in range(QB):
                    sp.dma_start(p_nat[:, t, :], p_prompt[layer, 0, t * P:(t + 1) * P, :]).then_inc(p_in, 16)
                sp.dma_start(p_nat[0:NS, QB, :], p_sample[layer].rearrange("b q e -> (b q) e")).then_inc(p_in, 16)
                sp.dma_start(wp_raw[:, :, :], w_ple_v[layer]).then_inc(wp_in, 16)

            for hf in range(HALF):
                with repeat(sp, N_UG // SLOTS, (panel, SLOTS)) as i:
                    for k in range(SLOTS):
                        at0 = hf * D + (k // 2) * P + (k % 2) * 2 * E_A
                        load(w_in_a_v[:, :, bass.ds(i * (2 * P) + at0, P)])
                if hf == HALF - 1:
                    for n in range(KT):
                        if n == AHEAD:
                            sp.wait_ge(vh_made, N_AV)
                            embed_inputs(0)
                        load(w_out_a_v[hf][:, :, n * P:(n + 1) * P])
                    continue
                with repeat(sp, KT // SLOTS, (panel, SLOTS)) as i:
                    for k in range(SLOTS):
                        load(w_out_a_v[hf][:, :, bass.ds(i * (SLOTS * P) + k * P, P)])
                if hf == 0:
                    sp.wait_ge(vout_done, 1)
                    sp.dma_start(chunk_v_sample[0].rearrange("b q e -> (b q) e"), v_out[:, :]).then_inc(out_done, 16)

            def embed_panels(layer):
                for n in range(KT):
                    load(w_gate_v[layer][:, :, n * P:(n + 1) * P])

            embed_panels(0)

            def load_pair(i):
                for k in range(2):
                    load(w_kv_v[:, :, bass.ds(i * P + k * D, P)] if not isinstance(i, int) else
                         w_kv_v[:, :, i * P + k * D:i * P + k * D + P])
                for k in range(2):
                    load(w_in_b_v[:, :, bass.ds(i * P + k * D, P)] if not isinstance(i, int) else
                         w_in_b_v[:, :, i * P + k * D:i * P + k * D + P])

            def store_pair(i, b):
                sp.wait_ge(acc_read, i * 6 + (ACC_B + 5 + 2))
                cs = bass.ds(i * P, P) if not isinstance(i, int) else slice(i * P, (i + 1) * P)
                sp.dma_start(kp_v[:, :, cs], k_nat[:, b, :, :]).then_inc(kv_out[b], 16)
                sp.dma_start(vp_v[:, :, cs], vb_nat[:, b, :, :]).then_inc(kv_out[b], 16)

            load_pair(0)
            load_pair(1)
            with repeat(sp, NP // 2 - 1, (panel, 8)) as m:
                for b in range(2):
                    load_pair(m * 2 + (2 + b))
                    store_pair(m * 2 + b, b)
            for n in range(AHEAD):
                load(w_out_b_v[:, :, n * P:(n + 1) * P])
            store_pair(NP - 2, 0)
            store_pair(NP - 1, 1)
            sp.dma_start(k_sample.rearrange("b q h d -> (b q) (h d)"), ks_nat[:, :]).then_inc(out_done, 16)
            sp.dma_start(v_sample.rearrange("b q h d -> (b q) (h d)"), vs_nat[:, :]).then_inc(out_done, 16)
            sp.wait_ge(pages_in, 16)

            def load_pages(k=None, v=None):
                for b, dst, src, landed in ((k, kpage, ck_v, k_in), (v, v is not None and vpage[v[1]], cv_v,
                                                                     v is not None and v_in[v[1]])):
                    if b is None:
                        continue
                    b = b[0]
                    for g in range(PAGES):
                        one = pages[0:1, bass.ds(b * PAGES + g, 1)] if not isinstance(b, int) else \
                            pages[0:1, b * PAGES + g:b * PAGES + g + 1]
                        page = sp.value_load(one, min_val=0, max_val=NPOOL - 1)
                        sp.dma_start(dst[:, g, :], src[bass.ds(page, 1), :, :].rearrange("a t d -> t (a d)"))\
                            .then_inc(landed, 16)

            sp.wait_ge(panel_done, END_B + SLOTS)
            load_pages((0,), (0, 0))
            sp.wait_ge(turned, TURN_S + KT // 2)
            load_pages((1,))
            sp.wait_ge(o_lo, NP)
            sp.wait_ge(kv_out[0], 16 * NP)
            sp.wait_ge(kv_out[1], 16 * NP)
            load_pages(None, (1, 1))
            with sp.Fori(0, NB // 2 - 1) as m:
                for b in range(2):
                    wait_apart(sp, turned, m * (2 * TURNS_B) + (TURN_S + TURNS_B * (b + 1) + KT // 2 - 1))
                    load_pages((m * 2 + (2 + b),))
                    wait_apart(sp, turned, m * (2 * TURNS_B) + (TURN_S + TURNS_B * (b + 1) + KT // 2))
                    load_pages(None, (m * 2 + (2 + b), b))
            sp.wait_ge(zrow_full, NB)
            embed_inputs(1)
            for n in range(AHEAD, KT):
                load(w_out_b_v[:, :, n * P:(n + 1) * P])
            embed_panels(1)
            for t in range(TT):
                sp.wait_ge(acc_read, ACC_Y + t + 1 + 2)
                if t < QB:
                    sp.dma_start(yp_v[:, t, :], y_nat[:, t, :]).then_inc(out_done, 16)
                else:
                    sp.dma_start(y_sample.rearrange("b q d -> (b q) d"), y_nat[0:NS, t, :]).then_inc(out_done, 16)
            sp.wait_ge(out_done, 16 * (3 + TT))
            assert panel.now() == END

        @block.gpsimd
        def _(pool):
            panel, accs, sq_n, news, blk = Count(), Count(), Count(), Count(), Count()

            pool.memset(ident[:, :], 0.0).then_inc(const_set, 1)
            pool.memset(ones[:, :], 1.0).then_inc(const_set, 1)
            pool.memset(negones[:, :], -1.0).then_inc(const_set, 1)
            pool.memset(negtri[:, :], -1.0).then_inc(const_set, 1)
            pool.memset(rep[:, :, :], 0.0).then_inc(const_set, 1)
            pool.memset(blockdiag[:, :, :], 1.0).then_inc(const_set, 1)
            pool.memset(mv[:, :, :], 1.0).then_inc(const_set, 1)
            pool.memset(eps[:, :], EPS).then_inc(const_set, 1)
            pool.memset(ws_ts[:, 0, 0, :], 0.0).then_inc(panel_done, SLOTS)
            pool.memset(ws_ts[:, 0, 1, :], 0.0).then_inc(acc_read, 2)
            pool.memset(ws_ts[:, 0, 2, :], 0.0).then_inc(o_read, 2)
            pool.memset(unseen[:, :], FAR).then_inc(const_set, 1)
            pool.memset(unseen_n[:, :, :, :], 0.0).then_inc(const_set, 1)
            pool.wait_ge(const_set, 10)
            pool.affine_select(out=ident[:, :], in_=ident[:, :], compare_op=ALU.not_equal, fill=1.0, base=0,
                               pattern=[[-1, P]], channel_multiplier=1).then_inc(const_set, 1)
            pool.affine_select(out=negtri[:, :], in_=negtri[:, :], compare_op=ALU.is_ge, fill=0.0, base=0,
                               pattern=[[-1, P]], channel_multiplier=1).then_inc(const_set, 1)
            pool.affine_select(out=rep[:, :, :], in_=rep[:, :, :], compare_op=ALU.not_equal, fill=1.0, base=0,
                               pattern=[[0, NB], [-1, NQ]], channel_multiplier=1).then_inc(const_set, 1)
            pool.affine_select(out=blockdiag[:, :, :], in_=blockdiag[:, :, :], compare_op=ALU.is_ge, fill=0.0,
                               base=0, pattern=[[-NQ, NB], [0, NQ]], channel_multiplier=1).then_inc(const_set, 1)
            pool.affine_select(out=unseen[:, :], in_=unseen[:, :], compare_op=ALU.is_ge, fill=0.0, base=0,
                               pattern=[[-1, P]], channel_multiplier=1).then_inc(const_set, 1)
            pool.affine_select(out=unseen_n[:, :, :, :], in_=unseen_n[:, :, :, :], compare_op=ALU.is_ge, fill=FAR,
                               base=0, pattern=[[0, NH], [-NQ, NB], [0, NQ]], channel_multiplier=1)\
                .then_inc(const_set, 1)
            pool.wait_ge(const_set, 16)
            pool.tensor_copy(ident_b[:, :], ident[:, :]).then_inc(const_set, 1)
            pool.tensor_copy(negtri_r[:, :], negtri[:, :]).then_inc(const_set, 1)
            pool.tensor_copy(negones_r[:, :], negones[:, :]).then_inc(const_set, 1)
            pool.affine_select(out=unseen_n[:, :, :, :], in_=unseen_n[:, :, :, :], compare_op=ALU.is_gt, fill=FAR,
                               base=0, pattern=[[0, NH], [NQ, NB], [1, NQ]], channel_multiplier=-1)\
                .then_inc(const_set, 1)
            pool.affine_select(out=blockdiag[:, :, :], in_=blockdiag[:, :, :], compare_op=ALU.is_ge, fill=0.0,
                               base=NQ - 1, pattern=[[NQ, NB], [0, NQ]], channel_multiplier=-1)\
                .then_inc(const_set, 1)

            def gain_of(p):
                if p < END_AV:
                    return g_norm_c[0]
                if p < END_A:
                    return g_norm_c[0] if (p - END_AV) % (N_UG + KT) < N_UG else None
                if p < END_PL0:
                    return g_ple_c[0]
                if p < END_B:
                    return g_kv_c if (p - END_PL0) % 4 < 2 else g_norm_c[1]
                if p < END_BO:
                    return None
                return g_ple_c[1]

            def scale(gain):
                s = panel.slot(SLOTS)
                pool.wait_ge(raw_in[s], panel.lap(SLOTS) * 16 + 16)
                if gain is None:
                    pool.engine_nop().then_inc(raw_scaled, 1)
                else:
                    pool.tensor_tensor(raw[:, s, :, :], raw[:, s, :, :], gain[:, :, None].to_broadcast([P, KT, P]),
                                       ALU.mult).then_inc(raw_scaled, 1)
                panel.step()

            def scale_next():
                if panel.reg is None and panel.now() >= END:
                    return
                p = panel.before + panel.here
                if panel.reg is not None:
                    for t in range(turns[0]):
                        assert gain_of(p + t * panel.per) is gain_of(p)
                scale(gain_of(p))

            turns = [0]

            sq_scratch = [g_r]

            def squares(n, embedded=False):
                if embedded:
                    news.step()
                    pool.wait_ge(h_new, news.now())
                else:
                    accs.step()
                    pool.wait_ge(acc_read, accs.now(2))
                sq_n.step()
                hn = h[:, n, :]
                if n == 0:
                    pool.tensor_tensor(sumsq[:, :], hn, hn, ALU.mult).then_inc(squared, 1)
                    return
                pool.wait_ge(squared, sq_n.now(-1))
                pool.tensor_tensor(sq_scratch[0][:, :], hn, hn, ALU.mult).then_inc(sq_step, 1)
                sq_steps.step()
                pool.wait_ge(sq_step, sq_steps.now())
                pool.tensor_tensor(sumsq[:, :], sumsq[:, :], sq_scratch[0][:, :], ALU.add).then_inc(squared, 1)

            sq_steps = Count()

            pool.wait_ge(acc_read, 2 + 1)
            for _ in range(AHEAD):
                scale_next()
            for n in range(KT):
                pool.wait_ge(x_squared, n + 1)
                sq_n.step()
                if n == 0:
                    pool.engine_nop().then_inc(squared, 1)
                    continue
                if n > 1:
                    pool.wait_ge(squared, sq_n.now(-1))
                pool.tensor_tensor(sumsq[:, :], sq_x[:, 0, :] if n == 1 else sumsq[:, :], sq_x[:, n, :], ALU.add)\
                    .then_inc(squared, 1)
            accs.step(1 + KT + 2)
            pool.wait_ge(acc_read, accs.now(2))
            pool.affine_select(out=ws_t[:, :, :], in_=ws_t[:, :, :], compare_op=ALU.is_ge, fill=0.0, base=0,
                               pattern=[[0, NG], [1, P]], channel_multiplier=-1).then_inc(ws_masked, 1)
            pool.wait_ge(small_in, 80)
            pool.tensor_copy(bs_bc[:, :, P:P + NS].rearrange("p g (b q) -> p g b q", q=NQ),
                             bs_bc[:, :, 0:NQ][:, :, None, :].to_broadcast([P, NG, NB, NQ]))\
                .then_inc(bs_ready, 1)

            turns[0] = N_AV // SLOTS - 1
            with repeat(pool, turns[0], (panel, SLOTS)):
                for k in range(SLOTS):
                    scale_next()
            for k in range(SLOTS):
                scale_next()
            pool.wait_ge(vout_step, 1)
            pool.tensor_tensor(v_out[:, :], v_out[:, :], lng_bc[:, :], ALU.mult).then_inc(vout_step, 1)
            pool.wait_ge(vout_step, 2)
            pool.tensor_tensor(v_out[:, :], v_out[:, :], lnb_bc[:, :], ALU.add).then_inc(vout_done, 1)
            ytile = Count()

            def mix(hf):
                def turn():
                    for k in range(2):
                        scale_next()
                        scale_next()
                        ytile.step()
                        pool.wait_ge(s_ready, ytile.now())
                        pool.tensor_tensor(u_r[:, :], u_r[:, :], s_t[:, :], ALU.mult).then_inc(us_done, 1)
                        pool.wait_ge(us_done, ytile.now())
                        pool.wait_ge(silu_done, ytile.now())
                        pool.tensor_tensor(s_t[:, :], u_r[:, :], g_r[:, :], ALU.mult).then_inc(y_made, 1)

                turns[0] = N_UG // SLOTS - 1
                with repeat(pool, turns[0], (panel, SLOTS), (ytile, 2)):
                    turn()
                turn()

            mix(0)
            for n in range(KT):
                scale_next()
            mix(1)
            accs.step(ACC_PL0 - KT - N_START)
            for n in range(KT):
                scale_next()
                squares(n)
            sq_scratch[0] = sq_a

            def embed():
                for n in range(KT):
                    scale_next()
                    if n > 0:
                        squares(n - 1, True)
                squares(KT - 1, True)

            embed()

            turns[0] = NP - 1
            with repeat(pool, turns[0], (panel, 4)):
                for k in range(4):
                    scale_next()
            for k in range(4):
                scale_next()

            pool.wait_ge(acc_read, ACC_S - 2 + 2)
            pool.wait_ge(o_lo, NP)
            pool.memset(qbd[:, :, :, :], 0.0).then_inc(qbd_set, 1)
            pool.wait_ge(qbd_set, 1)
            for e in range(2):
                r = slice(e * DH, (e + 1) * DH)
                pool.tensor_copy(qbd[r, :, e, :], qts[r, :, :]).then_inc(qbd_set, 1)
            pool.wait_ge(qbd_set, 3)
            pool.memset(qz_hi[:, :].bitcast(F32), 0.0).then_inc(qz_zeroed, 1)
            pool.wait_ge(qz_zeroed, 1)
            pool.memset(qz_lo[:, :].bitcast(F32), 0.0).then_inc(qz_zeroed, 1)
            pool.wait_ge(qz_zeroed, 2)
            pool.wait_ge(q_split, 2)

            def queries(b):
                bq = slice(b * NQ, (b + 1) * NQ) if isinstance(b, int) else bass.ds(b * NQ, NQ)
                for n, (dst, src) in enumerate(((qz_hi, qts_hi), (qz_lo, qts_lo))):
                    wait_apart(pool, qz_set, b * 4 + 2 * n)
                    for e in range(2):
                        r = slice(e * DH, (e + 1) * DH)
                        pool.tensor_copy(dst[r, :].rearrange("p (a n) -> p a n", n=QZ)[:, :, e * NQ:(e + 1) * NQ],
                                         src[r, :, bq]).then_inc(qz_set, 1)

            queries(0)
            with pool.Fori(0, NB - 1) as m:
                wait_apart(pool, zrow_full, m + 1)
                queries(m + 1)

            accs.step(ACC_BO - ACC_PL0)
            for n in range(KT):
                scale_next()
                squares(n)
            embed()

        @block.scalar
        def _(act):
            panel, accs, news, roots = Count(), Count(), Count(), Count()

            def split_next():
                if panel.reg is None and panel.now() >= END:
                    return
                s = panel.slot(SLOTS)
                act.wait_ge(raw_scaled, panel.now(1))
                act.wait_ge(panel_done, panel.now(1))
                nc.scalar.activation(w_hi[:, s, :, :], raw[:, s, :, :], ACT.Copy).then_inc(hi_made, 1)
                panel.step()

            def split_x(n, into, embedded=False):
                if embedded:
                    news.step()
                    act.wait_ge(h_new, news.now())
                else:
                    accs.step()
                    wait_apart(act, acc_read, accs.now(2))
                nc.scalar.activation(act_hi[into][:, sl(n), :], h[:, sl(n), :], ACT.Copy).then_inc(x_hi, 1)

            def exp_and_log():
                nc.scalar.preload_act_table_set("natural_log_exp_and_others")

            def root():
                roots.step()
                exp_and_log()
                act.wait_ge(ssq_out, norms.now(1))
                for c in range(2):
                    ins = nc.scalar.activation(rinv[:, c * TH:(c + 1) * TH], zb[c][:, 0:TH], ACT.Ln, scale=1.0 / D,
                                               bias=eps[:, 0:1])
                ins.then_inc(logged, 1)
                norms.step()
                act.wait_ge(logged, norms.now())
                nc.scalar.activation(rinv[:, :], rinv[:, :], ACT.Exp, scale=-0.5).then_inc(rooted, 1)

            norms = Count()

            accs.step()
            def split_p(layer):
                for kt in range(PKT):
                    accs.step()
                    act.wait_ge(acc_read, accs.now(2))
                    nc.scalar.activation(p_hi[:, kt, :], p_t[:, kt, :], ACT.Copy).then_inc(p_hi_made, 1)
                act.wait_ge(wp_in, 16 * (layer + 1))
                nc.scalar.activation(wp_hi[:, :, :], wp_raw[:, :, :], ACT.Copy).then_inc(wp_hi_made, 1)

            for n in range(KT):
                split_x(n, 0)
                nc.scalar.activation(sq_x[:, n, :], h[:, n, :], ACT.Square).then_inc(x_squared, 1)
                if n >= KT - AHEAD:
                    split_next()
            root()
            with repeat(act, N_AV // SLOTS, (panel, SLOTS)):
                for k in range(SLOTS):
                    split_next()
            act.wait_ge(normed, 1)
            nc.scalar.activation(ln_s[:, 1, :], ln_s[:, 0, :], ACT.Sqrt).then_inc(rooted, 1)
            act.wait_ge(normed, 2)
            nc.scalar.activation(v_out[:, :], v_nat[0:NS, QB, :], ACT.Identity, bias=ln_s[0:NS, 3, QB:QB + 1],
                                 scale=ln_s[0:NS, 2, QB:QB + 1]).then_inc(vout_step, 1)
            ytile = Count()

            def normalise(j, k):
                for t in range(TT):
                    n = P if t < QB else NS
                    ins = nc.scalar.activation(vhat[0:n, k, t, :], v_nat[0:n, t, bass.ds(j * P, P)], ACT.Identity,
                                               bias=ln_s[0:n, 3, t:t + 1], scale=ln_s[0:n, 2, t:t + 1])
                ins.then_inc(vh_made, 1)

            def mix_tile(j, jy, k, last=False):
                ytile.step()
                split_next()
                split_next()
                accs.step(2)
                act.wait_ge(acc_read, accs.now(2))
                nc.scalar.activation(g_r[:, :], g_r[:, :], ACT.Silu).then_inc(silu_done, 1)
                if not last:
                    normalise(j + 1, 1 - k)
                wait_apart(act, y_made, ytile.now())
                nc.scalar.activation(act_hi[1][:, bass.ds(jy, 1), :].rearrange("p a t -> p (a t)"), s_t[:, :],
                                     ACT.Copy).then_inc(x_hi, 1)

            accs.step(ACC_UG - 1 - KT)
            normalise(0, 0)
            for hf in range(HALF):
                turns = N_UG // SLOTS - (1 if hf == HALF - 1 else 0)
                with repeat(act, turns, (panel, SLOTS), (ytile, 2), (accs, 4)) as i:
                    for k in range(2):
                        mix_tile(i * 2 + (hf * KT + k), i * 2 + k, k)
                if hf == HALF - 1:
                    for k in range(2):
                        mix_tile(HALF * KT - 2 + k, KT - 2 + k, k, k == 1)
                    split_p(0)
                if hf == 0:
                    with repeat(act, KT // SLOTS, (panel, SLOTS), (accs, SLOTS)):
                        for k in range(SLOTS):
                            split_next()
                            accs.step()
                else:
                    with repeat(act, KT // SLOTS, (panel, SLOTS), (accs, SLOTS)) as i:
                        for k in range(SLOTS):
                            split_next()
                            split_x(i * SLOTS + k, 0)

            def embed(layer):
                for n in range(KT):
                    if n == 0:
                        root()
                    split_next()
                    accs.step()
                    act.wait_ge(acc_read, accs.now(2))
                    nc.scalar.activation(gate[:, n % 2, :], gate[:, n % 2, :], ACT.Sigmoid).then_inc(gate_sig, 1)
                    accs.step()
                    if n > 0:
                        embedded(layer, n - 1)
                embedded(layer, KT - 1)

            def embedded(layer, n):
                if layer == 0:
                    split_x(n, 1, True)
                    return
                news.step()
                act.wait_ge(h_new, news.now())
                nc.scalar.activation(y_t[:, n, :], h[:, n, :], ACT.Identity, scale=g_final_c[:, n:n + 1])\
                    .then_inc(y_scaled, 1)

            embed(0)
            root()

            blk, wblk, opair, ah = Count(), Count(), Count(), Count()

            def logs(n, a):
                e, kb = n // QB, QB - 1 - n % QB
                w = (QB - kb) * P
                blk.step()
                z = absz[:, n % 2, 0:w]
                wait_apart(act, z_full, blk.now())
                nc.scalar.activation(z, zb[n % 2][:, 0:w], ACT.Abs, bias=bias_of(a, e)).then_inc(act_step, 1)
                ah.step()
                act.wait_ge(act_step, ah.now())
                nc.scalar.activation(z, z, ACT.Exp, scale=-1.0).then_inc(act_step, 1)
                ah.step()
                act.wait_ge(act_step, ah.now())
                nc.scalar.activation(z, z, ACT.Ln, bias=1.0).then_inc(log_done, 1)

            def weights(n, a):
                e, kb = n // QB, QB - 1 - n % QB
                w = (QB - kb) * P
                wblk.step()
                wait_apart(act, after_done, wblk.now())
                nc.scalar.activation(wts[:, n % 2, 0:w], zb[n % 2][:, 0:w], ACT.Exp, bias=bias_of(a, e))\
                    .then_inc(exp_done, 1)

            def pair_step(i, par, dense, att, prev):
                for n in range(2 * QB):
                    if att:
                        logs(n, i - 1)
                    if att and (n > 0 or prev):
                        weights((n - 1) % (2 * QB), i - 1 if n > 0 else i - 2)
                    if dense and n % 2 == 0:
                        split_next()
                    if n == 2 and prev:
                        opair.step()
                        out_hi(i - 2)
                if att and not dense:
                    weights(2 * QB - 1, i - 1)
                    opair.step()
                    out_hi(i - 1)
                if dense:
                    accs.step(6)
                    act.wait_ge(acc_read, accs.now(2))
                    nc.scalar.activation(silu_g[:, par, :], gb_r[:, 0:TP], ACT.Silu)
                    nc.scalar.activation(silu_s[:, sl(i), :].rearrange("p a t -> p (a t)"), gb_r[:, TP:T], ACT.Silu)\
                        .then_inc(sg_ready, 1)
                    exp_and_log()

            def out_hi(a):
                wait_apart(act, o_read, opair.now(2))
                nc.scalar.activation(act_hi[0][:, sl(a), 0:TP].rearrange("p a t -> p (a t)"), o_s[:, :], ACT.Copy)\
                    .then_inc(o_hi, 1)

            pair_step(0, 0, True, False, False)
            pair_step(1, 1, True, True, False)
            with repeat(act, NP // 2 - 1, (panel, 8), (blk, 4 * QB), (wblk, 4 * QB), (ah, 8 * QB), (accs, 12),
                        (opair, 2)) as m:
                pair_step(m * 2 + 2, 0, True, True, True)
                pair_step(m * 2 + 3, 1, True, True, True)
            nc.scalar.activation(qts_hi[:, :, :], qts[:, :, :], ACT.Copy).then_inc(q_split, 1)
            pair_step(NP, 0, False, True, True)

            samp = Count()

            def logs_s(dst):
                ah.step()
                act.wait_ge(act_step, ah.now())
                nc.scalar.activation(dst, dst, ACT.Exp, scale=-1.0).then_inc(act_step, 1)
                ah.step()
                act.wait_ge(act_step, ah.now())
                nc.scalar.activation(dst, dst, ACT.Ln, bias=1.0).then_inc(logs_done, 1)

            tiles = Count(TURN_S)

            def split_keys():
                for two in range(KT // 2):
                    tiles.step()
                    wait_apart(act, turned, tiles.now())
                    nc.scalar.activation(kp_hi[:, 2 * two:2 * two + 2, :], acc[tiles_acc.slot(2)][:, :, :], ACT.Copy)\
                        .then_inc(kp_hi_made, 1)
                    tiles_acc.step()

            def weights_s(par):
                samp.step()
                wait_apart(act, afters_done, samp.now())
                nc.scalar.activation(ws_b[:, :, :].rearrange("p g n -> p (g n)"), zb[par][:, 0:PAGES * HQ], ACT.Exp)\
                    .then_inc(exps_done, 1)
                tiles.step()
                tiles_acc.step()

            def step_s(par, more):
                wait_apart(act, zs_full, samp.now(1))
                nc.scalar.activation(sp_b[:, :, :].rearrange("p g n -> p (g n)"), zb[par][:, 0:PAGES * HQ], ACT.Abs)\
                    .then_inc(act_step, 1)
                logs_s(sp_b[:, :, :].rearrange("p g n -> p (g n)"))
                if more:
                    split_keys()
                weights_s(par)

            tiles_acc = Count(ACC_S)
            act.wait_ge(kv_out[0], 16 * NP)
            act.wait_ge(kv_out[1], 16 * NP)
            split_keys()
            act.wait_ge(xs_done, 1)
            nc.scalar.activation(as_n[:, :, :], xs_n[:, :, :], ACT.Abs).then_inc(act_step, 1)
            logs_s(as_n[:, :, :])
            samp.step()
            act.wait_ge(ds_done, 1)
            nc.scalar.activation(ws_n[:, :, :], xs_n[:, :, :], ACT.Exp).then_inc(exps_done, 1)
            step_s(0, True)
            with repeat(act, NB // 2 - 1, (samp, 2), (ah, 4), (tiles, 2 * TURNS_B), (tiles_acc, 2 * TURNS_B)):
                step_s(1, True)
                step_s(0, True)
            step_s(1, False)
            act.wait_ge(os_sum, 1)
            nc.scalar.activation(act_hi[0][:, :, TP:T], os_s[:, :, :], ACT.Copy).then_inc(o_hi, 1)

            accs.step(ACC_BO - PKT - ACC_S)
            split_p(1)
            with repeat(act, KT // SLOTS, (panel, SLOTS), (accs, SLOTS)) as i:
                for k in range(SLOTS):
                    split_next()
                    split_x(i * SLOTS + k, 1)
            embed(1)
            roots.step()
            act.wait_ge(mean_sq, 1)
            nc.scalar.activation(ln_s[:, 1, :], ln_s[:, 0, :], ACT.Sqrt).then_inc(rooted, 1)

        @block.tensor
        def _(pe):
            panel, accs, blk = Count(), Count(), Count()

            def take_acc():
                pe.wait_ge(acc_read, accs.now(1))
                t = acc[accs.slot(2)]
                accs.step()
                return t

            def products(t, s, xh, xl, kts, start, stop, split=None, sum_at=None):
                for kt in kts:
                    if kt == sum_at:
                        sum_squares()
                    if split is not None:
                        pe.wait_ge(x_lo, split + kt + 1)
                    for wt, xt in ((w_hi, xh), (w_hi, xl), (w_lo, xh)):
                        for c in range(2):
                            mm = pe.matmul(t[:, c, 0:TH], wt[:, s, kt, :], xt[:, kt, c * TH:(c + 1) * TH],
                                           start=start and kt == kts[0] and wt is w_hi and xt is xh,
                                           stop=stop and kt == kts[-1] and wt is w_lo)
                return mm

            def gemm(a, split=None, sum_at=None):
                pe.wait_ge(lo_made, panel.now(1))
                t = take_acc()
                s = panel.slot(SLOTS)
                products(t, s, act_hi[a], act_lo[a], range(KT), True, True, split, sum_at).then_inc(panel_done, 1)
                panel.step()

            def turn_tokens(src):
                t = take_acc()
                for c in range(QB):
                    pe.transpose(t[:, 0, c * P:(c + 1) * P], src[:, c * P:(c + 1) * P], ident[:, :])
                pe.transpose(t[0:NS, 1, 0:P], src[:, TP:T], ident[:, :]).then_inc(turned, 1)

            def sum_squares():
                sums.step()
                pe.wait_ge(squared, sums.now() * KT)
                for c in range(2):
                    mm = pe.matmul(zb[c][:, 0:TH], ones[:, :], sumsq[:, c * TH:(c + 1) * TH], start=True, stop=True)
                mm.then_inc(ssq_out, 1)

            sums = Count()

            pe.wait_ge(const_set, N_CONST)
            pe.wait_ge(params_in, 16 * 8)
            t = take_acc()
            pe.transpose(t[:, 0, 0:N_COL], params[:, :], ident[0:N_COL, 0:N_COL]).then_inc(turned, 1)
            pe.wait_ge(x_in, 16 * TT)
            for n in range(KT):
                t = take_acc()
                for c in range(QB):
                    pe.transpose(t[:, 0, c * P:(c + 1) * P], x_nat[:, c, n * P:(n + 1) * P], ident[:, :])
                pe.transpose(t[:, 1, 0:NS], x_nat[0:NS, QB, n * P:(n + 1) * P], ident[0:NS, 0:NS])\
                    .then_inc(turned, 1)
            pe.wait_ge(small_in, 80)
            for half in range(2):
                t = take_acc()
                for g in range(NG // 2):
                    mm = pe.transpose(t[:, 0, g * P:(g + 1) * P], ws_nat[:, half * (NG // 2) + g, :], ident[:, :])
                mm.then_inc(turned, 1)
            assert accs.now() == N_START

            def value_tiles(first=False):
                for k in range(SLOTS + 1):
                    if k < SLOTS:
                        if first and k == 0:
                            gemm(0, 0, 2)
                        else:
                            gemm(0)
                    if k > 0:
                        turn_tokens(vt[:, (k - 1) % 2, :])

            value_tiles(True)
            with repeat(pe, N_AV // SLOTS - 1, (panel, SLOTS), (accs, 2 * SLOTS)):
                value_tiles()

            pe.wait_ge(ws_masked, 1)
            t = take_acc()
            pe.matmul(t[0:NS, 0, 0:NG * NQ], rep[:, :, :], ws_t[:, :, 0:NQ], start=True, stop=True)\
                .then_inc(turned, 1)
            for half in range(2):
                t = take_acc()
                pe.matmul(t[:, 0, :], ones[:, :], ws_t[:, half * 4:half * 4 + 4, :], start=True, stop=True)\
                    .then_inc(turned, 1)
            pe.wait_ge(acc_read, accs.now())
            t = take_acc()
            pe.matmul(t[:, 0, 0:NG * NS], ones[0:NS, :], ws_ts[:, :, :, :], start=True, stop=True)\
                .then_inc(turned, 1)

            ytile = Count()

            def turn_p(layer):
                pe.wait_ge(p_in, 16 * TT * (layer + 1))
                for kt in range(PKT):
                    t = take_acc()
                    for c in range(QB):
                        pe.transpose(t[:, 0, c * P:(c + 1) * P], p_nat[:, c, kt * P:(kt + 1) * P], ident[:, :])
                    pe.transpose(t[:, 1, 0:NS], p_nat[0:NS, QB, kt * P:(kt + 1) * P], ident[0:NS, 0:NS])\
                        .then_inc(turned, 1)

            def spatial(k, g):
                ytile.step()
                pe.wait_ge(vh_made, ytile.now())
                gs = bass.ds(g, 1)
                for c in range(QB):
                    pe.matmul(zb[k][:, c * P:(c + 1) * P], vhat[:, k, c, :], ws_t[:, gs, :].rearrange("p a t -> p (a t)"),
                              start=True, stop=True)
                pe.matmul(ob[k][:, 0:NS], vhat[0:NS, k, QB, :],
                          ws_ts[:, gs, :, :].rearrange("p a b q -> p (a b q)"), start=True, stop=True)\
                    .then_inc(mixed, 1)

            for hf in range(HALF):
                with repeat(pe, N_UG // SLOTS, (panel, SLOTS), (accs, 4), (ytile, 2)) as i:
                    for k in range(2):
                        gemm(0)
                        spatial(k, i + hf * (NG // 2))
                        gemm(0)
                if hf == HALF - 1:
                    turn_p(0)
                with repeat(pe, KT // SLOTS, (panel, SLOTS), (accs, SLOTS)):
                    for k in range(SLOTS):
                        gemm(1, KT * (1 + hf) if k == 0 else None)

            def embed(layer, a):
                for n in range(KT):
                    if n > 0:
                        gemm(a)
                    else:
                        gemm(a, KT * (3 + layer * 2), KT - 1)
                        pe.wait_ge(wp_lo_made, layer + 1)
                    t = take_acc()
                    cs = slice(n * P, (n + 1) * P)
                    for kt in range(PKT):
                        for wt, xt in ((wp_hi, p_hi), (wp_hi, p_lo), (wp_lo, p_hi)):
                            for c in range(2):
                                mm = pe.matmul(t[:, c, 0:TH], wt[:, kt, cs], xt[:, kt, c * TH:(c + 1) * TH],
                                               start=kt == 0 and wt is wp_hi and xt is p_hi,
                                               stop=kt == PKT - 1 and wt is wp_lo)
                    mm.then_inc(turned, 1)

            embed(0, 0)

            wblk, opair = Count(), Count()

            def logits(n, par):
                e, kb = n // QB, QB - 1 - n % QB
                w = (QB - kb) * P
                if not (blk.reg is None and blk.now() < 2):
                    pe.wait_ge(exp_done, blk.now(-1))
                r = slice(e * DH, (e + 1) * DH)
                pe.matmul(zb[n % 2][:, 0:w], kt_t[r, par, kb * P:(kb + 1) * P], qt_t[r, par, kb * P:TP],
                          start=True, stop=False, skip_group_check=True)
                pe.matmul(zb[n % 2][:, 0:P], ident_b[:, :], unseen[:, :], start=False, stop=False,
                          skip_group_check=True).then_inc(z_full, 1)
                blk.step()

            def after(n):
                e, kb = n // QB, QB - 1 - n % QB
                w = (QB - kb) * P
                wblk.step()
                pe.wait_ge(soft_split, wblk.now())
                for soft in (soft_hi, soft_lo):
                    for later in range(QB - 1, kb, -1):
                        lw = (QB - later) * P
                        pe.matmul(zb[n % 2][:, w - lw:w], negones_r[:, :],
                                  soft[:, e, soft_at(later):soft_at(later) + lw], start=False, stop=False,
                                  skip_group_check=True)
                    mm = pe.matmul(zb[n % 2][:, 0:w], negtri_r[:, :], soft[:, e, soft_at(kb):soft_at(kb) + w],
                                   start=False, stop=soft is soft_lo, skip_group_check=True)
                mm.then_inc(after_done, 1)

            def values(n, par):
                e, kb = n // QB, QB - 1 - n % QB
                w = (QB - kb) * P
                pe.wait_ge(exp_done, wblk.now())
                if n == 0:
                    opair.step()
                    pe.wait_ge(o_read, opair.now())
                r = slice(e * DH, (e + 1) * DH)
                mm = pe.matmul(ob[par][r, kb * P:TP], vb_nat[:, par, kb, r], wts[:, n % 2, 0:w],
                               start=kb == QB - 1, stop=kb == 0, skip_group_check=True)
                if n == 2 * QB - 1:
                    mm.then_inc(o_full, 1)

            def pair_step(par, dense, att, prev, first=False):
                for n in range(2 * QB):
                    if att:
                        logits(n, 1 - par)
                    if att and (n > 0 or prev):
                        after((n - 1) % (2 * QB))
                    if dense:
                        s = panel.slot(SLOTS)
                        if n % 2 == 0:
                            pe.wait_ge(lo_made, panel.now(1))
                            t = take_acc()
                        half = range(KT // 2) if n % 2 == 0 else range(KT // 2, KT)
                        mm = products(t, s, act_hi[1], act_lo[1], half, n % 2 == 0, n % 2 == 1,
                                      KT * 4 if first and n < 2 else None, KT - 1 if first and n == 1 else None)
                        if n % 2 == 1:
                            mm.then_inc(panel_done, 1)
                            panel.step()
                    if att and (n > 0 or prev):
                        values((n - 1) % (2 * QB), 1 - par if n > 0 else par)
                    if dense and n == 3:
                        turn_tokens(kt_t[:, par, :])
                    if dense and n == 5:
                        turn_tokens(vt_t[:, :])
                if att and not dense:
                    after(2 * QB - 1)
                    values(2 * QB - 1, 1 - par)

            pair_step(0, True, False, False, True)
            pair_step(1, True, True, False)
            with repeat(pe, NP // 2 - 1, (panel, 8), (accs, 12), (blk, 4 * QB), (wblk, 4 * QB), (opair, 2)):
                pair_step(0, True, True, True)
                pair_step(1, True, True, True)
            pe.wait_ge(acc_read, accs.now(2 - 1))
            pair_step(0, False, True, True)

            kseq, lseq, seq, oseq = Count(), Count(), Count(), Count()

            def keys():
                pe.wait_ge(k_in, kseq.now() * (16 * PAGES) + 16 * PAGES)
                kseq.step()
                for two in range(KT // 2):
                    t = take_acc()
                    for m in range(2):
                        for g in range(PAGES):
                            mm = pe.transpose(t[:, m, g * P:(g + 1) * P],
                                              kpage[:, g, (2 * two + m) * P:(2 * two + m + 1) * P], ident[:, :])
                    mm.then_inc(turned, 1)

            def logits_s():
                pe.wait_ge(acc_read, accs.now(2))
                pe.wait_ge(qz_set, lseq.now(1) * 4)
                lseq.step()
                for hp in range(NP):
                    cs = slice(hp * HQ, (hp + 1) * HQ)
                    for wt, xt in ((qz_hi, kp_hi), (qz_hi, kp_lo), (qz_lo, kp_hi)):
                        mm = pe.matmul(ob[0][0:HQ, :], wt[:, cs], xt[:, hp, :],
                                       start=hp == 0 and wt is qz_hi and xt is kp_hi, stop=hp == NP - 1 and wt is qz_lo)
                mm.then_inc(zrow_full, 1)

            def turn_logits(par):
                pe.wait_ge(zrow_read, lseq.now())
                for g in range(PAGES):
                    mm = pe.matmul(zb[par][:, g * HQ:(g + 1) * HQ], z_row[:, g * P:(g + 1) * P], ident[0:HQ, 0:HQ],
                                   start=g == 0, stop=False, skip_group_check=True)
                mm.then_inc(zs_full, 1)

            def after_s(par):
                pe.wait_ge(softs_done, seq.now(2))
                z = zb[par][:, 0:PAGES * HQ]
                zv = z.rearrange("p (g n) -> p g n", g=PAGES)
                bs = bass.ds(seq.now(), 1) if seq.reg is not None else slice(seq.now(), seq.now() + 1)
                sn = sp_n[:, :, :].rearrange("p h (b q) -> p b h q", q=NQ)[:, bs, :, :]
                for g in range(PAGES):
                    pe.matmul(zv[:, g, :], negones[0:NS, :], sn, start=False, stop=False, skip_group_check=True)
                for n in range(1, PAGES):
                    pe.matmul(z[:, 0:(PAGES - n) * HQ], negones[:, :],
                              sp_b[:, n:, :].rearrange("p g n -> p (g n)"), start=False, stop=False,
                              skip_group_check=True)
                pe.matmul(z, negtri[:, :], sp_b[:, :, :].rearrange("p g n -> p (g n)"), start=False, stop=True,
                          skip_group_check=True).then_inc(afters_done, 1)

            def values_s(par):
                pe.wait_ge(exps_done, seq.now(2))
                pe.wait_ge(v_in[par], seq.lap(2) * (16 * PAGES) + 16 * PAGES)
                seq.step()
                t = take_acc()
                for c in range(2):
                    for g in range(PAGES):
                        mm = pe.matmul(t[0:HQ, c, :], ws_b[:, g, :], vpage[par][:, g, c * 512:(c + 1) * 512],
                                       start=g == 0, stop=g == PAGES - 1)
                mm.then_inc(turned, 1)

            def turn_outputs():
                pe.wait_ge(os_read, oseq.now(1))
                oseq.step()
                for hp in range(NP):
                    mm = pe.matmul(ob[1][:, hp * 2 * NQ:(hp + 1) * 2 * NQ], o_row[:, hp * P:(hp + 1) * P],
                                   ident[0:HQ, hp * 2 * NQ:(hp + 1) * 2 * NQ], start=hp == 0, stop=hp == NP - 1,
                                   skip_group_check=True)
                mm.then_inc(os_full, 1)

            def step_s(par, outputs=True):
                keys()
                if outputs:
                    turn_outputs()
                after_s(par)
                logits_s()
                values_s(par)
                turn_logits(1 - par)

            keys()
            pe.wait_ge(qbd_set, 3)
            for hp in range(NP):
                mm = pe.matmul(zb[0][0:NS, hp * 2 * NS:(hp + 1) * 2 * NS], kts[:, hp, :],
                               qbd[:, hp, :, :], start=hp == 0, stop=False, skip_group_check=True)
            pe.matmul(zb[0][0:NS, :], ident_b[0:NS, 0:NS], unseen_n[:, :, :, :], start=False, stop=False,
                      skip_group_check=True).then_inc(zs_full, 1)
            pe.wait_ge(softs_done, 1)
            pe.matmul(zb[0][0:NS, :], negtri[0:NS, 0:NS], sp_n[:, :, :], start=False, stop=True,
                      skip_group_check=True).then_inc(afters_done, 1)
            pe.wait_ge(o_lo, NP)
            logits_s()
            pe.wait_ge(exps_done, 1)
            for hp in range(NP):
                mm = pe.matmul(ob[1][:, hp * 2 * NS:(hp + 1) * 2 * NS], vs_nat[:, hp * P:(hp + 1) * P],
                               ws_n[:, 2 * hp:2 * hp + 2, :], start=hp == 0, stop=hp == NP - 1,
                               skip_group_check=True)
            mm.then_inc(os_full, 1)
            turn_logits(0)
            step_s(0, False)
            with repeat(pe, NB // 2 - 1, (accs, 2 * TURNS_B), (kseq, 2), (lseq, 2), (seq, 2), (oseq, 2)):
                step_s(1)
                step_s(0)
            after_s(1)
            pe.wait_ge(acc_read, accs.now(2))
            turn_outputs()
            values_s(1)
            pe.wait_ge(acc_read, accs.now(2))
            turn_outputs()

            turn_p(1)
            pe.wait_ge(o_lo, NP + 1)
            with repeat(pe, KT // SLOTS, (panel, SLOTS), (accs, SLOTS)):
                for k in range(SLOTS):
                    gemm(0)
            embed(1, 1)
            pe.wait_ge(y_scaled, KT)
            for tt in range(TT):
                n = P if tt < QB else NS
                if tt == 2:
                    pe.wait_ge(squared, (sums.now() + 1) * KT)
                    for c in range(TT):
                        m = P if c < QB else NS
                        mm = pe.matmul(zb[0][0:m, c:c + 1], sumsq[:, c * P:c * P + m], ones[:, 0:1], start=c == 0,
                                       stop=c == TT - 1, skip_group_check=True)
                    mm.then_inc(ssq_out, 1)
                t = take_acc()
                for kt in range(KT):
                    mm = pe.transpose(t[0:n, kt // 4, (kt % 4) * P:(kt % 4 + 1) * P],
                                      y_t[:, kt, tt * P:tt * P + n], ident[:, :])
                mm.then_inc(turned, 1)
            assert panel.now() == END

        @block.vector
        def _(dve):
            panel, done, accs, turns, own, xt = Count(), Count(), Count(), Count(), Count(), Count()

            def split_next():
                if panel.reg is None and panel.now() >= END:
                    return
                s = panel.slot(SLOTS)
                dve.wait_ge(hi_made, panel.now(1))
                dve.tensor_tensor(w_lo[:, s, :, :], raw[:, s, :, :], w_hi[:, s, :, :].bitcast(F32), ALU.subtract)\
                    .then_inc(lo_made, 1)
                panel.step()

            def product():
                done.step()
                dve.wait_ge(panel_done, done.now(SLOTS))
                t = acc[accs.slot(2)]
                accs.step()
                return t

            def turn():
                turns.step()
                dve.wait_ge(turned, turns.now())
                t = acc[accs.slot(2)]
                accs.step()
                return t

            def lo_x(n, into, src=None):
                xt.step()
                dve.wait_ge(x_hi, xt.now())
                one = lambda x: x[:, sl(n), :].rearrange("p a t -> p (a t)")
                dve.tensor_tensor(one(act_lo[into]), one(h) if src is None else src[:, :],
                                  one(act_hi[into]).bitcast(F32), ALU.subtract).then_inc(x_lo, 1)

            def add_product(n):
                t = product()
                hn = halves(h[:, sl(n), :].rearrange("p a t -> p (a t)"))
                dve.tensor_tensor(hn, both(t), hn, ALU.add).then_inc(acc_read, 1)

            def self_wait(ins):
                ins.then_inc(vec, 1)
                own.step()
                dve.wait_ge(vec, own.now())

            norms = Count()

            def inverse_root(r, m, scratch):
                self_wait(dve.reciprocal(r, r))
                newton(r, m, scratch)

            def newton(r, m, scratch):
                self_wait(dve.tensor_tensor(scratch, r, r, ALU.mult))
                self_wait(dve.scalar_tensor_tensor(scratch, scratch, -0.5, m, ALU.mult, ALU.mult))
                self_wait(dve.scalar_tensor_tensor(r, scratch, 1.5, r, ALU.add, ALU.mult))

            def rms():
                norms.step()
                dve.wait_ge(logged, norms.now())
                for c in range(2):
                    dve.tensor_scalar(ms[:, c * TH:(c + 1) * TH], zb[c][:, 0:TH], 1.0 / D, EPS, ALU.mult, ALU.add)
                roots.step()
                dve.wait_ge(rooted, roots.now())
                newton(rinv[:, :], ms[:, :], sumsq[:, :])

            roots = Count()

            t = turn()
            dve.tensor_copy(cols[:, :], t[:, 0, 0:N_COL]).then_inc(acc_read, 1)
            for n in range(KT):
                t = turn()
                dve.tensor_copy(h[:, n, TP:T], t[:, 1, 0:NS])
                dve.tensor_copy(h[:, n, 0:TP], t[:, 0, 0:TP]).then_inc(acc_read, 1)
                if n > 0:
                    lo_x(n - 1, 0)
                if n > KT - AHEAD:
                    split_next()
            lo_x(KT - 1, 0)
            split_next()
            for half in range(2):
                t = turn()
                dve.tensor_copy(ws_t[:, half * (NG // 2):(half + 1) * (NG // 2), :], t[:, 0, :]).then_inc(acc_read, 1)
            rms()

            with repeat(dve, N_AV // SLOTS, (panel, SLOTS), (done, SLOTS), (accs, 2 * SLOTS), (turns, SLOTS)) as i:
                for k in range(SLOTS + 1):
                    if k < SLOTS:
                        split_next()
                        t = product()
                        dve.tensor_tensor(halves(vt[:, k % 2, :]), both(t), halves(rinv[:, :]), ALU.mult)\
                            .then_inc(acc_read, 1)
                    if k > 0:
                        t = turn()
                        cs = bass.ds(i * (SLOTS * P) + (k - 1) * P, P)
                        dve.tensor_copy(v_nat[0:NS, QB, cs], t[0:NS, 1, 0:P])
                        dve.tensor_copy(v_nat[:, 0:QB, cs], t[:, 0, :].rearrange("p (c n) -> p c n", n=P))\
                            .then_inc(acc_read, 1)
                dve.wait_ge(acc_read, accs.now(2))
                for tt in range(TT):
                    n = P if tt < QB else NS
                    ins = dve.bn_stats(bst[0:n, tt, bass.ds(i, 1), :].rearrange("p a s -> p (a s)"),
                                       v_nat[0:n, tt, bass.ds(i * (SLOTS * P), SLOTS * P)])
                ins.then_inc(stats_done, 1)
            dve.wait_ge(stats_done, N_AV // SLOTS)
            for tt in range(TT):
                n = P if tt < QB else NS
                ins = dve.bn_aggr(mv[0:n, tt, :], bst[0:n, tt, :, :].rearrange("p a s -> p (a s)"))
            self_wait(ins)
            dve.tensor_scalar(ln_s[:, 0, :], mv[:, :, 1], EPS, None, ALU.add).then_inc(normed, 1)
            roots.step()
            dve.wait_ge(rooted, roots.now())
            inverse_root(ln_s[:, 1, :], ln_s[:, 0, :], ln_s[:, 2, :])
            dve.tensor_copy(ln_s[:, 2, :], ln_s[:, 1, :])
            dve.scalar_tensor_tensor(ln_s[:, 3, :], mv[:, :, 0], -1.0, ln_s[:, 1, :], ALU.mult, ALU.mult)\
                .then_inc(normed, 1)
            t = turn()
            dve.tensor_tensor(ws_ts[:, :, :, :],
                              t[0:NS, 0, 0:NG * NQ].rearrange("p (g q) -> p g q", q=NQ)[:, :, None, :]
                              .to_broadcast([NS, NG, NB, NQ]),
                              blockdiag[:, None, :, :].to_broadcast([NS, NG, NB, NQ]), ALU.mult)\
                .then_inc(acc_read, 1)
            for half in range(2):
                t = turn()
                dve.tensor_copy(row_sum[:, half * 4:half * 4 + 4, 0:P], t[:, 0, :].rearrange("p (g t) -> p g t", t=P))\
                    .then_inc(acc_read, 1)
            t = turn()
            dve.tensor_copy(row_sum[:, :, P:P + NS], t[:, 0, 0:NG * NS].rearrange("p (g t) -> p g t", t=NS))\
                .then_inc(acc_read, 1)
            dve.wait_ge(acc_read, accs.now(2))
            dve.wait_ge(bs_ready, 1)

            def split_p(layer):
                for kt in range(PKT):
                    t = turn()
                    dve.tensor_copy(p_t[:, kt, TP:T], t[:, 1, 0:NS])
                    dve.tensor_copy(p_t[:, kt, 0:TP], t[:, 0, 0:TP]).then_inc(acc_read, 1)
                dve.wait_ge(acc_read, accs.now(2))
                for kt in range(PKT):
                    dve.wait_ge(p_hi_made, layer * PKT + kt + 1)
                    dve.tensor_tensor(p_lo[:, kt, :], p_t[:, kt, :], p_hi[:, kt, :].bitcast(F32), ALU.subtract)
                dve.wait_ge(wp_hi_made, layer + 1)
                dve.tensor_tensor(wp_lo[:, :, :], wp_raw[:, :, :], wp_hi[:, :, :].bitcast(F32), ALU.subtract)\
                    .then_inc(wp_lo_made, 1)

            ytile = Count()
            for hf in range(HALF):
                with repeat(dve, N_UG // SLOTS, (panel, SLOTS), (done, SLOTS), (accs, SLOTS), (ytile, 2), (xt, 2),
                            (own, 2)) as i:
                    for k in range(2):
                        j = i * 2 + (hf * KT + k)
                        split_next()
                        t = product()
                        dve.tensor_tensor(halves(u_r[:, :]), both(t), halves(rinv[:, :]), ALU.mult)\
                            .then_inc(acc_read, 1)
                        gs = bass.ds(i + hf * (NG // 2), 1)
                        self_wait(dve.scalar_tensor_tensor(
                            bs_ln[:, :], row_sum[:, gs, :].rearrange("p a t -> p (a t)"), ln_b_c[:, bass.ds(j, 1)],
                            bs_bc[:, gs, :].rearrange("p a t -> p (a t)"), ALU.mult, ALU.add))
                        ytile.step()
                        dve.wait_ge(mixed, ytile.now())
                        dve.scalar_tensor_tensor(s_t[:, TP:T], ob[k][:, 0:NS], ln_g_c[:, bass.ds(j, 1)],
                                                 bs_ln[:, P:P + NS], ALU.mult, ALU.add)
                        dve.scalar_tensor_tensor(
                            s_t[:, 0:TP].rearrange("p (c t) -> p c t", t=P),
                            zb[k][:, :].rearrange("p (c t) -> p c t", t=P), ln_g_c[:, bass.ds(j, 1)],
                            bs_ln[:, None, 0:P].to_broadcast([P, QB, P]), ALU.mult, ALU.add).then_inc(s_ready, 1)
                        split_next()
                        t = product()
                        dve.tensor_tensor(halves(g_r[:, :]), both(t), halves(rinv[:, :]), ALU.mult)\
                            .then_inc(acc_read, 1)
                        lo_x(i * 2 + k, 1, s_t)
                if hf == HALF - 1:
                    split_p(0)
                if hf < HALF - 1:
                    with repeat(dve, KT // SLOTS, (panel, SLOTS), (done, SLOTS), (accs, SLOTS)) as i:
                        for k in range(SLOTS):
                            split_next()
                            add_product(i * SLOTS + k)
                else:
                    with repeat(dve, KT // SLOTS, (panel, SLOTS), (done, SLOTS), (accs, SLOTS), (xt, SLOTS)) as i:
                        for k in range(SLOTS):
                            split_next()
                            add_product(i * SLOTS + k)
                            lo_x(i * SLOTS + k, 0)

            def embed(layer):
                for n in range(KT):
                    if n == 0:
                        rms()
                    split_next()
                    g = gate[:, n % 2, :]
                    t = product()
                    dve.tensor_tensor(halves(g), both(t), halves(rinv[:, :]), ALU.mult).then_inc(acc_read, 1)
                    if n > 0 and layer == 0:
                        lo_x(n - 1, 1)
                    t = turn()
                    dve.wait_ge(gate_sig, layer * KT + n + 1)
                    dve.tensor_tensor(halves(g), both(t), halves(g), ALU.mult).then_inc(acc_read, 1)
                    dve.wait_ge(acc_read, accs.now(2))
                    dve.tensor_tensor(h[:, n, :], h[:, n, :], g, ALU.add).then_inc(h_new, 1)
                if layer == 0:
                    lo_x(KT - 1, 1)

            embed(0)
            rms()

            blk, opair, pair = Count(), Count(), Count()

            def relu_z(n, a):
                e, kb = n // QB, QB - 1 - n % QB
                w = (QB - kb) * P
                dve.wait_ge(act_step, blk.now(1) * 2 - 1)
                dve.tensor_scalar(relz[:, n % 2, 0:w], zb[n % 2][:, 0:w], bias_of(a, e), 0.0, ALU.add, ALU.max)\
                    .then_inc(rel_done, 1)

            def softplus(n):
                e, kb = n // QB, QB - 1 - n % QB
                w = (QB - kb) * P
                blk.step()
                dve.wait_ge(rel_done, blk.now())
                dve.wait_ge(log_done, blk.now())
                a = soft_at(kb)
                r, z = relz[:, n % 2, 0:w], absz[:, n % 2, 0:w]
                dve.tensor_tensor(soft_hi[:, e, a:a + w], r, z, ALU.add).then_inc(soft_done, 1)
                dve.tensor_tensor(r, r, z, ALU.add).then_inc(soft_done, 1)
                dve.wait_ge(soft_done, blk.now() * 2)
                dve.tensor_tensor(soft_lo[:, e, a:a + w], r, soft_hi[:, e, a:a + w].bitcast(F32), ALU.subtract)\
                    .then_inc(soft_split, 1)

            def out_pair(a, par):
                opair.step()
                dve.wait_ge(o_full, opair.now())
                dve.wait_ge(sg_ready, opair.now())
                dve.tensor_tensor(o_s[:, :], ob[par][:, :], silu_g[:, par, :], ALU.mult).then_inc(o_read, 1)
                dve.wait_ge(o_read, opair.now(2))
                dve.wait_ge(o_hi, opair.now())
                one = lambda x: x[:, sl(a), 0:TP].rearrange("p a t -> p (a t)")
                dve.tensor_tensor(one(act_lo[0]), o_s[:, :], one(act_hi[0]).bitcast(F32), ALU.subtract)\
                    .then_inc(o_lo, 1)

            def turned_pair(dst, dst_s, i, par):
                t = turn()
                cs = slice(i * P, (i + 1) * P) if isinstance(i, int) else bass.ds(i * P, P)
                dve.tensor_copy(dst_s[:, cs], t[0:NS, 1, 0:P])
                dve.tensor_copy(dst[:, par, :, :], t[:, 0, :].rearrange("p (c n) -> p c n", n=P))\
                    .then_inc(acc_read, 1)

            def pair_step(i, par, dense, att, prev, stored):
                for n in range(2 * QB):
                    if att:
                        relu_z(n, i - 1)
                    if dense and n % 2 == 1:
                        split_next()
                    if dense and n == 4:
                        if stored is not None:
                            dve.wait_ge(kv_out[par], stored)
                        turned_pair(k_nat, ks_nat, i, par)
                    if dense and n == 6:
                        turned_pair(vb_nat, vs_nat, i, par)
                    if att:
                        softplus(n)
                    if n == 2 and prev:
                        out_pair(i - 2, par)
                    if dense and n == 1:
                        t = product()
                        dve.tensor_tensor(kts[:, sl(i), :].rearrange("p a t -> p (a t)"), t[:, 1, TH - NS:TH],
                                          rinv[:, TP:T], ALU.mult)
                        dve.tensor_tensor(halves(kt_t[:, par, :]), both(t), halves(rinv[:, :]), ALU.mult)\
                            .then_inc(acc_read, 1)
                    if dense and n == 3:
                        t = product()
                        dve.tensor_tensor(halves(vt_t[:, :]), both(t), halves(rinv[:, :]), ALU.mult)\
                            .then_inc(acc_read, 1)
                    if dense and n == 5:
                        t = product()
                        dve.scalar_tensor_tensor(qts[:, sl(i), :].rearrange("p a t -> p (a t)"), t[:, 1, TH - NS:TH],
                                                 SCALE, rinv[:, TP:T], ALU.mult, ALU.mult)
                        dve.scalar_tensor_tensor(halves(qt_t[:, par, :]), both(t), SCALE, halves(rinv[:, :]),
                                                 ALU.mult, ALU.mult).then_inc(acc_read, 1)
                    if dense and n == 7:
                        t = product()
                        if att:
                            dve.wait_ge(sg_ready, i if isinstance(i, int) else i)
                        dve.tensor_tensor(halves(gb_r[:, :]), both(t), halves(rinv[:, :]), ALU.mult)\
                            .then_inc(acc_read, 1)
                if att and not dense:
                    out_pair(i - 1, 1 - par)

            pair_step(0, 0, True, False, False, None)
            pair_step(1, 1, True, True, False, None)
            with repeat(dve, NP // 2 - 1, (panel, 8), (done, 8), (accs, 12), (turns, 4), (blk, 4 * QB),
                        (opair, 2)) as m:
                pair_step(m * 2 + 2, 0, True, True, True, m * 32 + 32)
                pair_step(m * 2 + 3, 1, True, True, True, m * 32 + 32)
            dve.wait_ge(q_split, 1)
            dve.tensor_tensor(qts_lo[:, :, :], qts[:, :, :], qts_hi[:, :, :].bitcast(F32), ALU.subtract)\
                .then_inc(q_split, 1)
            pair_step(NP, 0, False, True, True, None)

            samp, kseq = Count(), Count()

            def split_keys():
                for two in range(KT // 2):
                    kseq.step()
                    dve.wait_ge(kp_hi_made, kseq.now())
                    t = turn()
                    dve.tensor_tensor(kp_lo[:, 2 * two:2 * two + 2, :], t[:, :, :],
                                      kp_hi[:, 2 * two:2 * two + 2, :].bitcast(F32), ALU.subtract)\
                        .then_inc(acc_read, 1)

            def logits_out():
                zrow.step()
                dve.wait_ge(zrow_full, zrow.now())
                dve.tensor_scalar(z_row[:, :], ob[0][0:HQ, :], bias_row[:, 0:1], None, ALU.add).then_inc(zrow_read, 1)

            def outputs(b):
                outs.step()
                dve.wait_ge(os_full, outs.now())
                bq = bass.ds(b * NQ, NQ) if not isinstance(b, int) else slice(b * NQ, (b + 1) * NQ)
                for e in range(2):
                    r = slice(e * DH, (e + 1) * DH)
                    ov = ob[1][r, 0:HQ].rearrange("p (a e q) -> p a e q", e=2, q=NQ)[:, :, e, :]
                    ins = dve.tensor_tensor(os_s[r, :, bq], ov, on_s[r, :, bq], ALU.add)
                ins.then_inc(os_read, 1)

            def step_s(par, more, before=None):
                samp.step()
                dve.wait_ge(logs_done, samp.now())
                dve.scalar_tensor_tensor(sp_b[:, :, :].rearrange("p g n -> p (g n)"), zb[par][:, 0:PAGES * HQ], 0.0,
                                         sp_b[:, :, :].rearrange("p g n -> p (g n)"), ALU.max, ALU.add)\
                    .then_inc(softs_done, 1)
                if more:
                    split_keys()
                if before is not None:
                    outputs(before)
                if more:
                    logits_out()
                t = turn()
                dve.tensor_copy(o_row[:, :].rearrange("p (c n) -> p c n", c=2), t[0:HQ, :, :]).then_inc(acc_read, 1)

            zrow, outs = Count(), Count()
            z = zb[0][0:NS, :].rearrange("p (h t) -> p h t", t=NS)
            bc = bias[0:NS, :][:, :, None].to_broadcast([NS, NH, NS])
            samp.step()
            dve.wait_ge(kv_out[0], 16 * NP)
            dve.wait_ge(kv_out[1], 16 * NP)
            split_keys()
            dve.wait_ge(zs_full, 1)
            dve.tensor_tensor(xs_n[:, :, :], z, bc, ALU.add).then_inc(xs_done, 1)
            dve.wait_ge(xs_done, 1)
            dve.wait_ge(logs_done, 1)
            dve.scalar_tensor_tensor(sp_n[:, :, :], xs_n[:, :, :], 0.0, as_n[:, :, :], ALU.max, ALU.add)\
                .then_inc(softs_done, 1)
            dve.wait_ge(afters_done, 1)
            dve.tensor_tensor(xs_n[:, :, :], z, bc, ALU.add).then_inc(ds_done, 1)
            dve.wait_ge(bias_in, 16)
            logits_out()
            outs.step()
            dve.wait_ge(os_full, 1)
            for e in range(2):
                r = slice(e * DH, (e + 1) * DH)
                ins = dve.tensor_copy(on_s[r, :, :], ob[1][r, :].rearrange("p (a e n) -> p a e n", e=2, n=NS)[:, :, e, :])
            ins.then_inc(os_read, 1)
            dve.wait_ge(os_read, 1)
            step_s(0, True)
            with repeat(dve, NB // 2 - 1, (turns, 2 * TURNS_B), (accs, 2 * TURNS_B), (samp, 2), (kseq, KT),
                        (zrow, 2), (outs, 2)) as m:
                step_s(1, True, m * 2)
                step_s(0, True, m * 2 + 1)
            step_s(1, False, NB - 2)
            outputs(NB - 1)
            dve.wait_ge(os_read, NB + 1)
            dve.tensor_tensor(os_s[:, :, :], os_s[:, :, :], silu_s[:, :, :], ALU.mult).then_inc(os_sum, 1)
            dve.wait_ge(os_sum, 1)
            dve.wait_ge(o_hi, NP + 1)
            dve.tensor_tensor(act_lo[0][:, :, TP:T], os_s[:, :, :], act_hi[0][:, :, TP:T].bitcast(F32),
                              ALU.subtract).then_inc(o_lo, 1)

            split_p(1)
            with repeat(dve, KT // SLOTS, (panel, SLOTS), (done, SLOTS), (accs, SLOTS), (xt, SLOTS)) as i:
                for k in range(SLOTS):
                    split_next()
                    add_product(i * SLOTS + k)
                    lo_x(i * SLOTS + k, 1)
            embed(1)
            norms.step()
            dve.wait_ge(ssq_out, norms.now())
            dve.tensor_scalar(ln_s[:, 0, 0:QB], zb[0][:, 0:QB], 1.0 / D, EPS, ALU.mult, ALU.add)
            dve.tensor_scalar(ln_s[0:NS, 0, QB:TT], zb[0][0:NS, QB:TT], 1.0 / D, EPS, ALU.mult, ALU.add)\
                .then_inc(mean_sq, 1)
            roots.step()
            dve.wait_ge(rooted, roots.now())
            inverse_root(ln_s[:, 1, :], ln_s[:, 0, :], ln_s[:, 2, :])
            for tt in range(TT):
                n = P if tt < QB else NS
                t = turn()
                dve.tensor_scalar(y_nat[0:n, tt, :].rearrange("p (c n) -> p c n", c=2), t[0:n, :, :],
                                  ln_s[0:n, 1, tt:tt + 1], None, ALU.mult).then_inc(acc_read, 1)
            assert panel.now() == END and accs.now() == ACC_END


_INS = ['x_prompt', 'x_sample', 'cache_k', 'cache_v', 'page_table', 'p_prompt', 'p_sample', 'g_norm', 'w_in_a',
        'ln_v_g', 'ln_v_b', 'w_spatial', 'b_spatial', 'w_out_a', 'g_kv', 'w_kv', 'w_in_b', 'w_out_b', 'b_sb',
        'w_ple', 'g_ple', 'w_ple_gate', 'g_final']


def kernel(**inputs):
    import numpy as _np
    import concourse.bacc as _bacc
    from concourse import mybir as _mybir
    from concourse.bass_utils import run_bass_kernel_spmd as _run

    nc = _bacc.Bacc("TRN2", target_bir_lowering=False, num_devices=1, dynamic_dma_scratch_size=1024)
    arrays, args = {}, []
    for name in _INS:
        a = _np.ascontiguousarray(inputs[name])
        arrays[f"in_{name}_dram"] = a
        args.append(nc.dram_tensor(f"in_{name}_dram", a.shape, _mybir.dt.from_np(a.dtype), kind="ExternalInput").ap())
    xp, xs = inputs['x_prompt'].shape, inputs['x_sample'].shape
    heads = tuple(inputs['cache_k'].shape[2:])
    e_a = inputs['ln_v_g'].shape[1]
    outs = [xp, xs, tuple(xp[:2]) + heads, tuple(xp[:2]) + heads, tuple(xs[:2]) + heads, tuple(xs[:2]) + heads,
            (1,) + tuple(xs[:2]) + (e_a,)]
    for i, shape in enumerate(outs):
        args.append(nc.dram_tensor(f"out_{i}_dram", tuple(shape), _mybir.dt.float32, kind="ExternalOutput").ap())
    build(nc, *args)
    r = _run(nc, [arrays], core_ids=[0])
    return tuple(r.results[0][f"out_{i}_dram"] for i in range(len(outs)))
```

```python
from contextlib import ExitStack, contextmanager

import concourse.bass as bass
from concourse import mybir

F32 = mybir.dt.float32
F32R = mybir.dt.float32r
BF16 = mybir.dt.bfloat16
I32 = mybir.dt.int32
ACT = mybir.ActivationFunctionType
ALU = mybir.AluOpType

P = 128
SLOTS = 4
AHEAD = 3
EPS = 1e-6
FAR = -1e30


class Count:

    def __init__(self, start=0):
        self.before, self.here, self.reg, self.per = start, 0, None, 0

    def now(self, ahead=0):
        n = self.before + self.here + ahead
        return n if self.reg is None else self.reg * self.per + n

    def step(self, n=1):
        self.here += n

    def slot(self, ring, ahead=0):
        assert self.per % ring == 0
        return (self.before + self.here + ahead) % ring

    def lap(self, ring, ahead=0):
        assert self.per % ring == 0
        n = (self.before + self.here + ahead) // ring
        return n if self.reg is None else self.reg * (self.per // ring) + n


@contextmanager
def repeat(eng, turns, *counts):
    with eng.Fori(0, turns) as i:
        for c, per in counts:
            c.before, c.here, c.reg, c.per = c.before + c.here, 0, i, per
        yield i
        for c, per in counts:
            assert c.here == per, (c.here, per)
    for c, per in counts:
        c.before, c.here, c.reg, c.per = c.before + per * turns, 0, None, 0


def build(nc, x_prompt, x_sample, cache_k, cache_v, page_table, p_prompt, p_sample, g_norm, w_in_a, ln_v_g,
          ln_v_b, w_spatial, b_spatial, w_out_a, g_kv, w_kv, w_in_b, w_out_b, b_sb, w_ple, g_ple, w_ple_gate,
          g_final, y_prompt, y_sample, k_prompt, v_prompt, k_sample, v_sample, chunk_v_sample):
    D = g_kv.shape[0]
    TP = x_prompt.shape[1]
    NB, NQ = x_sample.shape[0], x_sample.shape[1]
    NS = NB * NQ
    T = TP + NS
    TH = T // 2
    KT = D // P
    E_A = ln_v_g.shape[1]
    NG = w_spatial.shape[1]
    NH = b_sb.shape[1]
    DH = D // NH
    NP = NH // 2
    QB = TP // P
    TT = QB + 1
    PLE = p_prompt.shape[3]
    PKT = PLE // P
    NPOOL = cache_k.shape[0]
    PAGES = page_table.shape[1]
    HALF = E_A // D
    SCALE = float(DH) ** -0.5
    HQ = NH * NQ
    QZ = HQ + 2 * NQ
    assert TH * 2 == T and TP == QB * P and D == KT * P and E_A == HALF * D and NP == KT
    assert g_norm.shape[0] == 2 and PAGES == QB and SCALE == 0.125 and NG == HALF * 4

    w_in_a_v = w_in_a[0].rearrange("(kt p) n -> p kt n", p=P)
    w_out_a_v = w_out_a[0].rearrange("(hf kt p) n -> hf p kt n", p=P, hf=HALF)
    w_kv_v = w_kv.rearrange("(kt p) n -> p kt n", p=P)
    w_in_b_v = w_in_b[0].rearrange("(kt p) n -> p kt n", p=P)
    w_out_b_v = w_out_b[0].rearrange("(kt p) n -> p kt n", p=P)
    w_gate_v = w_ple_gate.rearrange("l (kt p) n -> l p kt n", p=P)
    w_ple_v = w_ple.rearrange("l (kt p) n -> l p kt n", p=P)
    xp_v = x_prompt[0].rearrange("(t p) d -> p t d", p=P)
    xs_v = x_sample.rearrange("b q d -> (b q) d")
    kp_v = k_prompt[0].rearrange("(t p) h d -> p t (h d)", p=P)
    vp_v = v_prompt[0].rearrange("(t p) h d -> p t (h d)", p=P)
    yp_v = y_prompt[0].rearrange("(t p) d -> p t d", p=P)
    ck_v = cache_k.rearrange("g t h d -> g t (h d)")
    cv_v = cache_v.rearrange("g t h d -> g t (h d)")

    N_AV = E_A // P
    N_UG = 2 * KT
    N_PL = KT
    END_AV = N_AV
    END_A = N_AV + HALF * (N_UG + KT)
    END_PL0 = END_A + N_PL
    END_B = END_PL0 + 4 * NP
    END_BO = END_B + KT
    END = END_BO + N_PL

    with ExitStack() as ctx:
        def sem(name):
            return ctx.enter_context(nc.semaphore(name))

        top = [nc.sbuf_base + (-nc.sbuf_base) % 32]

        def size(shape):
            n = 4
            for s in shape[1:]:
                n *= s
            return n + (-n) % 32

        def place(name, shape, dt=F32, at=None):
            where = top[0] if at is None else at[0]
            t = nc.alloc_sbuf_tensor_at(name, shape, dt, offset=where)
            if at is None:
                top[0] += size(shape)
            else:
                at[0] += size(shape)
            return t

        ident = place("ident", [P, P])
        ones = place("ones", [P, P])
        negtri = place("negtri", [P, P])
        negones = place("negones", [P, P])
        negtri_r = place("negtri_r", [P, P], F32R)
        negones_r = place("negones_r", [P, P], F32R)
        rep = place("rep", [P, NB, NQ])
        blockdiag = place("blockdiag", [NS, NB, NQ])
        ident_b = place("ident_b", [P, P], BF16)
        unseen = place("unseen", [P, P], BF16)
        unseen_n = place("unseen_n", [NS, NH, NB, NQ], BF16)
        N_COL = 2 * KT + KT + 2 * KT + KT + 2 * (E_A // P)
        cols = place("cols", [P, N_COL])
        bias = place("bias", [P, NH])
        eps = place("eps", [P, 1])
        bias_row = place("bias_row", [HQ, 1])
        pages = place("pages", [1, NB * PAGES], I32)
        bst = place("bst", [P, TT, N_AV // 4, 6])
        mv = place("mv", [P, TT, 2])
        ln_s = place("ln_s", [P, 4, TT])
        c0 = [0]

        def col(n):
            a = c0[0]
            c0[0] += n
            return cols[:, a:a + n]

        g_norm_c = [col(KT), col(KT)]
        g_kv_c = col(KT)
        g_ple_c = [col(KT), col(KT)]
        g_final_c = col(KT)
        ln_g_c = col(E_A // P)
        ln_b_c = col(E_A // P)

        h = place("h", [P, KT, T])
        ms = place("ms", [P, T])
        rinv = place("rinv", [P, T])
        at = [top[0]]
        sumsq = place("sumsq", [P, T])
        ws_hi = place("ws_hi", [P, PAGES, NH * NQ], F32R, at)
        ws_lo = place("ws_lo", [P, PAGES, NH * NQ], F32R, at)
        assert at[0] <= top[0]
        at = [top[0]]
        raw = place("raw", [P, SLOTS, KT, P])
        vp_lo = place("vp_lo", [P, PAGES, D], F32R, at)
        assert at[0] <= top[0]
        w_hi = place("w_hi", [P, SLOTS, KT, P], F32R)
        w_lo = place("w_lo", [P, SLOTS, KT, P], F32R)
        at_x0, at_x1 = [top[0]], [top[0] + 2 * size([P, KT, T])]
        top[0] += 4 * size([P, KT, T])
        x1_base = at_x1[0]
        x0_base = at_x0[0]
        act_hi = [place("act_hi0", [P, KT, T], F32R, at_x0), None]
        act_lo = [place("act_lo0", [P, KT, T], F32R, at_x0), None]
        act_hi[1] = place("act_hi1", [P, KT, T], F32R, at_x1)
        act_lo[1] = place("act_lo1", [P, KT, T], F32R, at_x1)
        at = [x1_base]
        vt = place("vt", [P, 2, T], F32, at)
        ws_nat = place("ws_nat", [P, NG, P], F32, at)
        params = place("params", [N_COL, P], F32, at)
        lng_bc = place("lng_bc", [NS, E_A], F32, at)
        lnb_bc = place("lnb_bc", [NS, E_A], F32, at)
        assert at[0] <= at_x1[0]

        area = top[0]
        at = [area]
        v_nat = place("v_nat", [P, TT, E_A], F32, at)
        vhat = place("vhat", [P, 2, TT, P], F32, at)
        ws_t = place("ws_t", [P, NG, P], F32, at)
        ws_ts = place("ws_ts", [NS, NG, NB, NQ], F32, at)
        row_sum = place("row_sum", [P, NG, P + NS], F32, at)
        bs_bc = place("bs_bc", [P, NG, P + NS], F32, at)
        bs_ln = place("bs_ln", [P, P + NS], F32, at)
        u_r = place("u_r", [P, T], F32, at)
        g_r = place("g_r", [P, T], F32, at)
        assert at[0] - size([P, T]) > area + size([P, TT, E_A])
        s_t = place("s_t", [P, T], F32, at)
        v_out = place("v_out", [NS, E_A], F32, at)
        ends = [at[0]]
        at = [area]
        x_nat = place("x_nat", [P, TT, D], F32, at)
        sq_x = place("sq_x", [P, KT, T], F32, at)
        assert at[0] <= area + size([P, TT, E_A])
        at = [area]
        p_nat = place("p_nat", [P, TT, PLE], F32, at)
        wp_raw = place("wp_raw", [P, PKT, D], F32, at)
        p_t = place("p_t", [P, PKT, T], F32, at)
        p_hi = place("p_hi", [P, PKT, T], F32R, at)
        p_lo = place("p_lo", [P, PKT, T], F32R, at)
        wp_hi = place("wp_hi", [P, PKT, D], F32R, at)
        wp_lo = place("wp_lo", [P, PKT, D], F32R, at)
        gate = place("gate", [P, 2, T], F32, at)
        sq_a = place("sq_a", [P, T], F32, at)
        ends.append(at[0])
        at = [area]
        kt_t = place("kt_t", [P, 2, T], F32, at)
        qt_t = place("qt_t", [P, 2, T], F32, at)
        vt_t = place("vt_t", [P, T], F32, at)
        k_nat = place("k_nat", [P, 2, QB, P], F32, at)
        vb_nat = place("vb_nat", [P, 2, QB, P], F32, at)
        gb_r = place("gb_r", [P, T], F32, at)
        silu_g = place("silu_g", [P, 2, TP], F32, at)
        soft_hi = place("soft_hi", [P, 2, QB * (QB + 1) // 2 * P], F32R, at)
        soft_lo = place("soft_lo", [P, 2, QB * (QB + 1) // 2 * P], F32R, at)
        absz = place("absz", [P, 2, TP], F32, at)
        relz = place("relz", [P, 2, TP], F32, at)
        wts = place("wts", [P, 2, TP], F32, at)
        o_s = place("o_s", [P, TP], F32, at)
        ats = [area]
        kp_hi = place("kp_hi", [P, KT, PAGES * P], F32R, ats)
        kp_lo = place("kp_lo", [P, KT, PAGES * P], F32R, ats)
        vp_hi = place("vp_hi", [P, PAGES, D], F32R, ats)
        at_s = [max(at[0], ats[0] + size([NS, NH, NS]) + 2 * size([P, NP * QZ]) + size([P, NP, 2, NS]) +
                    3 * size([NS, NH, NS]))]
        at_s0 = at_s[0]
        kts = place("kts", [P, NP, NS], F32, at_s)
        qts = place("qts", [P, NP, NS], F32, at_s)
        qts_hi = place("qts_hi", [P, NP, NS], F32R, at_s)
        qts_lo = place("qts_lo", [P, NP, NS], F32R, at_s)
        silu_s = place("silu_s", [P, NP, NS], F32, at_s)
        ks_nat = place("ks_nat", [NS, D], F32, at_s)
        vs_nat = place("vs_nat", [NS, D], F32, at_s)
        ends.append(at_s[0])
        sp_n = place("sp_n", [NS, NH, NS], F32, ats)
        qz_hi = place("qz_hi", [P, NP * QZ], F32R, ats)
        qz_lo = place("qz_lo", [P, NP * QZ], F32R, ats)
        new = [ats[0]]
        qbd = place("qbd", [P, NP, 2, NS], F32, ats)
        xs_n = place("xs_n", [NS, NH, NS], F32, ats)
        as_n = place("as_n", [NS, NH, NS], F32, ats)
        ws_n = place("ws_n", [NS, NH, NS], F32, ats)
        z_row = place("z_row", [HQ, PAGES * P], F32, new)
        sp_b = place("sp_b", [P, PAGES, HQ], F32, new)
        ws_b = place("ws_b", [P, PAGES, HQ], F32, new)
        o_row = place("o_row", [HQ, D], F32, new)
        assert new[0] <= ats[0] and PAGES * P == NH * NS
        assert ats[0] <= at_s0
        at = [x1_base]
        kpage = place("kpage", [P, PAGES, D], F32, at)
        vpage = place("vpage", [P, PAGES, D], F32, at)
        os_s = place("os_s", [P, NP, NS], F32, at)
        on_s = place("on_s", [P, NP, NS], F32, at)
        assert at[0] <= at_x1[0]
        at = [x0_base]
        y_t = place("y_t", [P, KT, T], F32, at)
        at = [max(ends[1], area)]
        y_nat = place("y_nat", [P, TT, D], F32, at)
        ends.append(at[0])
        assert max(ends) <= nc.sbuf_usable_end, (max(ends), nc.sbuf_usable_end)
        sq_b = sq_a

        acc = [ctx.enter_context(nc.psum_tensor(f"acc{n}", [P, 2, 512], F32)) for n in range(2)]
        zb = [ctx.enter_context(nc.psum_tensor(f"zb{n}", [P, 512], F32)) for n in range(2)]
        ob = [ctx.enter_context(nc.psum_tensor(f"ob{n}", [P, 512], F32)) for n in range(2)]

        def wait_apart(eng, semaphore, value):
            if isinstance(value, int):
                if value > 0:
                    eng.wait_ge(semaphore, value)
                return
            value = eng.to_reg(value)
            eng.wait_ge(const_set, N_CONST)
            eng.wait_ge(semaphore, value)

        def rows(ap, n):
            return ap.partition_broadcast(n)

        def both(t):
            return t[:, :, 0:TH]

        def halves(ap):
            return ap.rearrange("p (c t) -> p c t", c=2)

        ident_set = sem("ident_set")
        const_set = sem("const_set")
        x_in = [sem(f"x_in{t}") for t in range(TT)]
        params_in = sem("params_in")
        small_in = sem("small_in")
        p_in = sem("p_in")
        raw_in = [sem(f"raw_in{s}") for s in range(SLOTS)]
        raw_scaled = sem("raw_scaled")
        hi_made = sem("hi_made")
        lo_made = sem("lo_made")
        panel_done = sem("panel_done")
        turned = sem("turned")
        acc_read = sem("acc_read")
        x_squared = sem("x_squared")
        h_new = sem("h_new")
        x_hi = sem("x_hi")
        x_lo = sem("x_lo")
        squared = sem("squared")
        sq_step = sem("sq_step")
        ssq_out = sem("ssq_out")
        vec = sem("vec")
        mean_sq = sem("mean_sq")
        logged = sem("logged")
        rooted = sem("rooted")
        normed = sem("normed")
        ws_masked = sem("ws_masked")
        bs_ready = sem("bs_ready")
        vh_made = sem("vh_made")
        mixed = sem("mixed")
        silu_done = sem("silu_done")
        s_ready = sem("s_ready")
        us_done = sem("us_done")
        y_made = sem("y_made")
        vout_step = sem("vout_step")
        vout_done = sem("vout_done")
        out_done = sem("out_done")
        kv_out = [sem(f"kv_out{b}") for b in range(2)]
        p_hi_made = sem("p_hi_made")
        p_lo_made = sem("p_lo_made")
        stats_done = sem("stats_done")
        gate_sig = sem("gate_sig")
        wp_in = sem("wp_in")
        wp_hi_made = sem("wp_hi_made")
        wp_lo_made = sem("wp_lo_made")
        z_full = sem("z_full")
        rel_done = sem("rel_done")
        act_step = sem("act_step")
        log_done = sem("log_done")
        soft_done = sem("soft_done")
        soft_split = sem("soft_split")
        after_done = sem("after_done")
        exp_done = sem("exp_done")
        o_full = sem("o_full")
        o_read = sem("o_read")
        sg_ready = sem("sg_ready")
        o_hi = sem("o_hi")
        o_lo = sem("o_lo")
        k_in = sem("k_in")
        v_in = [sem(f"v_in{c}") for c in range(2)]
        v_hi_made = sem("v_hi_made")
        v_lo_made = sem("v_lo_made")
        ws_split = sem("ws_split")
        bias_in = sem("bias_in")
        q_split = sem("q_split")
        qz_set = sem("qz_set")
        kp_hi_made = sem("kp_hi_made")
        zrow_full = sem("zrow_full")
        zrow_read = sem("zrow_read")
        v_full = sem("v_full")
        v_read = sem("v_read")
        os_sum = sem("os_sum")
        pages_in = sem("pages_in")
        qbd_set = sem("qbd_set")
        qz_zeroed = sem("qz_zeroed")
        zs_full = sem("zs_full")
        xs_done = sem("xs_done")
        logs_done = sem("logs_done")
        softs_done = sem("softs_done")
        afters_done = sem("afters_done")
        ds_done = sem("ds_done")
        exps_done = sem("exps_done")
        os_full = sem("os_full")
        os_read = sem("os_read")
        y_scaled = sem("y_scaled")

        N_CONST = 19

        N_START = 1 + TT + 2
        ACC_UG = N_START + 2 * N_AV + 4
        ACC_PL0 = ACC_UG + HALF * (N_UG + KT) + PKT
        ACC_B = ACC_PL0 + 2 * KT
        ACC_S = ACC_B + 6 * NP
        ACC_BO = ACC_S + NB * (KT // 2) + PKT
        TURN_S = N_START + N_AV + 4 + PKT + KT + 2 * NP
        TURNS_B = KT // 2
        ACC_Y = ACC_BO + 3 * KT
        ACC_END = ACC_Y + TT

        def tokens(t):
            return slice(t * P, (t + 1) * P) if t < QB else slice(TP, T)

        def sl(n):
            return slice(n, n + 1) if isinstance(n, int) else bass.ds(n, 1)

        def soft_at(kb):
            m = QB - 1 - kb
            return m * (m + 1) // 2 * P

        def bias_of(a, e):
            return bias[:, sl(a * 2 + e)]

        block = ctx.enter_context(nc.Block())

        @block.sync
        def _(sp):
            panel = Count()

            def load(src):
                if panel.reg is None and panel.now() < SLOTS:
                    pass
                else:
                    sp.wait_ge(lo_made, panel.now(1 - SLOTS))
                s = panel.slot(SLOTS)
                sp.dma_start(raw[:, s, :, :], src).then_inc(raw_in[s], 16)
                panel.step()

            for t in range(QB):
                sp.dma_start(x_nat[:, t, :], xp_v[:, t, :]).then_inc(x_in[t], 16)
            sp.dma_start(x_nat[0:NS, QB, :], xs_v).then_inc(x_in[QB], 16)
            r = 0
            for src, n in ((g_norm[0], KT), (g_norm[1], KT), (g_kv, KT), (g_ple[0], KT), (g_ple[1], KT),
                           (g_final, KT), (ln_v_g[0], E_A // P), (ln_v_b[0], E_A // P)):
                sp.dma_start(params[r:r + n, :], src.rearrange("(r c) -> r c", c=P)).then_inc(params_in, 16)
                r += n
            for k in range(SLOTS):
                load(w_in_a_v[:, :, E_A + k * P:E_A + (k + 1) * P])
            sp.dma_start(ws_nat[:, :, :], w_spatial[0].rearrange("g t s -> t g s")).then_inc(small_in, 16)
            sp.dma_start(bs_bc[:, :, 0:P], rows(b_spatial[0], P)).then_inc(small_in, 16)
            sp.dma_start(bias[:, :], rows(b_sb[0], P)).then_inc(small_in, 16)
            sp.dma_start(lng_bc[:, :], rows(ln_v_g[0], NS)).then_inc(small_in, 16)
            sp.dma_start(lnb_bc[:, :], rows(ln_v_b[0], NS)).then_inc(small_in, 16)
            sp.dma_start(bias_row[:, :], b_sb[0].rearrange("(h a b) -> h a b", a=1, b=1).to_broadcast([NH, NQ, 1]))\
                .then_inc(bias_in, 16)
            sp.dma_start(pages[:, :], page_table.rearrange("(a b) g -> a (b g)", a=1)).then_inc(pages_in, 16)
            with repeat(sp, N_AV // SLOTS - 1, (panel, SLOTS)) as i:
                for k in range(SLOTS):
                    load(w_in_a_v[:, :, bass.ds(i * (SLOTS * P) + (E_A + (SLOTS + k) * P), P)])
            def embed_inputs(layer):
                for t in range(QB):
                    sp.dma_start(p_nat[:, t, :], p_prompt[layer, 0, t * P:(t + 1) * P, :]).then_inc(p_in, 16)
                sp.dma_start(p_nat[0:NS, QB, :], p_sample[layer].rearrange("b q e -> (b q) e")).then_inc(p_in, 16)
                sp.dma_start(wp_raw[:, :, :], w_ple_v[layer]).then_inc(wp_in, 16)

            for hf in range(HALF):
                with repeat(sp, N_UG // SLOTS, (panel, SLOTS)) as i:
                    for k in range(SLOTS):
                        at0 = hf * D + (k // 2) * P + (k % 2) * 2 * E_A
                        load(w_in_a_v[:, :, bass.ds(i * (2 * P) + at0, P)])
                if hf == HALF - 1:
                    for n in range(KT):
                        if n == AHEAD:
                            sp.wait_ge(vh_made, N_AV)
                            embed_inputs(0)
                        load(w_out_a_v[hf][:, :, n * P:(n + 1) * P])
                    continue
                with repeat(sp, KT // SLOTS, (panel, SLOTS)) as i:
                    for k in range(SLOTS):
                        load(w_out_a_v[hf][:, :, bass.ds(i * (SLOTS * P) + k * P, P)])
                if hf == 0:
                    sp.wait_ge(vout_done, 1)
                    sp.dma_start(chunk_v_sample[0].rearrange("b q e -> (b q) e"), v_out[:, :]).then_inc(out_done, 16)

            def embed_panels(layer):
                for n in range(KT):
                    load(w_gate_v[layer][:, :, n * P:(n + 1) * P])

            embed_panels(0)

            def load_pair(i):
                for k in range(2):
                    load(w_kv_v[:, :, bass.ds(i * P + k * D, P)] if not isinstance(i, int) else
                         w_kv_v[:, :, i * P + k * D:i * P + k * D + P])
                for k in range(2):
                    load(w_in_b_v[:, :, bass.ds(i * P + k * D, P)] if not isinstance(i, int) else
                         w_in_b_v[:, :, i * P + k * D:i * P + k * D + P])

            def store_pair(i, b):
                sp.wait_ge(acc_read, i * 6 + (ACC_B + 5 + 2))
                cs = bass.ds(i * P, P) if not isinstance(i, int) else slice(i * P, (i + 1) * P)
                sp.dma_start(kp_v[:, :, cs], k_nat[:, b, :, :]).then_inc(kv_out[b], 16)
                sp.dma_start(vp_v[:, :, cs], vb_nat[:, b, :, :]).then_inc(kv_out[b], 16)

            load_pair(0)
            load_pair(1)
            with repeat(sp, NP // 2 - 1, (panel, 8)) as m:
                for b in range(2):
                    load_pair(m * 2 + (2 + b))
                    store_pair(m * 2 + b, b)
            for n in range(AHEAD):
                load(w_out_b_v[:, :, n * P:(n + 1) * P])
            store_pair(NP - 2, 0)
            store_pair(NP - 1, 1)
            sp.dma_start(k_sample.rearrange("b q h d -> (b q) (h d)"), ks_nat[:, :]).then_inc(out_done, 16)
            sp.dma_start(v_sample.rearrange("b q h d -> (b q) (h d)"), vs_nat[:, :]).then_inc(out_done, 16)
            sp.wait_ge(pages_in, 16)

            def page_of(b, g):
                one = pages[0:1, bass.ds(b * PAGES + g, 1)] if not isinstance(b, int) else \
                    pages[0:1, b * PAGES + g:b * PAGES + g + 1]
                return sp.value_load(one, min_val=0, max_val=NPOOL - 1)

            def load_keys(b):
                for g in range(PAGES):
                    src = ck_v[bass.ds(page_of(b, g), 1), :, :].rearrange("a t d -> t (a d)")
                    sp.dma_start(kpage[:, g, :], src).then_inc(k_in, 16)

            def load_values(b, before=True):
                for c in range(2):
                    if before:
                        wait_apart(sp, v_lo_made, b * 2 + (c - 1))
                    cs = slice(c * D // 2, (c + 1) * D // 2)
                    for g in range(PAGES):
                        src = cv_v[bass.ds(page_of(b, g), 1), :, cs].rearrange("a t d -> t (a d)")
                        sp.dma_start(vpage[:, g, cs], src).then_inc(v_in[c], 16)

            sp.wait_ge(panel_done, END_B + SLOTS)
            load_keys(0)
            load_values(0, False)
            sp.wait_ge(turned, TURN_S + TURNS_B)
            load_keys(1)
            with sp.Fori(0, NB - 2) as m:
                wait_apart(sp, turned, m * TURNS_B + (TURN_S + 2 * TURNS_B))
                load_keys(m + 2)
                load_values(m + 1)
            load_values(NB - 1)
            sp.wait_ge(zrow_full, NB)
            embed_inputs(1)
            sp.wait_ge(v_full, 2 * NB)
            for n in range(AHEAD, KT):
                load(w_out_b_v[:, :, n * P:(n + 1) * P])
            embed_panels(1)
            for t in range(TT):
                sp.wait_ge(acc_read, ACC_Y + t + 1 + 2)
                if t < QB:
                    sp.dma_start(yp_v[:, t, :], y_nat[:, t, :]).then_inc(out_done, 16)
                else:
                    sp.dma_start(y_sample.rearrange("b q d -> (b q) d"), y_nat[0:NS, t, :]).then_inc(out_done, 16)
            sp.wait_ge(out_done, 16 * (3 + TT))
            assert panel.now() == END

        @block.gpsimd
        def _(pool):
            panel, accs, sq_n, news, blk = Count(), Count(), Count(), Count(), Count()

            pool.memset(ident[:, :], 0.0).then_inc(ident_set, 1)
            pool.memset(ws_ts[:, 0, 0, :], 0.0).then_inc(panel_done, SLOTS)
            pool.memset(ws_ts[:, 0, 1, :], 0.0).then_inc(acc_read, 2)
            pool.memset(ws_ts[:, 0, 2, :], 0.0).then_inc(o_read, 2)
            pool.wait_ge(ident_set, 1)
            pool.affine_select(out=ident[:, :], in_=ident[:, :], compare_op=ALU.not_equal, fill=1.0, base=0,
                               pattern=[[-1, P]], channel_multiplier=1).then_inc(ident_set, 1)
            pool.memset(ones[:, :], 1.0).then_inc(const_set, 1)
            pool.memset(negones[:, :], -1.0).then_inc(const_set, 1)
            pool.memset(negtri[:, :], -1.0).then_inc(const_set, 1)
            pool.memset(rep[:, :, :], 0.0).then_inc(const_set, 1)
            pool.memset(blockdiag[:, :, :], 1.0).then_inc(const_set, 1)
            pool.memset(mv[:, :, :], 1.0).then_inc(const_set, 1)
            pool.memset(eps[:, :], EPS).then_inc(const_set, 1)
            pool.memset(unseen[:, :], FAR).then_inc(const_set, 1)
            pool.memset(unseen_n[:, :, :, :], 0.0).then_inc(const_set, 1)
            pool.wait_ge(const_set, 9)
            pool.affine_select(out=negtri[:, :], in_=negtri[:, :], compare_op=ALU.is_ge, fill=0.0, base=0,
                               pattern=[[-1, P]], channel_multiplier=1).then_inc(const_set, 1)
            pool.affine_select(out=rep[:, :, :], in_=rep[:, :, :], compare_op=ALU.not_equal, fill=1.0, base=0,
                               pattern=[[0, NB], [-1, NQ]], channel_multiplier=1).then_inc(const_set, 1)
            pool.affine_select(out=blockdiag[:, :, :], in_=blockdiag[:, :, :], compare_op=ALU.is_ge, fill=0.0,
                               base=0, pattern=[[-NQ, NB], [0, NQ]], channel_multiplier=1).then_inc(const_set, 1)
            pool.affine_select(out=unseen[:, :], in_=unseen[:, :], compare_op=ALU.is_ge, fill=0.0, base=0,
                               pattern=[[-1, P]], channel_multiplier=1).then_inc(const_set, 1)
            pool.affine_select(out=unseen_n[:, :, :, :], in_=unseen_n[:, :, :, :], compare_op=ALU.is_ge, fill=FAR,
                               base=0, pattern=[[0, NH], [-NQ, NB], [0, NQ]], channel_multiplier=1)\
                .then_inc(const_set, 1)
            pool.wait_ge(ident_set, 2)
            pool.wait_ge(const_set, 14)
            pool.tensor_copy(ident_b[:, :], ident[:, :]).then_inc(const_set, 1)
            pool.tensor_copy(negtri_r[:, :], negtri[:, :]).then_inc(const_set, 1)
            pool.tensor_copy(negones_r[:, :], negones[:, :]).then_inc(const_set, 1)
            pool.affine_select(out=unseen_n[:, :, :, :], in_=unseen_n[:, :, :, :], compare_op=ALU.is_gt, fill=FAR,
                               base=0, pattern=[[0, NH], [NQ, NB], [1, NQ]], channel_multiplier=-1)\
                .then_inc(const_set, 1)
            pool.affine_select(out=blockdiag[:, :, :], in_=blockdiag[:, :, :], compare_op=ALU.is_ge, fill=0.0,
                               base=NQ - 1, pattern=[[NQ, NB], [0, NQ]], channel_multiplier=-1)\
                .then_inc(const_set, 1)

            def gain_of(p):
                if p < END_AV:
                    return g_norm_c[0]
                if p < END_A:
                    return g_norm_c[0] if (p - END_AV) % (N_UG + KT) < N_UG else None
                if p < END_PL0:
                    return g_ple_c[0]
                if p < END_B:
                    return g_kv_c if (p - END_PL0) % 4 < 2 else g_norm_c[1]
                if p < END_BO:
                    return None
                return g_ple_c[1]

            def scale(gain):
                s = panel.slot(SLOTS)
                pool.wait_ge(raw_in[s], panel.lap(SLOTS) * 16 + 16)
                if gain is None:
                    pool.engine_nop().then_inc(raw_scaled, 1)
                else:
                    pool.tensor_tensor(raw[:, s, :, :], raw[:, s, :, :], gain[:, :, None].to_broadcast([P, KT, P]),
                                       ALU.mult).then_inc(raw_scaled, 1)
                panel.step()

            def scale_next():
                if panel.reg is None and panel.now() >= END:
                    return
                p = panel.before + panel.here
                if panel.reg is not None:
                    for t in range(turns[0]):
                        assert gain_of(p + t * panel.per) is gain_of(p)
                scale(gain_of(p))

            turns = [0]

            sq_scratch = [g_r]

            def squares(n, embedded=False):
                if embedded:
                    news.step()
                    pool.wait_ge(h_new, news.now())
                else:
                    accs.step()
                    pool.wait_ge(acc_read, accs.now(2))
                sq_n.step()
                hn = h[:, n, :]
                if n == 0:
                    pool.tensor_tensor(sumsq[:, :], hn, hn, ALU.mult).then_inc(squared, 1)
                    return
                pool.wait_ge(squared, sq_n.now(-1))
                pool.tensor_tensor(sq_scratch[0][:, :], hn, hn, ALU.mult).then_inc(sq_step, 1)
                sq_steps.step()
                pool.wait_ge(sq_step, sq_steps.now())
                pool.tensor_tensor(sumsq[:, :], sumsq[:, :], sq_scratch[0][:, :], ALU.add).then_inc(squared, 1)

            sq_steps = Count()

            pool.wait_ge(acc_read, 2 + TT + 1)
            for _ in range(AHEAD):
                scale_next()
            accs.step(N_START)
            pool.wait_ge(acc_read, accs.now(2))
            pool.affine_select(out=ws_t[:, :, :], in_=ws_t[:, :, :], compare_op=ALU.is_ge, fill=0.0, base=0,
                               pattern=[[0, NG], [1, P]], channel_multiplier=-1).then_inc(ws_masked, 1)
            pool.wait_ge(small_in, 80)
            pool.tensor_copy(bs_bc[:, :, P:P + NS].rearrange("p g (b q) -> p g b q", q=NQ),
                             bs_bc[:, :, 0:NQ][:, :, None, :].to_broadcast([P, NG, NB, NQ]))\
                .then_inc(bs_ready, 1)

            turns[0] = N_AV // SLOTS - 1
            with repeat(pool, turns[0], (panel, SLOTS)):
                for k in range(SLOTS):
                    scale_next()
            for k in range(SLOTS):
                scale_next()
            pool.wait_ge(vout_step, 1)
            pool.tensor_tensor(v_out[:, :], v_out[:, :], lng_bc[:, :], ALU.mult).then_inc(vout_step, 1)
            pool.wait_ge(vout_step, 2)
            pool.tensor_tensor(v_out[:, :], v_out[:, :], lnb_bc[:, :], ALU.add).then_inc(vout_done, 1)
            ytile = Count()

            def mix(hf):
                def turn():
                    for k in range(2):
                        scale_next()
                        scale_next()
                        ytile.step()
                        pool.wait_ge(s_ready, ytile.now())
                        pool.tensor_tensor(u_r[:, :], u_r[:, :], s_t[:, :], ALU.mult).then_inc(us_done, 1)
                        pool.wait_ge(us_done, ytile.now())
                        pool.wait_ge(silu_done, ytile.now())
                        pool.tensor_tensor(s_t[:, :], u_r[:, :], g_r[:, :], ALU.mult).then_inc(y_made, 1)

                turns[0] = N_UG // SLOTS - 1
                with repeat(pool, turns[0], (panel, SLOTS), (ytile, 2)):
                    turn()
                turn()

            mix(0)
            for n in range(KT):
                scale_next()
            mix(1)
            accs.step(ACC_PL0 - KT - N_START)
            for n in range(KT):
                squares(n)
                scale_next()
            sq_scratch[0] = sq_a

            def embed():
                for n in range(KT):
                    scale_next()
                    if n > 0:
                        squares(n - 1, True)
                squares(KT - 1, True)

            embed()

            turns[0] = NP - 1
            with repeat(pool, turns[0], (panel, 4)):
                for k in range(4):
                    scale_next()
            for k in range(4):
                scale_next()

            pool.wait_ge(acc_read, ACC_S - 2 + 2)
            pool.wait_ge(o_lo, NP)
            pool.memset(qbd[:, :, :, :], 0.0).then_inc(qbd_set, 1)
            pool.wait_ge(qbd_set, 1)
            for e in range(2):
                r = slice(e * DH, (e + 1) * DH)
                pool.tensor_copy(qbd[r, :, e, :], qts[r, :, :]).then_inc(qbd_set, 1)
            pool.wait_ge(qbd_set, 3)
            pool.memset(qz_hi[:, :].bitcast(F32), 0.0).then_inc(qz_zeroed, 1)
            pool.wait_ge(qz_zeroed, 1)
            pool.memset(qz_lo[:, :].bitcast(F32), 0.0).then_inc(qz_zeroed, 1)
            pool.wait_ge(qz_zeroed, 2)
            pool.wait_ge(q_split, 2)

            def queries(b):
                bq = slice(b * NQ, (b + 1) * NQ) if isinstance(b, int) else bass.ds(b * NQ, NQ)
                for n, (dst, src) in enumerate(((qz_hi, qts_hi), (qz_lo, qts_lo))):
                    wait_apart(pool, qz_set, b * 4 + 2 * n)
                    for e in range(2):
                        r = slice(e * DH, (e + 1) * DH)
                        pool.tensor_copy(dst[r, :].rearrange("p (a n) -> p a n", n=QZ)[:, :, e * NQ:(e + 1) * NQ],
                                         src[r, :, bq]).then_inc(qz_set, 1)

            def split_values(b):
                for c in range(2):
                    if c == 0:
                        wait_apart(pool, qz_set, b * 4 + (4 if isinstance(b, int) and b == NB - 1 else 8))
                    wait_apart(pool, v_hi_made, b * 2 + (c + 1))
                    cs = slice(c * D // 2, (c + 1) * D // 2)
                    pool.tensor_tensor(vp_lo[:, :, cs], vpage[:, :, cs], vp_hi[:, :, cs].bitcast(F32), ALU.subtract)\
                        .then_inc(v_lo_made, 1)

            queries(0)
            pool.wait_ge(lo_made, END_B + AHEAD)
            with pool.Fori(0, NB - 1) as m:
                wait_apart(pool, zrow_full, m + 1)
                wait_apart(pool, v_lo_made, m * 2)
                queries(m + 1)
                split_values(m)
            split_values(NB - 1)

            accs.step(ACC_BO - ACC_PL0)
            for n in range(KT):
                squares(n)
                scale_next()
            embed()

        @block.scalar
        def _(act):
            panel, accs, news, roots = Count(), Count(), Count(), Count()

            def split_next():
                if panel.reg is None and panel.now() >= END:
                    return
                s = panel.slot(SLOTS)
                act.wait_ge(raw_scaled, panel.now(1))
                act.wait_ge(panel_done, panel.now(1))
                nc.scalar.activation(w_hi[:, s, :, :], raw[:, s, :, :], ACT.Copy).then_inc(hi_made, 1)
                panel.step()

            def split_x(n, into, embedded=False):
                if embedded:
                    news.step()
                    act.wait_ge(h_new, news.now())
                else:
                    accs.step()
                    wait_apart(act, acc_read, accs.now(2))
                nc.scalar.activation(act_hi[into][:, sl(n), :], h[:, sl(n), :], ACT.Copy).then_inc(x_hi, 1)

            def exp_and_log():
                nc.scalar.preload_act_table_set("natural_log_exp_and_others")

            def root():
                roots.step()
                exp_and_log()
                act.wait_ge(ssq_out, norms.now(1))
                for c in range(2):
                    ins = nc.scalar.activation(rinv[:, c * TH:(c + 1) * TH], zb[c][:, 0:TH], ACT.Ln, scale=1.0 / D,
                                               bias=eps[:, 0:1])
                ins.then_inc(logged, 1)
                norms.step()
                act.wait_ge(logged, norms.now())
                nc.scalar.activation(rinv[:, :], rinv[:, :], ACT.Exp, scale=-0.5).then_inc(rooted, 1)

            norms = Count()

            def split_p(layer):
                for kt in range(PKT):
                    accs.step()
                    act.wait_ge(acc_read, accs.now(2))
                    nc.scalar.activation(p_hi[:, kt, :], p_t[:, kt, :], ACT.Copy).then_inc(p_hi_made, 1)
                act.wait_ge(wp_in, 16 * (layer + 1))
                nc.scalar.activation(wp_hi[:, :, :], wp_raw[:, :, :], ACT.Copy).then_inc(wp_hi_made, 1)

            for t in range(TT):
                accs.step()
                act.wait_ge(acc_read, accs.now(2))
                nc.scalar.activation(act_hi[0][:, :, tokens(t)], h[:, :, tokens(t)], ACT.Copy)\
                    .then_inc(x_hi, 1 if t < QB else KT - QB)
                nc.scalar.activation(sq_x[:, :, tokens(t)], h[:, :, tokens(t)], ACT.Square).then_inc(x_squared, 1)
            accs.step()
            for _ in range(AHEAD):
                split_next()
            root()
            with repeat(act, N_AV // SLOTS, (panel, SLOTS)):
                for k in range(SLOTS):
                    split_next()
            act.wait_ge(normed, 1)
            nc.scalar.activation(ln_s[:, 1, :], ln_s[:, 0, :], ACT.Sqrt).then_inc(rooted, 1)
            act.wait_ge(normed, 2)
            nc.scalar.activation(v_out[:, :], v_nat[0:NS, QB, :], ACT.Identity, bias=ln_s[0:NS, 3, QB:QB + 1],
                                 scale=ln_s[0:NS, 2, QB:QB + 1]).then_inc(vout_step, 1)
            ytile = Count()

            def normalise(j, k):
                for t in range(TT):
                    n = P if t < QB else NS
                    ins = nc.scalar.activation(vhat[0:n, k, t, :], v_nat[0:n, t, bass.ds(j * P, P)], ACT.Identity,
                                               bias=ln_s[0:n, 3, t:t + 1], scale=ln_s[0:n, 2, t:t + 1])
                ins.then_inc(vh_made, 1)

            def mix_tile(j, jy, k, last=False):
                ytile.step()
                split_next()
                split_next()
                accs.step(2)
                act.wait_ge(acc_read, accs.now(2))
                nc.scalar.activation(g_r[:, :], g_r[:, :], ACT.Silu).then_inc(silu_done, 1)
                if not last:
                    normalise(j + 1, 1 - k)
                wait_apart(act, y_made, ytile.now())
                nc.scalar.activation(act_hi[1][:, bass.ds(jy, 1), :].rearrange("p a t -> p (a t)"), s_t[:, :],
                                     ACT.Copy).then_inc(x_hi, 1)

            accs.step(ACC_UG - 1 - TT)
            normalise(0, 0)
            for hf in range(HALF):
                turns = N_UG // SLOTS - (1 if hf == HALF - 1 else 0)
                with repeat(act, turns, (panel, SLOTS), (ytile, 2), (accs, 4)) as i:
                    for k in range(2):
                        mix_tile(i * 2 + (hf * KT + k), i * 2 + k, k)
                if hf == HALF - 1:
                    for k in range(2):
                        mix_tile(HALF * KT - 2 + k, KT - 2 + k, k, k == 1)
                    split_p(0)
                if hf == 0:
                    with repeat(act, KT // SLOTS, (panel, SLOTS), (accs, SLOTS)):
                        for k in range(SLOTS):
                            split_next()
                            accs.step()
                else:
                    with repeat(act, KT // SLOTS, (panel, SLOTS), (accs, SLOTS)) as i:
                        for k in range(SLOTS):
                            split_x(i * SLOTS + k, 0)
                            split_next()

            def embed(layer):
                for n in range(KT):
                    if n == 0:
                        root()
                    split_next()
                    accs.step()
                    act.wait_ge(acc_read, accs.now(2))
                    nc.scalar.activation(gate[:, n % 2, :], gate[:, n % 2, :], ACT.Sigmoid).then_inc(gate_sig, 1)
                    accs.step()
                    if n > 0:
                        embedded(layer, n - 1)
                embedded(layer, KT - 1)

            def embedded(layer, n):
                if layer == 0:
                    split_x(n, 1, True)
                    return
                news.step()
                act.wait_ge(h_new, news.now())
                nc.scalar.activation(y_t[:, n, :], h[:, n, :], ACT.Identity, scale=g_final_c[:, n:n + 1])\
                    .then_inc(y_scaled, 1)

            embed(0)
            root()

            blk, wblk, opair, ah = Count(), Count(), Count(), Count()

            def logs(n, a):
                e, kb = n // QB, QB - 1 - n % QB
                w = (QB - kb) * P
                blk.step()
                z = absz[:, n % 2, 0:w]
                wait_apart(act, z_full, blk.now())
                nc.scalar.activation(z, zb[n % 2][:, 0:w], ACT.Abs, bias=bias_of(a, e)).then_inc(act_step, 1)
                ah.step()
                act.wait_ge(act_step, ah.now())
                nc.scalar.activation(z, z, ACT.Exp, scale=-1.0).then_inc(act_step, 1)
                ah.step()
                act.wait_ge(act_step, ah.now())
                nc.scalar.activation(z, z, ACT.Ln, bias=1.0).then_inc(log_done, 1)

            def weights(n, a):
                e, kb = n // QB, QB - 1 - n % QB
                w = (QB - kb) * P
                wblk.step()
                wait_apart(act, after_done, wblk.now())
                nc.scalar.activation(wts[:, n % 2, 0:w], zb[n % 2][:, 0:w], ACT.Exp, bias=bias_of(a, e))\
                    .then_inc(exp_done, 1)

            def pair_step(i, par, dense, att, prev):
                for n in range(2 * QB):
                    if att:
                        logs(n, i - 1)
                    if att and (n > 0 or prev):
                        weights((n - 1) % (2 * QB), i - 1 if n > 0 else i - 2)
                    if dense and n % 2 == 0:
                        split_next()
                    if n == 2 and prev:
                        opair.step()
                        out_hi(i - 2)
                if att and not dense:
                    weights(2 * QB - 1, i - 1)
                    opair.step()
                    out_hi(i - 1)
                if dense:
                    accs.step(6)
                    act.wait_ge(acc_read, accs.now(2))
                    nc.scalar.activation(silu_g[:, par, :], gb_r[:, 0:TP], ACT.Silu)
                    nc.scalar.activation(silu_s[:, sl(i), :].rearrange("p a t -> p (a t)"), gb_r[:, TP:T], ACT.Silu)\
                        .then_inc(sg_ready, 1)
                    exp_and_log()

            def out_hi(a):
                wait_apart(act, o_read, opair.now(2))
                nc.scalar.activation(act_hi[0][:, sl(a), 0:TP].rearrange("p a t -> p (a t)"), o_s[:, :], ACT.Copy)\
                    .then_inc(o_hi, 1)

            pair_step(0, 0, True, False, False)
            pair_step(1, 1, True, True, False)
            with repeat(act, NP // 2 - 1, (panel, 8), (blk, 4 * QB), (wblk, 4 * QB), (ah, 8 * QB), (accs, 12),
                        (opair, 2)) as m:
                pair_step(m * 2 + 2, 0, True, True, True)
                pair_step(m * 2 + 3, 1, True, True, True)
            nc.scalar.activation(qts_hi[:, :, :], qts[:, :, :], ACT.Copy).then_inc(q_split, 1)
            pair_step(NP, 0, False, True, True)

            samp = Count()

            def logs_s(dst):
                ah.step()
                act.wait_ge(act_step, ah.now())
                nc.scalar.activation(dst, dst, ACT.Exp, scale=-1.0).then_inc(act_step, 1)
                ah.step()
                act.wait_ge(act_step, ah.now())
                nc.scalar.activation(dst, dst, ACT.Ln, bias=1.0).then_inc(logs_done, 1)

            tiles = Count(TURN_S)

            def split_keys(twos):
                for two in twos:
                    tiles.step()
                    wait_apart(act, turned, tiles.now())
                    nc.scalar.activation(kp_hi[:, 2 * two:2 * two + 2, :], acc[tiles_acc.slot(2)][:, :, :], ACT.Copy)\
                        .then_inc(kp_hi_made, 1)
                    tiles_acc.step()

            def logs_b():
                wait_apart(act, zs_full, samp.now(1))
                nc.scalar.activation(sp_b[:, :, :].rearrange("p g n -> p (g n)"), zb[0][:, 0:PAGES * HQ], ACT.Abs)\
                    .then_inc(act_step, 1)
                logs_s(sp_b[:, :, :].rearrange("p g n -> p (g n)"))

            def step_s(logs=True, keys=True):
                samp.step()
                wait_apart(act, afters_done, samp.now())
                nc.scalar.activation(ws_b[:, :, :].rearrange("p g n -> p (g n)"), zb[0][:, 0:PAGES * HQ], ACT.Exp)\
                    .then_inc(act_step, 1)
                ah.step()
                act.wait_ge(act_step, ah.now())
                nc.scalar.activation(ws_hi[:, :, :], ws_b[:, :, :], ACT.Copy).then_inc(exps_done, 1)
                if keys:
                    split_keys(range(0, 2))
                if logs:
                    split_values(0)
                    logs_b()
                if keys:
                    split_keys(range(2, KT // 2))
                if logs:
                    split_values(1)

            vhalf = Count()

            def split_values(c, used=True):
                if used:
                    wait_apart(act, v_full, vhalf.now(-1))
                act.wait_ge(v_in[c], vhalf.lap(2) * (16 * PAGES) + 16 * PAGES)
                vhalf.step()
                cs = slice(c * D // 2, (c + 1) * D // 2)
                nc.scalar.activation(vp_hi[:, :, cs], vpage[:, :, cs], ACT.Copy).then_inc(v_hi_made, 1)

            tiles_acc = Count(ACC_S)
            act.wait_ge(kv_out[0], 16 * NP)
            act.wait_ge(kv_out[1], 16 * NP)
            split_keys(range(KT // 2))
            act.wait_ge(xs_done, 1)
            nc.scalar.activation(as_n[:, :, :], xs_n[:, :, :], ACT.Abs).then_inc(act_step, 1)
            logs_s(as_n[:, :, :])
            samp.step()
            act.wait_ge(ds_done, 1)
            nc.scalar.activation(ws_n[:, :, :], xs_n[:, :, :], ACT.Exp).then_inc(exps_done, 1)
            act.wait_ge(o_lo, NP)
            split_values(0, False)
            logs_b()
            split_keys(range(KT // 2))
            split_values(1, False)
            with repeat(act, NB - 2, (samp, 1), (ah, 3), (tiles, TURNS_B), (tiles_acc, TURNS_B), (vhalf, 2)):
                step_s()
            step_s(True, False)
            step_s(False, False)
            act.wait_ge(os_sum, 1)
            nc.scalar.activation(act_hi[0][:, :, TP:T], os_s[:, :, :], ACT.Copy).then_inc(o_hi, 1)

            accs.step(ACC_BO - PKT - ACC_S)
            split_p(1)
            with repeat(act, KT // SLOTS, (panel, SLOTS), (accs, SLOTS)) as i:
                for k in range(SLOTS):
                    split_x(i * SLOTS + k, 1)
                    split_next()
            embed(1)
            roots.step()
            act.wait_ge(mean_sq, 1)
            nc.scalar.activation(ln_s[:, 1, :], ln_s[:, 0, :], ACT.Sqrt).then_inc(rooted, 1)

        @block.tensor
        def _(pe):
            panel, accs, blk = Count(), Count(), Count()

            def take_acc():
                pe.wait_ge(acc_read, accs.now(1))
                t = acc[accs.slot(2)]
                accs.step()
                return t

            def products(t, s, xh, xl, kts, start, stop, split=None, sum_at=None):
                for kt in kts:
                    if kt == sum_at:
                        sum_squares()
                    if split is not None:
                        pe.wait_ge(x_lo, split + kt + 1)
                    for wt, xt in ((w_hi, xh), (w_hi, xl), (w_lo, xh)):
                        for c in range(2):
                            mm = pe.matmul(t[:, c, 0:TH], wt[:, s, kt, :], xt[:, kt, c * TH:(c + 1) * TH],
                                           start=start and kt == kts[0] and wt is w_hi and xt is xh,
                                           stop=stop and kt == kts[-1] and wt is w_lo)
                return mm

            def gemm_by_halves(a, ready, value):
                pe.wait_ge(lo_made, panel.now(1))
                t = take_acc()
                s = panel.slot(SLOTS)
                for c in range(2):
                    if c == 1:
                        pe.wait_ge(ready, value)
                    for kt in range(KT):
                        for wt, xt in ((w_hi, act_hi[a]), (w_hi, act_lo[a]), (w_lo, act_hi[a])):
                            mm = pe.matmul(t[:, c, 0:TH], wt[:, s, kt, :], xt[:, kt, c * TH:(c + 1) * TH],
                                           start=kt == 0 and wt is w_hi and xt is act_hi[a],
                                           stop=kt == KT - 1 and wt is w_lo)
                mm.then_inc(panel_done, 1)
                panel.step()

            def gemm(a, split=None, sum_at=None):
                pe.wait_ge(lo_made, panel.now(1))
                t = take_acc()
                s = panel.slot(SLOTS)
                products(t, s, act_hi[a], act_lo[a], range(KT), True, True, split, sum_at).then_inc(panel_done, 1)
                panel.step()

            def turn_tokens(src):
                t = take_acc()
                for c in range(QB):
                    pe.transpose(t[:, 0, c * P:(c + 1) * P], src[:, c * P:(c + 1) * P], ident[:, :])
                pe.transpose(t[0:NS, 1, 0:P], src[:, TP:T], ident[:, :]).then_inc(turned, 1)

            def sum_squares():
                sums.step()
                pe.wait_ge(squared, sums.now() * KT)
                for c in range(2):
                    mm = pe.matmul(zb[c][:, 0:TH], ones[:, :], sumsq[:, c * TH:(c + 1) * TH], start=True, stop=True)
                mm.then_inc(ssq_out, 1)

            sums = Count()

            pe.wait_ge(ident_set, 2)
            for c in range(TT):
                n = P if c < QB else NS
                pe.wait_ge(x_in[c], 16)
                t = take_acc()
                for kt in range(KT):
                    mm = pe.transpose(t[:, kt // 4, kt % 4 * P:kt % 4 * P + n], x_nat[0:n, c, kt * P:(kt + 1) * P],
                                      ident[0:n, 0:n])
                mm.then_inc(turned, 1)
            pe.wait_ge(params_in, 16 * 8)
            t = take_acc()
            pe.transpose(t[:, 0, 0:N_COL], params[:, :], ident[0:N_COL, 0:N_COL]).then_inc(turned, 1)
            pe.wait_ge(const_set, N_CONST)
            for c in range(2):
                pe.wait_ge(x_squared, (TH - 1) // P + 1 if c == 0 else TT)
                for kt in range(KT):
                    mm = pe.matmul(zb[c][:, 0:TH], ones[:, :], sq_x[:, kt, c * TH:(c + 1) * TH], start=kt == 0,
                                   stop=kt == KT - 1)
            mm.then_inc(ssq_out, 1)
            pe.wait_ge(small_in, 80)
            for half in range(2):
                t = take_acc()
                for g in range(NG // 2):
                    mm = pe.transpose(t[:, 0, g * P:(g + 1) * P], ws_nat[:, half * (NG // 2) + g, :], ident[:, :])
                mm.then_inc(turned, 1)
            assert accs.now() == N_START
            pe.wait_ge(x_lo, KT)

            def value_tiles():
                for k in range(SLOTS + 1):
                    if k < SLOTS:
                        gemm(0)
                    if k > 0:
                        turn_tokens(vt[:, (k - 1) % 2, :])

            with repeat(pe, N_AV // SLOTS, (panel, SLOTS), (accs, 2 * SLOTS)):
                value_tiles()

            pe.wait_ge(ws_masked, 1)
            t = take_acc()
            pe.matmul(t[0:NS, 0, 0:NG * NQ], rep[:, :, :], ws_t[:, :, 0:NQ], start=True, stop=True)\
                .then_inc(turned, 1)
            for half in range(2):
                t = take_acc()
                pe.matmul(t[:, 0, :], ones[:, :], ws_t[:, half * 4:half * 4 + 4, :], start=True, stop=True)\
                    .then_inc(turned, 1)
            pe.wait_ge(acc_read, accs.now())
            t = take_acc()
            pe.matmul(t[:, 0, 0:NG * NS], ones[0:NS, :], ws_ts[:, :, :, :], start=True, stop=True)\
                .then_inc(turned, 1)

            ytile = Count()

            def turn_p(layer):
                pe.wait_ge(p_in, 16 * TT * (layer + 1))
                for kt in range(PKT):
                    t = take_acc()
                    for c in range(QB):
                        pe.transpose(t[:, 0, c * P:(c + 1) * P], p_nat[:, c, kt * P:(kt + 1) * P], ident[:, :])
                    pe.transpose(t[:, 1, 0:NS], p_nat[0:NS, QB, kt * P:(kt + 1) * P], ident[0:NS, 0:NS])\
                        .then_inc(turned, 1)

            def spatial(k, g):
                ytile.step()
                pe.wait_ge(vh_made, ytile.now())
                gs = bass.ds(g, 1)
                for c in range(QB):
                    pe.matmul(zb[k][:, c * P:(c + 1) * P], vhat[:, k, c, :], ws_t[:, gs, :].rearrange("p a t -> p (a t)"),
                              start=True, stop=True)
                pe.matmul(ob[k][:, 0:NS], vhat[0:NS, k, QB, :],
                          ws_ts[:, gs, :, :].rearrange("p a b q -> p (a b q)"), start=True, stop=True)\
                    .then_inc(mixed, 1)

            for hf in range(HALF):
                with repeat(pe, N_UG // SLOTS, (panel, SLOTS), (accs, 4), (ytile, 2)) as i:
                    for k in range(2):
                        gemm(0)
                        spatial(k, i + hf * (NG // 2))
                        gemm(0)
                if hf == HALF - 1:
                    turn_p(0)
                with repeat(pe, KT // SLOTS, (panel, SLOTS), (accs, SLOTS)):
                    for k in range(SLOTS):
                        gemm(1, KT * (1 + hf) if k == 0 else None)

            def embed(layer, a):
                for n in range(KT):
                    if n > 0:
                        gemm(a)
                    else:
                        gemm(a, KT * (3 + layer * 2), KT - 1)
                        pe.wait_ge(wp_lo_made, layer + 1)
                    t = take_acc()
                    cs = slice(n * P, (n + 1) * P)
                    for kt in range(PKT):
                        for wt, xt in ((wp_hi, p_hi), (wp_hi, p_lo), (wp_lo, p_hi)):
                            for c in range(2):
                                mm = pe.matmul(t[:, c, 0:TH], wt[:, kt, cs], xt[:, kt, c * TH:(c + 1) * TH],
                                               start=kt == 0 and wt is wp_hi and xt is p_hi,
                                               stop=kt == PKT - 1 and wt is wp_lo)
                    mm.then_inc(turned, 1)

            embed(0, 0)

            wblk, opair = Count(), Count()

            def logits(n, par):
                e, kb = n // QB, QB - 1 - n % QB
                w = (QB - kb) * P
                if not (blk.reg is None and blk.now() < 2):
                    pe.wait_ge(exp_done, blk.now(-1))
                r = slice(e * DH, (e + 1) * DH)
                pe.matmul(zb[n % 2][:, 0:w], kt_t[r, par, kb * P:(kb + 1) * P], qt_t[r, par, kb * P:TP],
                          start=True, stop=False, skip_group_check=True)
                pe.matmul(zb[n % 2][:, 0:P], ident_b[:, :], unseen[:, :], start=False, stop=False,
                          skip_group_check=True).then_inc(z_full, 1)
                blk.step()

            def after(n):
                e, kb = n // QB, QB - 1 - n % QB
                w = (QB - kb) * P
                wblk.step()
                pe.wait_ge(soft_split, wblk.now())
                for soft in (soft_hi, soft_lo):
                    for later in range(QB - 1, kb, -1):
                        lw = (QB - later) * P
                        pe.matmul(zb[n % 2][:, w - lw:w], negones_r[:, :],
                                  soft[:, e, soft_at(later):soft_at(later) + lw], start=False, stop=False,
                                  skip_group_check=True)
                    mm = pe.matmul(zb[n % 2][:, 0:w], negtri_r[:, :], soft[:, e, soft_at(kb):soft_at(kb) + w],
                                   start=False, stop=soft is soft_lo, skip_group_check=True)
                mm.then_inc(after_done, 1)

            def values(n, par):
                e, kb = n // QB, QB - 1 - n % QB
                w = (QB - kb) * P
                pe.wait_ge(exp_done, wblk.now())
                if n == 0:
                    opair.step()
                    pe.wait_ge(o_read, opair.now())
                r = slice(e * DH, (e + 1) * DH)
                mm = pe.matmul(ob[par][r, kb * P:TP], vb_nat[:, par, kb, r], wts[:, n % 2, 0:w],
                               start=kb == QB - 1, stop=kb == 0, skip_group_check=True)
                if n == 2 * QB - 1:
                    mm.then_inc(o_full, 1)

            def pair_step(par, dense, att, prev, first=False):
                for n in range(2 * QB):
                    if att and n == 0:
                        logits(n, 1 - par)
                    if att and (n > 0 or prev):
                        after((n - 1) % (2 * QB))
                    if dense:
                        s = panel.slot(SLOTS)
                        if n % 2 == 0:
                            pe.wait_ge(lo_made, panel.now(1))
                            t = take_acc()
                        half = range(KT // 2) if n % 2 == 0 else range(KT // 2, KT)
                        mm = products(t, s, act_hi[1], act_lo[1], half, n % 2 == 0, n % 2 == 1,
                                      KT * 4 if first and n < 2 else None, KT - 1 if first and n == 1 else None)
                        if n % 2 == 1:
                            mm.then_inc(panel_done, 1)
                            panel.step()
                    if att and n < 2 * QB - 1 and (n > 0 or prev):
                        logits(n + 1, 1 - par)
                    if att and (n > 0 or prev):
                        values((n - 1) % (2 * QB), 1 - par if n > 0 else par)
                    if att and n == 0 and not prev:
                        logits(1, 1 - par)
                    if dense and n == 3:
                        turn_tokens(kt_t[:, par, :])
                    if dense and n == 5:
                        turn_tokens(vt_t[:, :])
                if att and not dense:
                    after(2 * QB - 1)
                    values(2 * QB - 1, 1 - par)

            pair_step(0, True, False, False, True)
            pair_step(1, True, True, False)
            with repeat(pe, NP // 2 - 1, (panel, 8), (accs, 12), (blk, 4 * QB), (wblk, 4 * QB), (opair, 2)):
                pair_step(0, True, True, True)
                pair_step(1, True, True, True)
            pe.wait_ge(acc_read, accs.now(2 - 1))
            pair_step(0, False, True, True)

            kseq, lseq, seq = Count(), Count(), Count()

            def keys(twos):
                if twos[0] == 0:
                    pe.wait_ge(k_in, kseq.now() * (16 * PAGES) + 16 * PAGES)
                    kseq.step()
                for two in twos:
                    t = take_acc()
                    for m in range(2):
                        for g in range(PAGES):
                            mm = pe.transpose(t[:, m, g * P:(g + 1) * P],
                                              kpage[:, g, (2 * two + m) * P:(2 * two + m + 1) * P], ident[:, :])
                    mm.then_inc(turned, 1)

            def logits_s(outputs=False):
                pe.wait_ge(acc_read, accs.now(1))
                pe.wait_ge(qz_set, lseq.now(1) * 4)
                lseq.step()
                for hp in range(NP):
                    if outputs and hp == NP // 2:
                        turn_outputs()
                    if hp == NP - 2:
                        pe.wait_ge(acc_read, accs.now(2))
                    cs = slice(hp * HQ, (hp + 1) * HQ)
                    for wt, xt in ((qz_hi, kp_hi), (qz_hi, kp_lo), (qz_lo, kp_hi)):
                        mm = pe.matmul(ob[0][0:HQ, :], wt[:, cs], xt[:, hp, :],
                                       start=hp == 0 and wt is qz_hi and xt is kp_hi, stop=hp == NP - 1 and wt is qz_lo)
                mm.then_inc(zrow_full, 1)

            def turn_logits():
                pe.wait_ge(zrow_read, lseq.now())
                for g in range(PAGES):
                    mm = pe.matmul(zb[0][:, g * HQ:(g + 1) * HQ], z_row[:, g * P:(g + 1) * P], ident[0:HQ, 0:HQ],
                                   start=g == 0, stop=False, skip_group_check=True)
                mm.then_inc(zs_full, 1)

            def after_s():
                pe.wait_ge(softs_done, seq.now(2))
                z = zb[0][:, 0:PAGES * HQ]
                zv = z.rearrange("p (g n) -> p g n", g=PAGES)
                bs = bass.ds(seq.now(), 1) if seq.reg is not None else slice(seq.now(), seq.now() + 1)
                sn = sp_n[:, :, :].rearrange("p h (b q) -> p b h q", q=NQ)[:, bs, :, :]
                for g in range(PAGES):
                    pe.matmul(zv[:, g, :], negones[0:NS, :], sn, start=False, stop=False, skip_group_check=True)
                for n in range(1, PAGES):
                    pe.matmul(z[:, 0:(PAGES - n) * HQ], negones[:, :],
                              sp_b[:, n:, :].rearrange("p g n -> p (g n)"), start=False, stop=False,
                              skip_group_check=True)
                pe.matmul(z, negtri[:, :], sp_b[:, :, :].rearrange("p g n -> p (g n)"), start=False, stop=True,
                          skip_group_check=True).then_inc(afters_done, 1)

            def values_s(c):
                if c == 0:
                    pe.wait_ge(ws_split, seq.now(1))
                    seq.step()
                pe.wait_ge(v_lo_made, seq.now() * 2 + (c - 1))
                cs = slice(c * D // 2, (c + 1) * D // 2)
                for g in range(PAGES):
                    for wt, xt in ((ws_hi, vp_hi), (ws_hi, vp_lo), (ws_lo, vp_hi)):
                        mm = pe.matmul(v_bank[c][0:HQ, :], wt[:, g, :], xt[:, g, cs],
                                       start=g == 0 and wt is ws_hi and xt is vp_hi,
                                       stop=g == PAGES - 1 and wt is ws_lo)
                mm.then_inc(v_full, 1)

            def turn_outputs():
                pe.wait_ge(v_read, seq.now() * 2)
                for hp in range(NP):
                    mm = pe.matmul(zb[1][:, hp * 2 * NQ:(hp + 1) * 2 * NQ], o_row[:, hp * P:(hp + 1) * P],
                                   ident[0:HQ, hp * 2 * NQ:(hp + 1) * 2 * NQ], start=hp == 0, stop=hp == NP - 1,
                                   skip_group_check=True)
                mm.then_inc(os_full, 1)

            def step_s(outputs=True, logits=True, more=True):
                after_s()
                if logits:
                    logits_s(outputs)
                else:
                    turn_outputs()
                pe.wait_ge(os_read, seq.now(1))
                values_s(0)
                if more:
                    keys(range(0, 2))
                values_s(1)
                if logits:
                    turn_logits()
                if more:
                    keys(range(2, KT // 2))

            v_bank = [zb[1], ob[1]]
            keys(range(KT // 2))
            pe.wait_ge(qbd_set, 3)
            for hp in range(NP):
                mm = pe.matmul(zb[0][0:NS, hp * 2 * NS:(hp + 1) * 2 * NS], kts[:, hp, :],
                               qbd[:, hp, :, :], start=hp == 0, stop=False, skip_group_check=True)
            pe.matmul(zb[0][0:NS, :], ident_b[0:NS, 0:NS], unseen_n[:, :, :, :], start=False, stop=False,
                      skip_group_check=True).then_inc(zs_full, 1)
            pe.wait_ge(o_lo, NP)
            logits_s()
            pe.wait_ge(softs_done, 1)
            pe.matmul(zb[0][0:NS, :], negtri[0:NS, 0:NS], sp_n[:, :, :], start=False, stop=True,
                      skip_group_check=True).then_inc(afters_done, 1)
            pe.wait_ge(exps_done, 1)
            for hp in range(NP):
                mm = pe.matmul(ob[1][:, hp * 2 * NS:(hp + 1) * 2 * NS], vs_nat[:, hp * P:(hp + 1) * P],
                               ws_n[:, 2 * hp:2 * hp + 2, :], start=hp == 0, stop=hp == NP - 1,
                               skip_group_check=True)
            mm.then_inc(os_full, 1)
            turn_logits()
            keys(range(KT // 2))
            step_s(False)
            with repeat(pe, NB - 3, (accs, TURNS_B), (kseq, 1), (lseq, 1), (seq, 1)):
                step_s()
            step_s(True, True, False)
            step_s(True, False, False)
            turn_outputs()

            turn_p(1)
            for n in range(KT):
                if n == 0:
                    gemm_by_halves(0, o_lo, NP + 1)
                else:
                    gemm(0)
            embed(1, 1)
            pe.wait_ge(y_scaled, KT)
            for tt in range(TT):
                n = P if tt < QB else NS
                if tt == 2:
                    pe.wait_ge(squared, (sums.now() + 1) * KT)
                    for c in range(TT):
                        m = P if c < QB else NS
                        mm = pe.matmul(zb[0][0:m, c:c + 1], sumsq[:, c * P:c * P + m], ones[:, 0:1], start=c == 0,
                                       stop=c == TT - 1, skip_group_check=True)
                    mm.then_inc(ssq_out, 1)
                t = take_acc()
                for kt in range(KT):
                    mm = pe.transpose(t[0:n, kt // 4, (kt % 4) * P:(kt % 4 + 1) * P],
                                      y_t[:, kt, tt * P:tt * P + n], ident[:, :])
                mm.then_inc(turned, 1)
            assert panel.now() == END

        @block.vector
        def _(dve):
            panel, done, accs, turns, own, xt = Count(), Count(), Count(), Count(), Count(), Count()

            def split_next():
                if panel.reg is None and panel.now() >= END:
                    return
                s = panel.slot(SLOTS)
                dve.wait_ge(hi_made, panel.now(1))
                dve.tensor_tensor(w_lo[:, s, :, :], raw[:, s, :, :], w_hi[:, s, :, :].bitcast(F32), ALU.subtract)\
                    .then_inc(lo_made, 1)
                panel.step()

            def product():
                done.step()
                dve.wait_ge(panel_done, done.now(SLOTS))
                t = acc[accs.slot(2)]
                accs.step()
                return t

            def turn():
                turns.step()
                dve.wait_ge(turned, turns.now())
                t = acc[accs.slot(2)]
                accs.step()
                return t

            def lo_x(n, into, src=None):
                xt.step()
                dve.wait_ge(x_hi, xt.now())
                one = lambda x: x[:, sl(n), :].rearrange("p a t -> p (a t)")
                dve.tensor_tensor(one(act_lo[into]), one(h) if src is None else src[:, :],
                                  one(act_hi[into]).bitcast(F32), ALU.subtract).then_inc(x_lo, 1)

            def add_product(n):
                t = product()
                hn = halves(h[:, sl(n), :].rearrange("p a t -> p (a t)"))
                dve.tensor_tensor(hn, both(t), hn, ALU.add).then_inc(acc_read, 1)

            def self_wait(ins):
                ins.then_inc(vec, 1)
                own.step()
                dve.wait_ge(vec, own.now())

            norms = Count()

            def inverse_root(r, m, scratch):
                self_wait(dve.reciprocal(r, r))
                newton(r, m, scratch)

            def newton(r, m, scratch):
                self_wait(dve.tensor_tensor(scratch, r, r, ALU.mult))
                self_wait(dve.scalar_tensor_tensor(scratch, scratch, -0.5, m, ALU.mult, ALU.mult))
                self_wait(dve.scalar_tensor_tensor(r, scratch, 1.5, r, ALU.add, ALU.mult))

            def rms():
                norms.step()
                dve.wait_ge(logged, norms.now())
                for c in range(2):
                    dve.tensor_scalar(ms[:, c * TH:(c + 1) * TH], zb[c][:, 0:TH], 1.0 / D, EPS, ALU.mult, ALU.add)
                roots.step()
                dve.wait_ge(rooted, roots.now())
                newton(rinv[:, :], ms[:, :], sumsq[:, :])

            roots = Count()

            def lo_tokens(t):
                xt.step(1 if t < QB else KT - QB)
                dve.wait_ge(x_hi, xt.now())
                dve.tensor_tensor(act_lo[0][:, :, tokens(t)], h[:, :, tokens(t)],
                                  act_hi[0][:, :, tokens(t)].bitcast(F32), ALU.subtract)\
                    .then_inc(x_lo, 1 if t < QB else KT - QB)

            for c in range(TT):
                t = turn()
                n = P if c < QB else NS
                dve.tensor_copy(h[:, :, tokens(c)].rearrange("p (a b) t -> p a b t", a=2),
                                t[:, :, :].rearrange("p a (b t) -> p a b t", t=P)[:, :, :, 0:n]).then_inc(acc_read, 1)
                if c > 0:
                    lo_tokens(c - 1)
            t = turn()
            dve.tensor_copy(cols[:, :], t[:, 0, 0:N_COL]).then_inc(acc_read, 1)
            lo_tokens(QB)
            split_next()
            for half in range(2):
                t = turn()
                dve.tensor_copy(ws_t[:, half * (NG // 2):(half + 1) * (NG // 2), :], t[:, 0, :]).then_inc(acc_read, 1)
            for _ in range(AHEAD - 1):
                split_next()
            rms()

            with repeat(dve, N_AV // SLOTS, (panel, SLOTS), (done, SLOTS), (accs, 2 * SLOTS), (turns, SLOTS)) as i:
                for k in range(SLOTS + 1):
                    if k < SLOTS:
                        split_next()
                        t = product()
                        dve.tensor_tensor(halves(vt[:, k % 2, :]), both(t), halves(rinv[:, :]), ALU.mult)\
                            .then_inc(acc_read, 1)
                    if k > 0:
                        t = turn()
                        cs = bass.ds(i * (SLOTS * P) + (k - 1) * P, P)
                        dve.tensor_copy(v_nat[0:NS, QB, cs], t[0:NS, 1, 0:P])
                        dve.tensor_copy(v_nat[:, 0:QB, cs], t[:, 0, :].rearrange("p (c n) -> p c n", n=P))\
                            .then_inc(acc_read, 1)
                dve.wait_ge(acc_read, accs.now(2))
                for tt in range(TT):
                    n = P if tt < QB else NS
                    ins = dve.bn_stats(bst[0:n, tt, bass.ds(i, 1), :].rearrange("p a s -> p (a s)"),
                                       v_nat[0:n, tt, bass.ds(i * (SLOTS * P), SLOTS * P)])
                ins.then_inc(stats_done, 1)
            dve.wait_ge(stats_done, N_AV // SLOTS)
            for tt in range(TT):
                n = P if tt < QB else NS
                ins = dve.bn_aggr(mv[0:n, tt, :], bst[0:n, tt, :, :].rearrange("p a s -> p (a s)"))
            self_wait(ins)
            dve.tensor_scalar(ln_s[:, 0, :], mv[:, :, 1], EPS, None, ALU.add).then_inc(normed, 1)
            roots.step()
            dve.wait_ge(rooted, roots.now())
            inverse_root(ln_s[:, 1, :], ln_s[:, 0, :], ln_s[:, 2, :])
            dve.tensor_copy(ln_s[:, 2, :], ln_s[:, 1, :])
            dve.scalar_tensor_tensor(ln_s[:, 3, :], mv[:, :, 0], -1.0, ln_s[:, 1, :], ALU.mult, ALU.mult)\
                .then_inc(normed, 1)
            t = turn()
            dve.tensor_tensor(ws_ts[:, :, :, :],
                              t[0:NS, 0, 0:NG * NQ].rearrange("p (g q) -> p g q", q=NQ)[:, :, None, :]
                              .to_broadcast([NS, NG, NB, NQ]),
                              blockdiag[:, None, :, :].to_broadcast([NS, NG, NB, NQ]), ALU.mult)\
                .then_inc(acc_read, 1)
            for half in range(2):
                t = turn()
                dve.tensor_copy(row_sum[:, half * 4:half * 4 + 4, 0:P], t[:, 0, :].rearrange("p (g t) -> p g t", t=P))\
                    .then_inc(acc_read, 1)
            t = turn()
            dve.tensor_copy(row_sum[:, :, P:P + NS], t[:, 0, 0:NG * NS].rearrange("p (g t) -> p g t", t=NS))\
                .then_inc(acc_read, 1)
            dve.wait_ge(acc_read, accs.now(2))
            dve.wait_ge(bs_ready, 1)

            def split_p(layer):
                for kt in range(PKT):
                    t = turn()
                    dve.tensor_copy(p_t[:, kt, TP:T], t[:, 1, 0:NS])
                    dve.tensor_copy(p_t[:, kt, 0:TP], t[:, 0, 0:TP]).then_inc(acc_read, 1)
                dve.wait_ge(acc_read, accs.now(2))
                for kt in range(PKT):
                    dve.wait_ge(p_hi_made, layer * PKT + kt + 1)
                    dve.tensor_tensor(p_lo[:, kt, :], p_t[:, kt, :], p_hi[:, kt, :].bitcast(F32), ALU.subtract)
                dve.wait_ge(wp_hi_made, layer + 1)
                dve.tensor_tensor(wp_lo[:, :, :], wp_raw[:, :, :], wp_hi[:, :, :].bitcast(F32), ALU.subtract)\
                    .then_inc(wp_lo_made, 1)

            ytile = Count()
            for hf in range(HALF):
                with repeat(dve, N_UG // SLOTS, (panel, SLOTS), (done, SLOTS), (accs, SLOTS), (ytile, 2), (xt, 2),
                            (own, 2)) as i:
                    for k in range(2):
                        j = i * 2 + (hf * KT + k)
                        split_next()
                        t = product()
                        dve.tensor_tensor(halves(u_r[:, :]), both(t), halves(rinv[:, :]), ALU.mult)\
                            .then_inc(acc_read, 1)
                        gs = bass.ds(i + hf * (NG // 2), 1)
                        self_wait(dve.scalar_tensor_tensor(
                            bs_ln[:, :], row_sum[:, gs, :].rearrange("p a t -> p (a t)"), ln_b_c[:, bass.ds(j, 1)],
                            bs_bc[:, gs, :].rearrange("p a t -> p (a t)"), ALU.mult, ALU.add))
                        ytile.step()
                        dve.wait_ge(mixed, ytile.now())
                        dve.scalar_tensor_tensor(s_t[:, TP:T], ob[k][:, 0:NS], ln_g_c[:, bass.ds(j, 1)],
                                                 bs_ln[:, P:P + NS], ALU.mult, ALU.add)
                        dve.scalar_tensor_tensor(
                            s_t[:, 0:TP].rearrange("p (c t) -> p c t", t=P),
                            zb[k][:, :].rearrange("p (c t) -> p c t", t=P), ln_g_c[:, bass.ds(j, 1)],
                            bs_ln[:, None, 0:P].to_broadcast([P, QB, P]), ALU.mult, ALU.add).then_inc(s_ready, 1)
                        split_next()
                        t = product()
                        dve.tensor_tensor(halves(g_r[:, :]), both(t), halves(rinv[:, :]), ALU.mult)\
                            .then_inc(acc_read, 1)
                        lo_x(i * 2 + k, 1, s_t)
                if hf == HALF - 1:
                    split_p(0)
                if hf < HALF - 1:
                    with repeat(dve, KT // SLOTS, (panel, SLOTS), (done, SLOTS), (accs, SLOTS)) as i:
                        for k in range(SLOTS):
                            split_next()
                            add_product(i * SLOTS + k)
                else:
                    with repeat(dve, KT // SLOTS, (panel, SLOTS), (done, SLOTS), (accs, SLOTS), (xt, SLOTS)) as i:
                        for k in range(SLOTS):
                            add_product(i * SLOTS + k)
                            lo_x(i * SLOTS + k, 0)
                            split_next()

            def embed(layer):
                for n in range(KT):
                    if n == 0:
                        rms()
                    g = gate[:, n % 2, :]
                    t = product()
                    dve.tensor_tensor(halves(g), both(t), halves(rinv[:, :]), ALU.mult).then_inc(acc_read, 1)
                    split_next()
                    if n > 0 and layer == 0:
                        lo_x(n - 1, 1)
                    t = turn()
                    dve.wait_ge(gate_sig, layer * KT + n + 1)
                    dve.tensor_tensor(halves(g), both(t), halves(g), ALU.mult).then_inc(acc_read, 1)
                    dve.wait_ge(acc_read, accs.now(2))
                    dve.tensor_tensor(h[:, n, :], h[:, n, :], g, ALU.add).then_inc(h_new, 1)
                if layer == 0:
                    lo_x(KT - 1, 1)

            embed(0)
            rms()

            blk, opair, pair = Count(), Count(), Count()

            def relu_z(n, a):
                e, kb = n // QB, QB - 1 - n % QB
                w = (QB - kb) * P
                dve.wait_ge(act_step, blk.now(1) * 2 - 1)
                dve.tensor_scalar(relz[:, n % 2, 0:w], zb[n % 2][:, 0:w], bias_of(a, e), 0.0, ALU.add, ALU.max)\
                    .then_inc(rel_done, 1)

            def softplus(n):
                e, kb = n // QB, QB - 1 - n % QB
                w = (QB - kb) * P
                blk.step()
                dve.wait_ge(rel_done, blk.now())
                dve.wait_ge(log_done, blk.now())
                a = soft_at(kb)
                r, z = relz[:, n % 2, 0:w], absz[:, n % 2, 0:w]
                dve.tensor_tensor(soft_hi[:, e, a:a + w], r, z, ALU.add).then_inc(soft_done, 1)
                dve.tensor_tensor(r, r, z, ALU.add).then_inc(soft_done, 1)
                dve.wait_ge(soft_done, blk.now() * 2)
                dve.tensor_tensor(soft_lo[:, e, a:a + w], r, soft_hi[:, e, a:a + w].bitcast(F32), ALU.subtract)\
                    .then_inc(soft_split, 1)

            def out_pair(a, par):
                opair.step()
                dve.wait_ge(o_full, opair.now())
                dve.wait_ge(sg_ready, opair.now())
                dve.tensor_tensor(o_s[:, :], ob[par][:, :], silu_g[:, par, :], ALU.mult).then_inc(o_read, 1)
                dve.wait_ge(o_read, opair.now(2))
                dve.wait_ge(o_hi, opair.now())
                one = lambda x: x[:, sl(a), 0:TP].rearrange("p a t -> p (a t)")
                dve.tensor_tensor(one(act_lo[0]), o_s[:, :], one(act_hi[0]).bitcast(F32), ALU.subtract)\
                    .then_inc(o_lo, 1)

            def turned_pair(dst, dst_s, i, par):
                t = turn()
                cs = slice(i * P, (i + 1) * P) if isinstance(i, int) else bass.ds(i * P, P)
                dve.tensor_copy(dst_s[:, cs], t[0:NS, 1, 0:P])
                dve.tensor_copy(dst[:, par, :, :], t[:, 0, :].rearrange("p (c n) -> p c n", n=P))\
                    .then_inc(acc_read, 1)

            def pair_step(i, par, dense, att, prev, stored):
                for n in range(2 * QB):
                    if att:
                        relu_z(n, i - 1)
                    if dense and n % 2 == 1:
                        split_next()
                    if dense and n == 4:
                        if stored is not None:
                            dve.wait_ge(kv_out[par], stored)
                        turned_pair(k_nat, ks_nat, i, par)
                    if dense and n == 6:
                        turned_pair(vb_nat, vs_nat, i, par)
                    if att:
                        softplus(n)
                    if n == 2 and prev:
                        out_pair(i - 2, par)
                    if dense and n == 1:
                        t = product()
                        dve.tensor_tensor(kts[:, sl(i), :].rearrange("p a t -> p (a t)"), t[:, 1, TH - NS:TH],
                                          rinv[:, TP:T], ALU.mult)
                        dve.tensor_tensor(halves(kt_t[:, par, :]), both(t), halves(rinv[:, :]), ALU.mult)\
                            .then_inc(acc_read, 1)
                    if dense and n == 3:
                        t = product()
                        dve.tensor_tensor(halves(vt_t[:, :]), both(t), halves(rinv[:, :]), ALU.mult)\
                            .then_inc(acc_read, 1)
                    if dense and n == 5:
                        t = product()
                        dve.scalar_tensor_tensor(qts[:, sl(i), :].rearrange("p a t -> p (a t)"), t[:, 1, TH - NS:TH],
                                                 SCALE, rinv[:, TP:T], ALU.mult, ALU.mult)
                        dve.scalar_tensor_tensor(halves(qt_t[:, par, :]), both(t), SCALE, halves(rinv[:, :]),
                                                 ALU.mult, ALU.mult).then_inc(acc_read, 1)
                    if dense and n == 7:
                        t = product()
                        if att:
                            dve.wait_ge(sg_ready, i if isinstance(i, int) else i)
                        dve.tensor_tensor(halves(gb_r[:, :]), both(t), halves(rinv[:, :]), ALU.mult)\
                            .then_inc(acc_read, 1)
                if att and not dense:
                    out_pair(i - 1, 1 - par)

            pair_step(0, 0, True, False, False, None)
            pair_step(1, 1, True, True, False, None)
            with repeat(dve, NP // 2 - 1, (panel, 8), (done, 8), (accs, 12), (turns, 4), (blk, 4 * QB),
                        (opair, 2)) as m:
                pair_step(m * 2 + 2, 0, True, True, True, m * 32 + 32)
                pair_step(m * 2 + 3, 1, True, True, True, m * 32 + 32)
            dve.wait_ge(q_split, 1)
            dve.tensor_tensor(qts_lo[:, :, :], qts[:, :, :], qts_hi[:, :, :].bitcast(F32), ALU.subtract)\
                .then_inc(q_split, 1)
            pair_step(NP, 0, False, True, True, None)

            samp, kseq = Count(), Count()

            def split_keys(twos):
                for two in twos:
                    kseq.step()
                    dve.wait_ge(kp_hi_made, kseq.now())
                    t = turn()
                    dve.tensor_tensor(kp_lo[:, 2 * two:2 * two + 2, :], t[:, :, :],
                                      kp_hi[:, 2 * two:2 * two + 2, :].bitcast(F32), ALU.subtract)\
                        .then_inc(acc_read, 1)

            def logits_out():
                zrow.step()
                dve.wait_ge(zrow_full, zrow.now())
                dve.tensor_scalar(z_row[:, :], ob[0][0:HQ, :], bias_row[:, 0:1], None, ALU.add).then_inc(zrow_read, 1)

            def soft_b():
                samp.step()
                dve.wait_ge(logs_done, samp.now())
                dve.scalar_tensor_tensor(sp_b[:, :, :].rearrange("p g n -> p (g n)"), zb[0][:, 0:PAGES * HQ], 0.0,
                                         sp_b[:, :, :].rearrange("p g n -> p (g n)"), ALU.max, ALU.add)\
                    .then_inc(softs_done, 1)

            def output_row(c):
                halves_v.step()
                dve.wait_ge(v_full, halves_v.now())
                dve.tensor_copy(o_row[:, c * 512:(c + 1) * 512], [zb[1], ob[1]][c][0:HQ, :]).then_inc(v_read, 1)

            def outputs(b):
                outs.step()
                dve.wait_ge(os_full, outs.now())
                bq = bass.ds(b * NQ, NQ) if not isinstance(b, int) else slice(b * NQ, (b + 1) * NQ)
                for e in range(2):
                    r = slice(e * DH, (e + 1) * DH)
                    ov = zb[1][r, 0:HQ].rearrange("p (a e q) -> p a e q", e=2, q=NQ)[:, :, e, :]
                    ins = dve.tensor_tensor(os_s[r, :, bq], ov, on_s[r, :, bq], ALU.add)
                ins.then_inc(os_read, 1)

            def step_s(before, logits=True, more=True):
                wlo.step()
                dve.wait_ge(exps_done, wlo.now(1))
                dve.tensor_tensor(ws_lo[:, :, :], ws_b[:, :, :], ws_hi[:, :, :].bitcast(F32), ALU.subtract)\
                    .then_inc(ws_split, 1)
                if before is not None:
                    outputs(before)
                if logits:
                    logits_out()
                output_row(0)
                if more:
                    split_keys(range(0, 2))
                output_row(1)
                if logits:
                    soft_b()
                if more:
                    split_keys(range(2, KT // 2))

            zrow, outs, halves_v, wlo = Count(), Count(), Count(), Count()
            z = zb[0][0:NS, :].rearrange("p (h t) -> p h t", t=NS)
            bc = bias[0:NS, :][:, :, None].to_broadcast([NS, NH, NS])
            samp.step()
            dve.wait_ge(kv_out[0], 16 * NP)
            dve.wait_ge(kv_out[1], 16 * NP)
            split_keys(range(KT // 2))
            dve.wait_ge(zs_full, 1)
            dve.tensor_tensor(xs_n[:, :, :], z, bc, ALU.add).then_inc(xs_done, 1)
            dve.wait_ge(xs_done, 1)
            dve.wait_ge(logs_done, 1)
            dve.scalar_tensor_tensor(sp_n[:, :, :], xs_n[:, :, :], 0.0, as_n[:, :, :], ALU.max, ALU.add)\
                .then_inc(softs_done, 1)
            dve.wait_ge(afters_done, 1)
            dve.tensor_tensor(xs_n[:, :, :], z, bc, ALU.add).then_inc(ds_done, 1)
            dve.wait_ge(bias_in, 16)
            logits_out()
            outs.step()
            dve.wait_ge(os_full, 1)
            for e in range(2):
                r = slice(e * DH, (e + 1) * DH)
                ins = dve.tensor_copy(on_s[r, :, :], ob[1][r, :].rearrange("p (a e n) -> p a e n", e=2, n=NS)[:, :, e, :])
            ins.then_inc(os_read, 1)
            dve.wait_ge(os_read, 1)
            soft_b()
            split_keys(range(KT // 2))
            step_s(None)
            with repeat(dve, NB - 3, (turns, TURNS_B), (accs, TURNS_B), (samp, 1), (kseq, TURNS_B), (zrow, 1),
                        (outs, 1), (halves_v, 2), (wlo, 1)) as m:
                step_s(m)
            step_s(NB - 3, True, False)
            step_s(NB - 2, False, False)
            outputs(NB - 1)
            dve.wait_ge(os_read, NB + 1)
            dve.tensor_tensor(os_s[:, :, :], os_s[:, :, :], silu_s[:, :, :], ALU.mult).then_inc(os_sum, 1)
            dve.wait_ge(os_sum, 1)
            dve.wait_ge(o_hi, NP + 1)
            dve.tensor_tensor(act_lo[0][:, :, TP:T], os_s[:, :, :], act_hi[0][:, :, TP:T].bitcast(F32),
                              ALU.subtract).then_inc(o_lo, 1)

            split_p(1)
            with repeat(dve, KT // SLOTS, (panel, SLOTS), (done, SLOTS), (accs, SLOTS), (xt, SLOTS)) as i:
                for k in range(SLOTS):
                    add_product(i * SLOTS + k)
                    lo_x(i * SLOTS + k, 1)
                    split_next()
            embed(1)
            norms.step()
            dve.wait_ge(ssq_out, norms.now())
            dve.tensor_scalar(ln_s[:, 0, 0:QB], zb[0][:, 0:QB], 1.0 / D, EPS, ALU.mult, ALU.add)
            dve.tensor_scalar(ln_s[0:NS, 0, QB:TT], zb[0][0:NS, QB:TT], 1.0 / D, EPS, ALU.mult, ALU.add)\
                .then_inc(mean_sq, 1)
            roots.step()
            dve.wait_ge(rooted, roots.now())
            inverse_root(ln_s[:, 1, :], ln_s[:, 0, :], ln_s[:, 2, :])
            for tt in range(TT):
                n = P if tt < QB else NS
                t = turn()
                dve.tensor_scalar(y_nat[0:n, tt, :].rearrange("p (c n) -> p c n", c=2), t[0:n, :, :],
                                  ln_s[0:n, 1, tt:tt + 1], None, ALU.mult).then_inc(acc_read, 1)
            assert panel.now() == END and accs.now() == ACC_END


_INS = ['x_prompt', 'x_sample', 'cache_k', 'cache_v', 'page_table', 'p_prompt', 'p_sample', 'g_norm', 'w_in_a',
        'ln_v_g', 'ln_v_b', 'w_spatial', 'b_spatial', 'w_out_a', 'g_kv', 'w_kv', 'w_in_b', 'w_out_b', 'b_sb',
        'w_ple', 'g_ple', 'w_ple_gate', 'g_final']


def kernel(**inputs):
    import numpy as _np
    import concourse.bacc as _bacc
    from concourse import mybir as _mybir
    from concourse.bass_utils import run_bass_kernel_spmd as _run

    nc = _bacc.Bacc("TRN2", target_bir_lowering=False, num_devices=1, dynamic_dma_scratch_size=1024)
    arrays, args = {}, []
    for name in _INS:
        a = _np.ascontiguousarray(inputs[name])
        arrays[f"in_{name}_dram"] = a
        args.append(nc.dram_tensor(f"in_{name}_dram", a.shape, _mybir.dt.from_np(a.dtype), kind="ExternalInput").ap())
    xp, xs = inputs['x_prompt'].shape, inputs['x_sample'].shape
    heads = tuple(inputs['cache_k'].shape[2:])
    e_a = inputs['ln_v_g'].shape[1]
    outs = [xp, xs, tuple(xp[:2]) + heads, tuple(xp[:2]) + heads, tuple(xs[:2]) + heads, tuple(xs[:2]) + heads,
            (1,) + tuple(xs[:2]) + (e_a,)]
    for i, shape in enumerate(outs):
        args.append(nc.dram_tensor(f"out_{i}_dram", tuple(shape), _mybir.dt.float32, kind="ExternalOutput").ap())
    build(nc, *args)
    r = _run(nc, [arrays], core_ids=[0])
    return tuple(r.results[0][f"out_{i}_dram"] for i in range(len(outs)))
```
